# Optimizing a Trainium2 kernel written in Bass

```python
import functools
import jax, jax.numpy as jnp
from jax import lax
import numpy as np

D_MODEL = 1024
BATCH = 1
SEQ = 1024
DEPTH = 1
DEC_BATCH = 8
DEC_SEQ = 4
PAST_LEN = 8192
PAGE_SIZE = 128

V_DIM = 128
N_HEADS = D_MODEL // V_DIM
MLA_WIDTH = N_HEADS * V_DIM
Q_LORA = 384
KV_LORA = 256
NOPE_DIM = 128
ROPE_DIM = 64
ROPE_THETA = 10000.0
ATTN_SCALE = (NOPE_DIM + ROPE_DIM) ** -0.5
Q_BLOCK = 128
CHUNK = 128
SGU_WIDTH = D_MODEL
SGU_GROUP_WIDTH = 128
SGU_GROUPS = SGU_WIDTH // SGU_GROUP_WIDTH
_IN_PARTS = (Q_LORA, KV_LORA, ROPE_DIM, SGU_WIDTH, SGU_WIDTH, MLA_WIDTH, SGU_WIDTH)
IN_WIDTH = sum(_IN_PARTS)
IN_SPLITS = tuple(int(c) for c in np.cumsum(_IN_PARTS)[:-1])
N_GROUPS = 8
EXPERTS_PER_GROUP = 8
N_EXPERTS = N_GROUPS * EXPERTS_PER_GROUP
TOP_K = 2
D_EXPERT = 256
ROW_BLOCK = 128
EPS = 1e-6
POOL_NUM, POOL_DEN = 5, 4

kernel_name = "mla_sgu_gated_hier_moe_step"

def rmsnorm(x, g):
    xf = x.astype(jnp.float32)
    y = xf * lax.rsqrt(jnp.mean(xf * xf, axis=-1, keepdims=True) + EPS)
    return (y * g.astype(jnp.float32)).astype(x.dtype)

def rope(x, pos):
    half = ROPE_DIM // 2
    freq = ROPE_THETA ** (-jnp.arange(half, dtype=jnp.float32) / half)
    ang = pos.astype(jnp.float32)[:, None] * freq[None, :]
    cos = jnp.cos(ang)[None, :, None, :]
    sin = jnp.sin(ang)[None, :, None, :]
    xf = x.astype(jnp.float32)
    x1, x2 = xf[..., :half], xf[..., half:]
    return jnp.concatenate([x1 * cos - x2 * sin, x2 * cos + x1 * sin], axis=-1).astype(x.dtype)

def mla_project(z_q, z_kv, z_kr, pos, q_norm_g, kv_norm_g, w_uq, w_qr, w_uk):
    c_q = rmsnorm(z_q, q_norm_g)
    q_nope = jnp.einsum('bsr,rhd->bshd', c_q, w_uq)
    q_rope = rope(jnp.einsum('bsr,rhd->bshd', c_q, w_qr), pos)
    q_lat = jnp.einsum('bshd,chd->bshc', q_nope, w_uk)
    c_kv = rmsnorm(z_kv, kv_norm_g)
    k_rope = rope(z_kr[:, :, None, :], pos)[:, :, 0, :]
    return q_lat, q_rope, c_kv, k_rope

def mla_scores(q_lat, q_rope, c_kv, k_rope):
    s = (jnp.einsum('bqhc,bkc->bhqk', q_lat, c_kv, preferred_element_type=jnp.float32)
         + jnp.einsum('bqhr,bkr->bhqk', q_rope, k_rope, preferred_element_type=jnp.float32))
    return s * ATTN_SCALE

def prompt_attention(q_lat, q_rope, c_kv, k_rope):
    b, s, h, c = q_lat.shape
    nb = s // Q_BLOCK
    ql = jnp.moveaxis(q_lat.reshape(b, nb, Q_BLOCK, h, c), 1, 0)
    qr = jnp.moveaxis(q_rope.reshape(b, nb, Q_BLOCK, h, ROPE_DIM), 1, 0)
    kpos = jnp.arange(s, dtype=jnp.int32)

    def one_block(args):
        i, qlb, qrb = args
        qpos = i * Q_BLOCK + jnp.arange(Q_BLOCK, dtype=jnp.int32)
        sc = mla_scores(qlb, qrb, c_kv, k_rope)
        sc = jnp.where(kpos[None, :] <= qpos[:, None], sc, -jnp.inf)
        p = jax.nn.softmax(sc, axis=-1)
        return jnp.einsum('bhqk,bkc->bqhc', p, c_kv, preferred_element_type=jnp.float32)

    o = lax.map(one_block, (jnp.arange(nb, dtype=jnp.int32), ql, qr))
    return jnp.moveaxis(o, 0, 1).reshape(b, s, h, c).astype(q_lat.dtype)

def sample_attention(q_lat, q_rope, c_kv, k_rope, cache_ckv, cache_krope, page_table):
    t = q_lat.shape[1]
    sc = mla_scores(q_lat, q_rope, c_kv, k_rope)
    causal = jnp.tril(jnp.ones((t, t), dtype=bool))
    sc = jnp.where(causal, sc, -jnp.inf)
    m0 = jnp.max(sc, axis=-1)
    p0 = jnp.exp(sc - m0[..., None])
    l0 = jnp.sum(p0, axis=-1)
    acc0 = jnp.einsum('bhqk,bkc->bhqc', p0, c_kv, preferred_element_type=jnp.float32)

    def step(carry, pages):
        m, l, acc = carry
        ck = cache_ckv[pages]
        kr = cache_krope[pages]
        s = mla_scores(q_lat, q_rope, ck, kr)
        m_new = jnp.maximum(m, jnp.max(s, axis=-1))
        alpha = jnp.exp(m - m_new)
        p = jnp.exp(s - m_new[..., None])
        l = l * alpha + jnp.sum(p, axis=-1)
        acc = acc * alpha[..., None] + jnp.einsum('bhqk,bkc->bhqc', p, ck, preferred_element_type=jnp.float32)
        return (m_new, l, acc), None

    (m, l, acc), _ = lax.scan(step, (m0, l0, acc0), page_table.T)
    o = acc / l[..., None]
    return jnp.transpose(o, (0, 2, 1, 3)).astype(q_lat.dtype)

def spatial_gate(v, w_s, b_s, rows):
    b, s, _ = v.shape
    causal = jnp.tril(jnp.ones((rows, rows), dtype=bool))
    ws = jnp.where(causal[None], w_s[:, :rows, :rows], 0)
    vc = v.reshape(b, s // rows, rows, SGU_GROUPS, SGU_GROUP_WIDTH)
    mixed = jnp.einsum('gij,bnjgc->bnigc', ws, vc) + b_s[:, :rows].T[None, None, :, :, None]
    return mixed.reshape(b, s, SGU_WIDTH)

def token_mixer(x, pos, attend, rows, norm1_g, w_in, q_norm_g, kv_norm_g, w_uq, w_qr, w_uk, w_uv,
                sgu_norm_g, w_s, b_s, w_o):
    b, s, _ = x.shape
    z = rmsnorm(x, norm1_g) @ w_in
    z_q, z_kv, z_kr, z_u, z_v, z_ga, z_gb = jnp.split(z, IN_SPLITS, axis=-1)
    q_lat, q_rope, c_kv, k_rope = mla_project(z_q, z_kv, z_kr, pos, q_norm_g, kv_norm_g, w_uq, w_qr, w_uk)
    o_lat = attend(q_lat, q_rope, c_kv, k_rope)
    attn = jnp.einsum('bshc,che->bshe', o_lat, w_uv).reshape(b, s, MLA_WIDTH)
    u = jax.nn.gelu(z_u)
    v = rmsnorm(jax.nn.gelu(z_v), sgu_norm_g)
    sgu = u * spatial_gate(v, w_s, b_s, rows)
    merged = jax.nn.sigmoid(z_ga) * attn + jax.nn.sigmoid(z_gb) * sgu
    return x + merged @ w_o, c_kv, k_rope, v

def grouped_expert_ffn(xt, expert, weights, w_gate, w_up, w_down):
    t, d = xt.shape
    a = t * TOP_K
    flat_e = expert.reshape(a)
    order = jnp.argsort(flat_e)
    e_sorted = flat_e[order]
    tok_sorted = order // TOP_K
    w_sorted = weights.reshape(a)[order]
    sizes = jnp.bincount(flat_e, length=N_EXPERTS)
    start = jnp.cumsum(sizes) - sizes
    padded = (sizes + ROW_BLOCK - 1) // ROW_BLOCK * ROW_BLOCK
    pad_end = jnp.cumsum(padded)
    pad_start = pad_end - padded
    pos = pad_start[e_sorted] + (jnp.arange(a, dtype=jnp.int32) - start[e_sorted])
    n_blocks = -(-a // ROW_BLOCK) + N_EXPERTS
    xs = jnp.zeros((n_blocks * ROW_BLOCK, d), xt.dtype).at[pos].set(xt[tok_sorted])
    block_start = jnp.arange(n_blocks, dtype=jnp.int32) * ROW_BLOCK
    block_expert = jnp.minimum(jnp.searchsorted(pad_end, block_start, side='right'), N_EXPERTS - 1)

    def run_block(args):
        xb, e = args
        h = jax.nn.silu(xb @ w_gate[e]) * (xb @ w_up[e])
        return h @ w_down[e]

    ys = lax.map(run_block, (xs.reshape(n_blocks, ROW_BLOCK, d), block_expert)).reshape(-1, d)
    out = ys[pos] * w_sorted[:, None].astype(ys.dtype)
    return jnp.zeros_like(xt).at[tok_sorted].add(out.astype(xt.dtype))

def channel_mixer(x, norm2_g, w_rg, b_rg, w_re, b_re, w_gate, w_up, w_down):
    b, s, d = x.shape
    xt = rmsnorm(x, norm2_g).reshape(b * s, d)
    g_logit = (xt @ w_rg).astype(jnp.float32) + b_rg.astype(jnp.float32)
    g_w, g_idx = lax.top_k(jax.nn.softmax(g_logit, axis=-1), 1)
    e_logit = ((xt @ w_re).astype(jnp.float32) + b_re.astype(jnp.float32)).reshape(b * s, N_GROUPS, EXPERTS_PER_GROUP)
    e_logit = jnp.take_along_axis(e_logit, g_idx[:, :, None], axis=1)[:, 0]
    e_w, e_idx = lax.top_k(jax.nn.softmax(e_logit, axis=-1), TOP_K)
    e_w = e_w / jnp.sum(e_w, axis=-1, keepdims=True)
    weights = g_w * e_w
    expert = g_idx * EXPERTS_PER_GROUP + e_idx
    y = grouped_expert_ffn(xt, expert, weights, w_gate, w_up, w_down)
    return x + y.reshape(b, s, d)

def setup_inputs(seed: int = 0) -> dict:
    key = jax.random.key(seed)
    ks = jax.random.split(key, 32)
    f32 = jnp.float32
    L = DEPTH
    n_pages = PAST_LEN // PAGE_SIZE
    n_phys = (DEC_BATCH * n_pages * POOL_NUM) // POOL_DEN

    def nrm(k, shape, scale):
        return jax.random.normal(k, shape, f32) * scale

    def gain(k, shape):
        return 1.0 + 0.01 * jax.random.normal(k, shape, f32)

    page_table = jax.random.permutation(ks[4], n_phys)[: DEC_BATCH * n_pages].reshape(DEC_BATCH, n_pages).astype(jnp.int32)
    return {
        "x_prompt": nrm(ks[0], (BATCH, SEQ, D_MODEL), 1.0),
        "x_sample": nrm(ks[1], (DEC_BATCH, DEC_SEQ, D_MODEL), 1.0),
        "cache_ckv": nrm(ks[2], (L, n_phys, PAGE_SIZE, KV_LORA), 1.0),
        "cache_krope": nrm(ks[3], (L, n_phys, PAGE_SIZE, ROPE_DIM), 1.0),
        "page_table": page_table,
        "norm1_g": gain(ks[5], (L, D_MODEL)),
        "w_in": nrm(ks[6], (L, D_MODEL, IN_WIDTH), D_MODEL ** -0.5),
        "q_norm_g": gain(ks[7], (L, Q_LORA)),
        "kv_norm_g": gain(ks[8], (L, KV_LORA)),
        "w_uq": nrm(ks[9], (L, Q_LORA, N_HEADS, NOPE_DIM), Q_LORA ** -0.5),
        "w_qr": nrm(ks[10], (L, Q_LORA, N_HEADS, ROPE_DIM), Q_LORA ** -0.5),
        "w_uk": nrm(ks[11], (L, KV_LORA, N_HEADS, NOPE_DIM), KV_LORA ** -0.5),
        "w_uv": nrm(ks[12], (L, KV_LORA, N_HEADS, V_DIM), KV_LORA ** -0.5),
        "sgu_norm_g": gain(ks[13], (L, SGU_WIDTH)),
        "w_s": nrm(ks[14], (L, SGU_GROUPS, CHUNK, CHUNK), CHUNK ** -0.5),
        "b_s": gain(ks[15], (L, SGU_GROUPS, CHUNK)),
        "w_o": nrm(ks[16], (L, D_MODEL, D_MODEL), D_MODEL ** -0.5),
        "norm2_g": gain(ks[17], (L, D_MODEL)),
        "w_rg": nrm(ks[18], (L, D_MODEL, N_GROUPS), D_MODEL ** -0.5),
        "b_rg": nrm(ks[19], (L, N_GROUPS), 0.01),
        "w_re": nrm(ks[20], (L, D_MODEL, N_EXPERTS), D_MODEL ** -0.5),
        "b_re": nrm(ks[21], (L, N_EXPERTS), 0.01),
        "w_gate": nrm(ks[22], (L, N_EXPERTS, D_MODEL, D_EXPERT), D_MODEL ** -0.5),
        "w_up": nrm(ks[23], (L, N_EXPERTS, D_MODEL, D_EXPERT), D_MODEL ** -0.5),
        "w_down": nrm(ks[24], (L, N_EXPERTS, D_EXPERT, D_MODEL), D_EXPERT ** -0.5),
        "norm_f_g": gain(ks[25], (D_MODEL,)),
    }

def reference(x_prompt, x_sample, cache_ckv, cache_krope, page_table, norm1_g, w_in, q_norm_g, kv_norm_g,
              w_uq, w_qr, w_uk, w_uv, sgu_norm_g, w_s, b_s, w_o, norm2_g, w_rg, b_rg, w_re, b_re,
              w_gate, w_up, w_down, norm_f_g):
    b_p, s_p, _ = x_prompt.shape
    b_s_, t_s, _ = x_sample.shape
    past_len = page_table.shape[1] * PAGE_SIZE
    pos_p = jnp.arange(s_p, dtype=jnp.int32)
    pos_s = past_len + jnp.arange(t_s, dtype=jnp.int32)
    xp, xs = x_prompt, x_sample
    ckv_p, kr_p, ckv_s, kr_s, v_s = [], [], [], [], []
    for l in range(DEPTH):
        mix = (norm1_g[l], w_in[l], q_norm_g[l], kv_norm_g[l], w_uq[l], w_qr[l], w_uk[l], w_uv[l],
               sgu_norm_g[l], w_s[l], b_s[l], w_o[l])
        moe = (norm2_g[l], w_rg[l], b_rg[l], w_re[l], b_re[l], w_gate[l], w_up[l], w_down[l])
        xp, c_p, k_p, _ = token_mixer(xp, pos_p, prompt_attention, CHUNK, *mix)
        xp = channel_mixer(xp, *moe)
        attend_s = functools.partial(sample_attention, cache_ckv=cache_ckv[l], cache_krope=cache_krope[l],
                                     page_table=page_table)
        xs, c_s, k_s, vv = token_mixer(xs, pos_s, attend_s, t_s, *mix)
        xs = channel_mixer(xs, *moe)
        ckv_p.append(c_p.reshape(b_p, s_p // PAGE_SIZE, PAGE_SIZE, KV_LORA))
        kr_p.append(k_p.reshape(b_p, s_p // PAGE_SIZE, PAGE_SIZE, ROPE_DIM))
        ckv_s.append(c_s)
        kr_s.append(k_s)
        v_s.append(vv)
    y_prompt = rmsnorm(xp, norm_f_g)
    y_sample = rmsnorm(xs, norm_f_g)
    new_ckv_prompt = jnp.stack(ckv_p)
    new_krope_prompt = jnp.stack(kr_p)
    new_ckv_sample = jnp.stack(ckv_s)
    new_krope_sample = jnp.stack(kr_s)
    new_sgu_v_sample = jnp.stack(v_s)
    return (y_prompt, y_sample, new_ckv_prompt, new_krope_prompt, new_ckv_sample, new_krope_sample, new_sgu_v_sample)


_drawn_inputs = setup_inputs


def setup_inputs(seed=0):
    import zlib

    import numpy as np

    out = dict(_drawn_inputs(seed))
    spreads = {}
    factors = {'cache_ckv': 6.007,
     'cache_krope': 3.513,
     'norm1_g': 5.207,
     'q_norm_g': 8.0,
     'kv_norm_g': 5.921,
     'sgu_norm_g': 5.461,
     'b_s': 5.861,
     'norm2_g': 2.972,
     'b_rg': 3.394,
     'b_re': 3.73,
     'norm_f_g': 5.547}
    for name, (base, spread) in spreads.items():
        noise = np.random.default_rng([zlib.crc32(name.encode()), seed]).standard_normal(out[name].shape)
        drawn = base * np.exp(spread * noise) if base else spread * noise
        out[name] = __import__('jax').numpy.asarray(drawn.astype(out[name].dtype))
    for name, factor in factors.items():
        out[name] = (out[name] * factor).astype(out[name].dtype)
    return out
```

```python
from contextlib import ExitStack

import numpy as np

import concourse.bass as bass
from concourse import mybir

F32 = mybir.dt.float32
I32 = mybir.dt.int32
U32 = mybir.dt.uint32
ALU = mybir.AluOpType
ACT = mybir.ActivationFunctionType
AX = mybir.AxisListType

P = 128
D = 1024
KD = D // P
SEQ = 1024
NTP = SEQ // P
NB, TS = 8, 4
RS = NB * TS
NT = NTP + 1
TOK = SEQ + RS
H = 8
DN = 128
DR = 64
DV = 128
QL, KVL = 384, 256
ZL = QL + KVL + DR
NG = 8
NE = 64
DE = 256
EPS = 1e-6
SCALE = float(np.float32((DN + DR) ** -0.5))
NEG = -1e30
PAST = 8192
PAGES = PAST // P
PG = 16
NCH = NB * PAGES // PG
NOVF = 2 * TOK // P
NBLK = NE + NOVF
PAD = 1e6
CAP_STEPS = (TOK + P - 1) // P - 1
QB = 2 * H * P


def rows_of(t):
    return P if t < NTP else RS


def const_layout():
    at, off = {}, 0
    for name, n in (("ident", P), ("negmask", P), ("before", P), ("ones", P), ("keep", P), ("keep_s", RS),
                    ("cos", NT * 32), ("sin", NT * 32), ("iota", NE), ("steps", CAP_STEPS),
                    ("pad", NT), ("blocks", NOVF), ("mask_new", NB * H * TS), ("p_mod", 1), ("eps", 1)):
        at[name] = (off, n)
        off += n
    return at, off


def const_tables():
    at, n = const_layout()
    k = np.zeros((P, n), np.float32)

    def put(name, a):
        o, w = at[name]
        k[:a.shape[0], o:o + w] = a.reshape(a.shape[0], w)

    i = np.arange(P)
    put("ident", np.eye(P, dtype=np.float32))
    put("negmask", np.where(i[None, :] <= i[:, None], 0, NEG).astype(np.float32))
    put("before", (i[:, None] < i[None, :]).astype(np.float32))
    put("ones", np.ones((P, P), np.float32))
    put("keep", (i[None, :] <= i[:, None]).astype(np.float32))
    r = np.arange(RS)
    same = r[None, :] // TS == r[:, None] // TS
    put("keep_s", (same & (r[None, :] <= r[:, None])).astype(np.float32))
    half = DR // 2
    freq = np.float32(10000.0) ** (-np.arange(half, dtype=np.float32) / np.float32(half))
    pos = np.zeros((P, NT), np.float32)
    for t in range(NTP):
        pos[:, t] = t * P + i
    pos[:RS, NTP] = PAST + r % TS
    ang = pos[:, :, None] * freq[None, None, :]
    put("cos", np.cos(ang).astype(np.float32))
    put("sin", np.sin(ang).astype(np.float32))
    put("iota", np.tile(np.arange(NE, dtype=np.float32), (P, 1)))
    put("steps", np.tile(P * np.arange(1, CAP_STEPS + 1, dtype=np.float32), (P, 1)))
    pad = np.zeros((P, NT), np.float32)
    pad[RS:, NTP] = PAD + i[RS:]
    put("pad", pad)
    put("blocks", np.tile(np.arange(NOVF, dtype=np.float32), (P, 1)))
    col = np.arange(NB * H * TS)
    cb, ct = col // (H * TS), col % TS
    ok = (r[:, None] // TS == cb[None, :]) & (r[:, None] % TS <= ct[None, :])
    put("mask_new", np.where(ok, 0, NEG).astype(np.float32))
    put("p_mod", (i % 8).astype(np.float32)[:, None])
    put("eps", np.full((P, 1), EPS, np.float32))
    ids = np.zeros((P, NT, 2, 2), np.int32)
    for t in range(NT):
        for c in range(2):
            ids[:, t, c, 0] = (t * P + i) * 2 + c
            ids[:, t, c, 1] = t * P + i
    return k, ids.reshape(P, NT * 4)


def q_units(sched, tile):
    n = 0
    for what, k in sched:
        if what == "Q" and k == tile:
            return n + 1
        n += 6 if what == "Q" else int(what in ("PV", "UV") and k % 2 == 0)


class Count:

    def __init__(self, eng, sem, base=0):
        self.eng, self.sem, self.base, self.n = eng, sem, base, 0

    def __call__(self, ins):
        self.n += 1
        ins.then_inc(self.sem, 1)
        self.eng.wait_ge(self.sem, self.base + self.n)


def attention_schedule():
    units = [(t, h) for t in range(NTP) for h in range(H)]
    todo = [("prep", 0), ("Q", 0), ("S", 0)]
    for n, (t, h) in enumerate(units):
        if n + 1 < len(units):
            if h == 1:
                todo.append(("prep", t + 1))
            if h == 3:
                todo.append(("Q", t + 1))
            todo.append(("S", n + 1))
        todo.append(("T", n))
        if t == NTP - 1 and h == 1:
            todo.append(("prep", NTP))
        if t == NTP - 1 and h == 3:
            todo.append(("Q", NTP))
        if n >= 1:
            todo.append(("PV", n - 1))
        if n >= 2:
            todo.append(("UV", n - 2))
    last = len(units) - 1
    todo += [("PV", last), ("UV", last - 1), ("UV", last)]
    out = []
    for x in todo:
        if x not in out:
            out.append(x)
    return units, out


def build(nc, x_prompt, x_sample, cache_ckv, cache_krope, page_table, norm1_g, w_in, q_norm_g, kv_norm_g,
          w_uq, w_qr, w_uk, w_uv, sgu_norm_g, w_s, b_s, w_o, norm2_g, w_rg, b_rg, w_re, b_re,
          w_gate, w_up, w_down, norm_f_g, tables, ids,
          y_prompt, y_sample, ckv_prompt, kr_prompt, ckv_sample, kr_sample, v_sample,
          z_act, xt_rows, slot_rows, y_rows):
    with ExitStack() as ctx:
        def sem(name):
            return ctx.enter_context(nc.semaphore(name))

        SIZE = 53200
        arena = ctx.enter_context(nc.sbuf_tensor("arena", [P, SIZE], F32))
        psum = ctx.enter_context(nc.psum_tensor("psum", [P, 8 * 512], F32))
        top = [0]
        end = [SIZE]

        def take(n, where=None, dt=F32):
            where = where or top
            v = arena[:, where[0]:where[0] + n]
            where[0] += n
            assert where[0] <= end[0], (where, n)
            return v

        def bank(b, n=1):
            return psum[:, 512 * b:512 * (b + n)]

        at, n_const = const_layout()
        K = take(n_const)

        def const(name):
            o, w = at[name]
            return K[:, o:o + w]

        ident, ones, eps = const("ident"), const("ones"), const("eps")
        cos, sin = (const(x).rearrange("p (t f) -> p t f", t=NT) for x in ("cos", "sin"))
        ids_sb = take(NT * 4).bitcast(I32)
        gains_base = top[0]
        g1, g2, gf, gv = take(D), take(D), take(D), take(D)
        gq, gkv = take(QL), take(KVL)
        rbias = take(NG + NE)
        w_router = take(KD * (NG + NE)).rearrange("p (k n) -> p k n", k=KD)
        ws_t = take(KD * P).rearrange("p (g i) -> p g i", g=KD)
        ws_ts = take(KD * RS).rearrange("p (g i) -> p g i", g=KD)
        bs_t, bs_ts = take(KD), take(KD)
        logits = take(NT * 72).rearrange("p (t n) -> p t n", t=NT)
        small = take(64)
        stat = small[:, 8:8 + 2 * NT].rearrange("p (t n) -> p t n", t=NT)
        rstd = small[:, 30:30 + 2 * NT].rearrange("p (t n) -> p t n", t=NT)
        page_idx = take(NCH)
        page_int = take(NCH).bitcast(I32)
        page_raw = take(NCH).bitcast(I32)
        x2_at = [SIZE - NT * D]
        x2 = arena[:, x2_at[0]:SIZE].rearrange("p (t n) -> p t n", t=NT)

        attn_base = top[0]
        attn = take(NT * D).rearrange("p (t n) -> p t n", t=NT)
        kv_base = top[0]
        ckv_n = take(NT * KVL).rearrange("p (t n) -> p t n", t=NT)
        kr_n = take(NT * DR).rearrange("p (t n) -> p t n", t=NT)
        ckv_t = take(2 * TOK).rearrange("p (c n) -> p c n", c=2)
        kr_t = take(TOK)
        w_uv_sb = take(2 * H * DV).rearrange("p (c n) -> p c n", c=2)
        qs = take(2 * NB * H * TS).rearrange("p (c n) -> p c n", c=2)
        qsr = take(NB * H * TS)
        z0_base = top[0]
        z0 = take(NT * ZL).rearrange("p (t n) -> p t n", t=NT)
        w_uq_sb = take(3 * H * DN).rearrange("p (r n) -> p r n", r=3)
        w_qr_sb = take(3 * H * DR).rearrange("p (r n) -> p r n", r=3)
        w_uk_t = take(H * KVL).rearrange("p (h c) -> p h c", h=H)
        o_base = top[0]

        o, kv = [o_base], [kv_base]
        xn_t = take(KD * TOK, o).rearrange("p (k n) -> p k n", k=KD)
        w_blk = [take(KD * 512, x).rearrange("p (k n) -> p k n", k=KD) for x in (o, kv)]
        zst = [take(512, kv) for _ in range(2)]
        a = [attn_base]
        x_in = [take(D, a) for _ in range(2)]
        xn = [take(D, a) for _ in range(2)]
        junk1 = take(D, a)
        junk2 = take(QL + KVL, a)
        w_uk_n = take(2 * H * DN, a).rearrange("p (c h d) -> p c h d", c=2, h=H)
        ws_n = take(KD * P, a).rearrange("p (g j) -> p g j", g=KD)
        ws_ns = take(KD * RS, a).rearrange("p (g j) -> p g j", g=KD)

        o = [o_base]
        cq = take(QL, o)
        cq_t = take(3 * P, o).rearrange("p (r n) -> p r n", r=3)
        early = [gains_base]
        qr_tmp = take(H * 32 * 4, early)
        qn_t = take(H * P, early).rearrange("p (h n) -> p h n", h=H)
        qr_n, qr_r = take(H * DR, o), take(H * DR, o)
        ql_t = [take(QB, o).rearrange("p (h c n) -> p h c n", h=H, c=2) for _ in range(2)]
        qr_t = [take(H * P, o).rearrange("p (h n) -> p h n", h=H) for _ in range(2)]
        prob = [take(SEQ, o) for _ in range(2)]
        prob_t = [take(SEQ, early).rearrange("p (j n) -> p j n", j=8) for _ in range(2)]
        pv_t = [take(2 * P, o).rearrange("p (c n) -> p c n", c=2) for _ in range(2)]
        kr_tmp = take(DR * 2, o)
        negmax, psumq, rinv = take(64, o), take(64, o), take(64, o)

        o = [z0_base]
        ck = [take(PG * KVL, o).rearrange("p (r n) -> p r n", r=PG) for _ in range(4)]
        kr = [take(PG * DR, o).rearrange("p (r n) -> p r n", r=PG) for _ in range(4)]
        ck_t = take(4 * 2 * P, o).rearrange("p (r c n) -> p r c n", r=4, c=2)
        kr_tt = take(4 * P, o).rearrange("p (r n) -> p r n", r=4)
        p_sub = take(512, o)
        p_exp = [take(512, o) for _ in range(2)]
        old = [kv_base]
        s_new, p_new = take(256, old), take(256, old)
        m_all, l_all = take(256, old), take(256, old)
        acc = take(512, old).rearrange("p (c n) -> p c n", c=2)
        m_part, m_col, m_diag, m_new, m_dif, alpha, l_add = (take(32, o) for _ in range(7))
        m_col2, m_diag2 = take(2, o), take(256, old)
        l_inv = take(256, old)
        assert old[0] <= kv_base + NTP * KVL
        o_lat = take(512, o).rearrange("p (c n) -> p c n", c=2)
        idx_now = [take(1, o).bitcast(U32) for _ in range(4)]

        o = [kv_base]
        w_o_sb = take(KD * D, o).rearrange("p (k n) -> p k n", k=KD)
        zt = [take(4 * D, o) for _ in range(2)]
        xr = [take(D, o) for _ in range(2)]
        m_t = take(KD * P, o).rearrange("p (k n) -> p k n", k=KD)
        x2_t = take(KD * P, o).rearrange("p (k n) -> p k n", k=KD)
        xo = [take(D, o) for _ in range(2)]
        junk5 = take(D, o)
        stat5 = [take(4, o) for _ in range(2)]
        assert o[0] <= x2_at[0], (o, x2_at)

        o = [attn_base]
        w_e = [(take(KD * DE, o).rearrange("p (k n) -> p k n", k=KD),
                take(KD * DE, o).rearrange("p (k n) -> p k n", k=KD),
                take(2 * D, o).rearrange("p (f n) -> p f n", f=2)) for _ in range(4)]
        xg = [take(D, o) for _ in range(2)]
        xg_t = take(KD * P, o).rearrange("p (k n) -> p k n", k=KD)
        h_n, h_t = take(DE, o), take(DE, o).rearrange("p (f n) -> p f n", f=2)
        h_s = take(DE, o)
        yo = [take(D, o) for _ in range(2)]
        slot_idx = take(2 * NBLK, o).bitcast(U32).rearrange("p (b c) -> p b c", c=2)
        idx_tok, idx_row = [take(1, o).bitcast(U32) for _ in range(2)], [take(1, o).bitcast(U32) for _ in range(2)]
        ovf_id = take(NOVF + 1, o).bitcast(I32)
        gates = take(NT * 2, o).rearrange("p (t c) -> p t c", t=NT)
        rt_base = o[0]
        g_top = take(NT * 8, o).rearrange("p (t n) -> p t n", t=NT)
        g_ind = take(NT * 8, o).bitcast(U32).rearrange("p (t n) -> p t n", t=NT)
        g_f = take(NT, o)
        pen = take(NT * 8, o).rearrange("p (t n) -> p t n", t=NT)
        e_top = take(NT * 8, o).rearrange("p (t n) -> p t n", t=NT)
        e_ind = take(NT * 8, o).bitcast(U32).rearrange("p (t n) -> p t n", t=NT)
        e_f = take(NT * 2, o).rearrange("p (t c) -> p t c", t=NT)
        n_rt = [take(NT * 2, o).rearrange("p (t c) -> p t c", t=NT) for _ in range(6)]
        cnt = [take(NE, o) for _ in range(4)]
        g_sub, g_exp = (take(NT * 8, o).rearrange("p (t n) -> p t n", t=NT) for _ in range(2))
        d_sub, d_exp, g_den, w_one, w_two = (take(NT, o) for _ in range(5))
        pos_i = take(NT * 2, o).bitcast(U32)
        assert o[0] <= x2_at[0], (o, x2_at)
        o2 = [attn_base + 4 * 6144]
        e_log = take(NT * NE, o2).rearrange("p (t n) -> p t n", t=NT)
        hot = take(NT * 2 * NE, o2).rearrange("p (t c n) -> p t c n", t=NT, c=2)
        mask = take(NT * NE, o2).rearrange("p (t n) -> p t n", t=NT)
        rank = take(NT * NE, o2).rearrange("p (t n) -> p t n", t=NT)
        assert o2[0] <= attn_base + 4 * 6144 + 2 * D + KD * P + 3 * DE + 2 * D
        o3 = [x2_at[0] - 2700]
        assert o[0] <= o3[0], (o, o3)
        cum = take(NT * NE, o3).rearrange("p (t n) -> p t n", t=NT)
        prod = take(NT * 2 * NE, o3).rearrange("p (t c n) -> p t c n", t=NT, c=2)
        slot_f = take(256, o3)
        fill = take(256, o3)
        o = [attn_base]
        y2 = [take(2 * D, o) for _ in range(2)]
        fin = [take(D, o) for _ in range(2)]
        junk8 = take(D, o)
        stat8 = [take(2, o) for _ in range(2)]

        tab_in, small_in, wuk_in, wuq_in, uv_in, wo_in = (sem(n) for n in (
            "tables_in", "small_in", "wuk_in", "wuq_in", "wuv_in", "wo_in"))
        ws_zero, ws_ready, wsm_ready = sem("ws_zeroed"), sem("ws_loaded"), sem("ws_masked")
        setup_mm, setup_ev = sem("setup_turned"), sem("setup_copied")
        x_loaded = [sem(f"x_loaded{i}") for i in range(2)]
        x_sq, x_rstd, xn_ready = sem("x_squared"), sem("x_rstd"), sem("xn_ready")
        xt_mm = sem("xn_turned")
        xt_ev = [sem("xn_copied_act"), sem("xn_copied_dve")]
        w_loaded = [sem(f"w_in_loaded{i}") for i in range(2)]
        z_mm, z_ev = sem("z_summed"), sem("z_taken")
        z_stored = [sem(f"z_stored{i}") for i in range(2)]
        lat_stored = sem("latent_stored")
        lat_ready = sem("latent_ready")
        p_sq, p_rs, p_cn, p_kr = sem("latent_squared"), sem("latent_rstd"), sem("latent_normed"), sem("krope_ready")
        b_mm = [sem(f"bank{i}_written") for i in range(2)]
        b_ev = [sem(f"bank{i}_taken") for i in range(2)]
        qrope_done = sem("qrope_done")
        s_mm, s_nm, s_exp, s_rinv = sem("scores_ready"), sem("negmax_ready"), sem("probs_ready"), sem("rinv_ready")
        t_mm = [sem("probs_turned_lo"), sem("probs_turned_hi")]
        t_ev = [sem("probs_t_lo"), sem("probs_t_hi")]
        act_c, dve_c, pool_c = sem("act_steps"), sem("dve_steps"), sem("pool_steps")
        ends = sem("stage_ends")
        done = {"n": 0}
        idx_ready = sem("page_index_ready")
        pt_in = sem("page_table_in")
        c_in = [sem(f"cache_in{i}") for i in range(4)]
        c_tr = sem("cache_turned")
        c_ea, c_ed = sem("ckv_t_copied"), sem("kr_t_copied")
        c_s, c_mt, c_md, c_mb = sem("cache_scores"), sem("max_turned"), sem("max_diag"), sem("max_spread")
        c_sub, c_p, c_al, c_pv, c_acc = sem("shifted"), sem("cache_probs"), sem("alpha_ready"), sem("pv_ready"), sem("acc_done")
        late_in = sem("late_gains_in")
        c_mpart = sem("max_part")
        n_pe, n_dve, n_act = sem("new_pe"), sem("new_dve"), sem("new_act")
        z_in = [sem(f"z_in{i}") for i in range(2)]
        v_sq, v_rs, v_n = sem("v_squared"), sem("v_rstd"), sem("v_normed")
        mix_mm, sgu_ok, mrg_ok, at_ok = sem("mixed"), sem("sgu_ready"), sem("merged"), sem("gated_attn")
        mt_mm, mt_ev, y_mm, x2_ok = sem("merged_turned"), sem("merged_t"), sem("wo_summed"), sem("x2_ready")
        o_sq, o_rs, o_n, ot_mm, ot_ev = (sem(n) for n in ("x2_squared", "x2_rstd", "x2_normed", "x2n_turned", "x2n_t"))
        lg_mm, lg_ok = sem("logits_summed"), sem("logits_ready")
        xt_st = [sem(f"xt_stored{i}") for i in range(2)]
        v_st = sem("v_stored")
        r_pe, r_dve, r_sub, r_exp = sem("route_pe"), sem("route_dve"), sem("route_exp_in"), sem("route_exp_out")
        r_pos = sem("slot_positions")
        x_inv, v_inv, o_inv, f_inv = sem("x_inv"), sem("v_inv"), sem("x2_inv"), sem("f_inv")
        small_zero = sem("stats_zeroed")
        x2_cp = sem("x2_kept")
        fill_ok = sem("fill_ready")
        qrn_ready, idx_step, x_idx = sem("qrope_copied"), sem("page_index_steps"), sem("slot_index_steps")
        fill_in, scat_in, slots_in, slots_ok = sem("slots_filled"), sem("slots_scattered"), sem("slots_in"), sem("slot_index")
        e_w = [sem(f"expert_w{i}") for i in range(4)]
        e_x = [sem(f"expert_rows{i}") for i in range(2)]
        xg_zero = sem("rows_zeroed")
        e_xt, e_xe, e_g, e_u, e_si, e_h, e_ht, e_he = (sem(n) for n in (
            "rows_turned", "rows_t", "gate_summed", "up_summed", "gate_silu", "hidden", "hidden_turned", "hidden_t"))
        e_y = [sem("y_lo"), sem("y_hi")]
        e_ye = [sem("y_lo_copied"), sem("y_hi_copied")]
        e_sc = [sem(f"y_scattered{i}") for i in range(2)]
        yo_free = [sem(f"y_slot_free{i}") for i in range(2)]
        marks = sem("marks")
        moe_end = sem("experts_done")
        f_in = [sem(f"y_rows_in{i}") for i in range(2)]
        f_sum, f_sq, f_rs, f_ok = sem("f_summed"), sem("f_squared"), sem("f_rstd"), sem("f_ready")
        f_st = [sem(f"out_stored{i}") for i in range(2)]

        xp = x_prompt.rearrange("b s d -> (b s) d")
        xs = x_sample.rearrange("b s d -> (b s) d")
        yp = y_prompt.rearrange("b s d -> (b s) d")
        ys = y_sample.rearrange("b s d -> (b s) d")
        w_in_v = w_in[0].rearrange("(k p) n -> p k n", p=P)
        units, sched = attention_schedule()
        bank0_units = 6 * NT + NTP * H
        block = ctx.enter_context(nc.Block())

        def stage_end(eng, k):
            eng.drain().then_inc(ends, 1)
            eng.wait_ge(ends, 4 * k)

        @block.sync
        def _(sp):
            sp.dma_start(K, tables).then_inc(tab_in, 16)

            def x_load(t, s, rows, src):
                sp.dma_start(x_in[s][0:rows, :], src).then_inc(x_loaded[s], 16)

            x_load(0, 0, P, xp[0:P, :])
            x_load(1, 1, P, xp[P:2 * P, :])
            sp.dma_start(g1, norm1_g[0].partition_broadcast(P)).then_inc(small_in, 16)
            sp.dma_start(w_blk[0][:, :, 0:352], w_in_v[:, :, 0:352]).then_inc(w_loaded[0], 16)
            for dst, src in ((gq, q_norm_g[0]),
                             (gkv, kv_norm_g[0]), (rbias[:, 0:NG], b_rg[0]), (rbias[:, NG:], b_re[0])):
                sp.dma_start(dst, src.partition_broadcast(P)).then_inc(small_in, 16)
            sp.dma_start(ids_sb, ids).then_inc(small_in, 16)
            with nc.allow_non_contiguous_dma(reason="small tables"):
                sp.dma_start(w_router[:, :, 0:NG], w_rg[0].rearrange("(k p) n -> p k n", p=P)).then_inc(small_in, 16)
                sp.dma_start(w_router[:, :, NG:], w_re[0].rearrange("(k p) n -> p k n", p=P)).then_inc(small_in, 16)
                sp.dma_start(bs_t, b_s[0].rearrange("g i -> i g")).then_inc(small_in, 16)
                for b in range(NB):
                    sp.dma_start(bs_ts[TS * b:TS * b + TS, :], b_s[0, :, 0:TS].rearrange("g i -> i g")).then_inc(small_in, 16)
                pt = page_table.rearrange("b (c g) -> g (b c)", g=PG)
                for g in range(PG):
                    sp.dma_start(page_raw[8 * g:8 * g + 8, :], pt[g].partition_broadcast(8)).then_inc(pt_in, 16)
                sp.dma_start(w_uk_n, w_uk[0].rearrange("(c p) h d -> p c h d", p=P)).then_inc(wuk_in, 16)
                sp.dma_start(ws_n, w_s[0].rearrange("g i j -> i g j")).then_inc(ws_ready, 16)
                sp.wait_ge(ws_zero, 1)
                for b in range(NB):
                    sp.dma_start(ws_ns[TS * b:TS * b + TS, :, TS * b:TS * b + TS],
                                 w_s[0, :, 0:TS, 0:TS].rearrange("g i j -> i g j")).then_inc(ws_ready, 16)
            sp.dma_start(w_blk[1][:, :, 0:352], w_in_v[:, :, 352:704]).then_inc(w_loaded[1], 16)
            sp.dma_start(w_uq_sb, w_uq[0].rearrange("(r p) h d -> p r (h d)", p=P)).then_inc(wuq_in, 16)
            sp.dma_start(w_qr_sb, w_qr[0].rearrange("(r p) h d -> p r (h d)", p=P)).then_inc(wuq_in, 16)
            sp.dma_start(w_uv_sb, w_uv[0].rearrange("(c p) h d -> p c (h d)", p=P)).then_inc(uv_in, 16)
            with sp.Fori(0, 3) as i:
                for s in range(2):
                    sp.wait_ge(xn_ready, 2 * i + s + 1)
                    x_load(None, s, P, xp[bass.ds(2 * P * i + (s + 2) * P, P), :])
            sp.wait_ge(xn_ready, 7)
            x_load(8, 0, RS, xs)

            sp.wait_ge(z_mm, NT)
            sp.dma_start(w_blk[0], w_in_v[:, :, ZL:ZL + 512]).then_inc(w_loaded[0], 16)

            def block_moves(b, s, load):
                if load:
                    sp.wait_ge(z_mm, NT * 2 + NT * b)
                    sp.dma_start(w_blk[1 - s], w_in_v[:, :, bass.ds(512 * b + ZL + 512, 512)]).then_inc(w_loaded[1 - s], 16)
                cols = [z_act[t * P:t * P + rows_of(t), bass.ds(512 * b, 512)] for t in range(NT)]
                for t in range(NT):
                    u = (s * NT + t) % 2
                    r = rows_of(t)
                    sp.wait_ge(z_ev, NT * 2 + NT * b + t + 1)
                    sp.sem_inc(marks, 1)
                    sp.dma_start(cols[t], zst[u][0:r, :]).then_inc(z_stored[u], 16)

            with sp.Fori(0, 3) as i:
                block_moves(2 * i, 0, True)
                block_moves(2 * i + 1, 1, True)
            block_moves(6, 0, True)
            block_moves(7, 1, False)

            sp.wait_ge(lat_ready, 2)
            sp.dma_start(ckv_prompt.rearrange("l b t p c -> p (l b t) c"), ckv_n[:, 0:NTP, :]).then_inc(lat_stored, 16)
            sp.dma_start(kr_prompt.rearrange("l b t p c -> p (l b t) c"), kr_n[:, 0:NTP, :]).then_inc(lat_stored, 16)
            sp.dma_start(ckv_sample.rearrange("l b t c -> (l b t) c"), ckv_n[0:RS, NTP, :]).then_inc(lat_stored, 16)
            sp.dma_start(kr_sample.rearrange("l b t c -> (l b t) c"), kr_n[0:RS, NTP, :]).then_inc(lat_stored, 16)
            sp.wait_ge(lat_stored, 64)

            sp.wait_ge(ends, 8)
            for dst, src in ((g2, norm2_g[0]), (gf, norm_f_g), (gv, sgu_norm_g[0])):
                sp.dma_start(dst, src.partition_broadcast(P)).then_inc(late_in, 16)
            sp.wait_ge(ends, 12)
            for u in range(2):
                sp.wait_ge(z_stored[u], 16 * (8 * NT // 2) + 16)

            def z_load(s, r, z_src, x_src):
                sp.dma_start(zt[s][0:r, :], z_src).then_inc(z_in[s], 16)
                sp.dma_start(xr[s][0:r, :], x_src).then_inc(z_in[s], 16)

            z_load(0, P, z_act[0:P, :], xp[0:P, :])
            sp.dma_start(w_o_sb, w_o[0].rearrange("(k p) n -> p k n", p=P)).then_inc(wo_in, 16)
            z_load(1, P, z_act[P:2 * P, :], xp[P:2 * P, :])
            with sp.Fori(0, 3) as i:
                for s in range(2):
                    sp.wait_ge(o_n, 2 * i + s + 1)
                    sp.wait_ge(x2_cp, 2 * i + s + 1)
                    z_load(s, P, z_act[bass.ds(2 * P * i + (s + 2) * P, P), :], xp[bass.ds(2 * P * i + (s + 2) * P, P), :])
                    sp.dma_start(xt_rows[bass.ds(2 * P * i + s * P, P), :], xo[s]).then_inc(xt_st[s], 16)
            sp.wait_ge(o_n, 7)
            sp.wait_ge(x2_cp, 7)
            z_load(0, RS, z_act[8 * P:TOK, :], xs)
            for t in range(6, NT):
                sp.wait_ge(o_n, t + 1)
                r = rows_of(t)
                sp.dma_start(xt_rows[t * P:t * P + r, :], xo[t % 2][0:r, :]).then_inc(xt_st[t % 2], 16)
            sp.wait_ge(v_n, NT)
            sp.dma_start(v_sample.rearrange("l b t c -> (l b t) c"), zt[0][0:RS, D:2 * D]).then_inc(v_st, 16)
            sp.wait_ge(v_st, 16)

            sp.wait_ge(fill_ok, 1)
            slots_v = slot_rows.rearrange("(b r) c -> b (r c)", r=P)
            sp.dma_start(slots_v, fill[0:NBLK, :].bitcast(I32)).then_inc(fill_in, 16)

            def w_load(s, e):
                g, u, dn = w_e[s]
                for dst, src, k in ((g, w_gate, KD), (u, w_up, KD), (dn, w_down, 2)):
                    sp.dma_start(dst.rearrange("p k n -> p (k n)"),
                                 src[0, bass.ds(e, 1)].rearrange("e (p k) n -> p (e k n)", p=P)).then_inc(e_w[s], 16)

            sp.wait_ge(ends, 16)
            for s in range(4):
                w_load(s, s)
            sp.wait_ge(scat_in, 16 * 2 * NT)
            sp.dma_start(fill[0:NBLK, :].bitcast(I32), slots_v).then_inc(slots_in, 16)
            with sp.Fori(0, 15) as i:
                for s in range(4):
                    sp.wait_ge(e_y[1], 4 * i + s + 1)
                    w_load(s, 4 * i + s + 4)
            sp.wait_ge(slots_ok, 1)
            total = sp.value_load(ovf_id[0:1, NOVF:NOVF + 1], min_val=0, max_val=NOVF)
            sp.wait_ge(e_y[1], NE)
            with sp.Fori(0, NOVF) as j:
                with sp.If(total > j):
                    e = sp.value_load(ovf_id[0:1, bass.ds(j, 1)], min_val=0, max_val=NE - 1)
                    sp.wait_ge(e_y[1], NE + j)
                    w_load(0, e)

            sp.wait_ge(moe_end, 1)
            yr = y_rows.rearrange("(n c) d -> n (c d)", c=2)
            sp.dma_start(y2[0], yr[0:P, :]).then_inc(f_in[0], 16)
            sp.dma_start(y2[1], yr[P:2 * P, :]).then_inc(f_in[1], 16)
            with sp.Fori(0, 3) as i:
                for s in range(2):
                    sp.wait_ge(f_sum, 2 * i + s + 1)
                    sp.dma_start(y2[s], yr[bass.ds(2 * P * i + (s + 2) * P, P), :]).then_inc(f_in[s], 16)
                    sp.wait_ge(f_ok, 2 * i + s + 1)
                    sp.dma_start(yp[bass.ds(2 * P * i + s * P, P), :], fin[s]).then_inc(f_st[s], 16)
            sp.wait_ge(f_sum, 7)
            sp.dma_start(y2[0][0:RS, :], yr[8 * P:TOK, :]).then_inc(f_in[0], 16)
            for t in range(6, NT):
                sp.wait_ge(f_ok, t + 1)
                if t < NTP:
                    sp.dma_start(yp[t * P:(t + 1) * P, :], fin[t % 2]).then_inc(f_st[t % 2], 16)
                else:
                    sp.dma_start(ys, fin[0][0:RS, :]).then_inc(f_st[0], 16)
            sp.wait_ge(f_st[0], 16 * 6)
            sp.wait_ge(f_st[1], 16 * 5)

        @block.tensor
        def _(pe):
            mm, tr = nc.tensor.matmul, nc.tensor.transpose
            pe.wait_ge(tab_in, 16)
            pe.wait_ge(wuk_in, 16)
            for u in range(4):
                b = 6 + u % 2
                if u >= 2:
                    pe.wait_ge(setup_ev, u - 1)
                for i in range(4):
                    h, c = 2 * u + i // 2, i % 2
                    last = tr(bank(b)[:, P * i:P * i + P], w_uk_n[:, c, h, :], ident)
                last.then_inc(setup_mm, 1)
            pe.wait_ge(wsm_ready, 1)
            for u in range(2):
                pe.wait_ge(setup_ev, 3 + u)
                for i in range(4):
                    last = tr(bank(6 + u)[:, P * i:P * i + P], ws_n[:, 4 * u + i, :], ident)
                last.then_inc(setup_mm, 1)
            pe.wait_ge(setup_ev, 5)
            for g in range(KD):
                last = tr(bank(6)[0:RS, RS * g:RS * g + RS], ws_ns[0:RS, g, :], ident[0:RS, 0:RS])
            last.then_inc(setup_mm, 1)

            def turn_x(n, s, r):
                pe.wait_ge(xn_ready, n + 1)
                pe.wait_ge(xt_ev[0], n + 1)
                pe.wait_ge(xt_ev[1], n + 1)
                for k in range(KD):
                    last = tr(bank(2 * s, 2)[:, P * k:P * k + r], xn[s][0:r, P * k:P * k + P], ident[0:r, 0:r])
                last.then_inc(xt_mm, 1)

            with pe.Fori(0, 4) as i:
                for s in range(2):
                    turn_x(2 * i + s, s, P)
            turn_x(8, 0, RS)
            pe.wait_ge(xt_ev[0], NT + 2)
            pe.wait_ge(xt_ev[1], NT + 2)

            def z_block(n, s, w, i_loaded, first=False):
                pe.wait_ge(w_loaded[s], 16 * i_loaded)
                for t in range(NT):
                    r = rows_of(t)
                    u = (s * NT + t) % 2
                    if not (first and t < 2):
                        pe.wait_ge(z_ev, NT * n + t - 1)
                    for k in range(KD):
                        last = mm(bank(4 + u)[0:r, 0:w], xn_t[:, k, t * P:t * P + r], w_blk[s][:, k, 0:w],
                                  start=(k == 0), stop=(k == KD - 1))
                    last.then_inc(z_mm, 1)

            z_block(0, 0, 352, 1, True)
            z_block(1, 1, 352, 1)
            with pe.Fori(0, 4) as i:
                z_block(2 * i + 2, 0, 512, i + 2)
                z_block(2 * i + 3, 1, 512, i + 2)
            pe.wait_ge(z_ev, 10 * NT)
            stage_end(pe, 1)

            pe.wait_ge(wuq_in, 32)
            pe.wait_ge(uv_in, 16)
            pe.wait_ge(setup_ev, 7)
            used = [0, 0]

            def open_bank(b):
                if used[b]:
                    pe.wait_ge(b_ev[b], used[b])
                used[b] += 1

            for what, n in sched:
                if what == "Q":
                    t, r, s = n, rows_of(n), n % 2
                    pe.wait_ge(p_cn, t + 1)
                    pe.wait_ge(p_kr, t + 1)
                    open_bank(0)
                    for i in range(3):
                        tr(bank(0)[:, P * i:P * i + r], cq[0:r, P * i:P * i + P], ident[0:r, 0:r])
                    tr(bank(0)[0:DR, 384:384 + r], kr_n[0:r, t, :], ident[0:r, 0:r]).then_inc(b_mm[0], 1)
                    open_bank(1)
                    for c in range(2):
                        last = tr(bank(1)[:, P * c:P * c + r], ckv_n[0:r, t, P * c:P * c + P], ident[0:r, 0:r])
                    last.then_inc(b_mm[1], 1)
                    pe.wait_ge(b_ev[0], used[0])
                    for u in range(2):
                        open_bank(u)
                        for i in range(4):
                            h = 4 * u + i
                            for c in range(3):
                                last = mm(bank(u)[:, P * i:P * i + r], w_uq_sb[:, c, P * h:P * h + P], cq_t[:, c, 0:r],
                                          start=(c == 0), stop=(c == 2))
                        last.then_inc(b_mm[u], 1)
                    open_bank(0)
                    for c in range(3):
                        last = mm(bank(0)[0:r, :], cq_t[:, c, 0:r], w_qr_sb[:, c, :], start=(c == 0), stop=(c == 2))
                    last.then_inc(b_mm[0], 1)
                    for u in range(4):
                        b = 1 - u % 2
                        open_bank(b)
                        for i in range(4):
                            h, c = 2 * u + i // 2, i % 2
                            last = mm(bank(b)[:, P * i:P * i + r], w_uk_t[:, h, P * c:P * c + P], qn_t[:, h, 0:r],
                                      start=True, stop=True)
                        last.then_inc(b_mm[b], 1)
                    pe.wait_ge(qrope_done, t + 1)
                    for u in range(2):
                        b = 1 - u
                        open_bank(b)
                        for i in range(4):
                            h = 4 * u + i
                            last = tr(bank(b)[0:DR, P * i:P * i + r], qr_r[0:r, DR * h:DR * h + DR], ident[0:r, 0:r])
                        last.then_inc(b_mm[b], 1)
                    pe.wait_ge(b_ev[0], used[0])
                    pe.wait_ge(b_ev[1], used[1])
                elif what == "S":
                    t, h = units[n]
                    s, sl = t % 2, n % 2
                    if n >= 2:
                        pe.wait_ge(s_exp, n - 1)
                    for c0 in range(0, P * (t + 1), 512):
                        w = min(512, P * (t + 1) - c0)
                        out = bank(2 + 2 * sl, 2)[:, c0:c0 + w]
                        mm(out, ql_t[s][:, h, 0, :], ckv_t[:, 0, c0:c0 + w], start=True, stop=False)
                        mm(out, ql_t[s][:, h, 1, :], ckv_t[:, 1, c0:c0 + w], start=False, stop=False)
                        diag = c0 <= P * t < c0 + w
                        last = mm(out, qr_t[s][0:DR, h, :], kr_t[0:DR, c0:c0 + w], start=False, stop=True)
                        if diag:
                            last = mm(bank(2 + 2 * sl, 2)[:, P * t:P * t + P], ident, const("negmask"),
                                      start=False, stop=True, skip_group_check=True)
                    last.then_inc(s_mm, 1)
                elif what == "T":
                    t, h = units[n]
                    pe.wait_ge(s_exp, n + 1)
                    for half in range(2):
                        js = range(4 * half, min(4 * half + 4, t + 1))
                        if not js:
                            continue
                        k = n if half == 0 else n - 4 * H
                        if k >= 1:
                            pe.wait_ge(t_ev[half], k)
                        for j in js:
                            last = tr(bank(6 + half)[:, P * (j % 4):P * (j % 4) + P], prob[n % 2][:, P * j:P * j + P], ident)
                        last.then_inc(t_mm[half], 1)
                elif what == "PV":
                    t, h = units[n]
                    b = n % 2
                    pe.wait_ge(t_ev[0], n + 1)
                    if t >= 4:
                        pe.wait_ge(t_ev[1], n - 4 * H + 1)
                    open_bank(b)
                    for c in range(2):
                        for j in range(t + 1):
                            last = mm(bank(b)[:, P * c:P * c + P], ckv_n[:, j, P * c:P * c + P], prob_t[b][:, j, :],
                                      start=(j == 0), stop=(j == t))
                    last.then_inc(b_mm[b], 1)
                elif what == "UV":
                    t, h = units[n]
                    b = n % 2
                    open_bank(b)
                    for c in range(2):
                        last = mm(bank(b)[:, 0:DV], pv_t[b][:, c, :], w_uv_sb[:, c, DV * h:DV * h + DV],
                                  start=(c == 0), stop=(c == 1))
                    last.then_inc(b_mm[b], 1)
            pe.wait_ge(b_ev[0], used[0])
            pe.wait_ge(b_ev[1], used[1])
            stage_end(pe, 2)

            pe.wait_ge(n_dve, 1)
            new = bank(6)[0:RS, 0:256]
            mm(new, ckv_t[:, 0, SEQ:TOK], qs[:, 0, :], start=True, stop=False)
            mm(new, ckv_t[:, 1, SEQ:TOK], qs[:, 1, :], start=False, stop=False)
            mm(new, kr_t[0:DR, SEQ:TOK], qsr[0:DR, :], start=False, stop=True).then_inc(n_pe, 1)
            pe.wait_ge(n_dve, 2)
            for g in range(2):
                last = tr(bank(7)[:, RS * g:RS * g + RS], s_new[0:RS, P * g:P * g + P], ident[0:RS, 0:RS])
            last.then_inc(n_pe, 1)
            pe.wait_ge(n_dve, 3)
            mm(bank(6)[:, 0:256], ones, m_diag2, start=True, stop=True).then_inc(n_pe, 1)
            pe.wait_ge(n_act, 1)
            for c in range(2):
                last = mm(bank(7)[:, 256 * c:256 * c + 256], ckv_n[0:RS, NTP, P * c:P * c + P], p_new[0:RS, :],
                          start=True, stop=True)
            last.then_inc(n_pe, 1)
            pe.wait_ge(n_dve, 4)

            def max_turn(n):
                pe.wait_ge(c_mpart, n + 1)
                tr(bank(6)[0:32, 0:P], m_part, ident).then_inc(c_mt, 1)

            def max_spread(n):
                pe.wait_ge(c_md, n + 1)
                mm(bank(6)[:, P:P + 32], ones[0:32, :], m_diag[0:32, :], start=True, stop=True).then_inc(c_mb, 1)

            def turn_score(n, q, i_in, col, before):
                pe.wait_ge(c_in[q], 32 * i_in)
                for g in range(PG // 2 + 1):
                    if g < PG // 2:
                        v = g % 2
                        pe.wait_ge(c_ea, 8 * n + g + 1)
                        pe.wait_ge(c_ed, 8 * n + g + 1)
                        for i in range(2):
                            rr = 2 * g + i
                            for c in range(2):
                                tr(bank(2 * v)[:, P * (2 * i + c):P * (2 * i + c) + P], ck[q][:, rr, P * c:P * c + P], ident)
                            last = tr(bank(2 * v + 1)[0:DR, P * i:P * i + P], kr[q][:, rr, :], ident)
                        last.then_inc(c_tr, 1)
                    if g >= 1:
                        pe.wait_ge(c_ea, 8 * n + g + 2)
                        pe.wait_ge(c_ed, 8 * n + g + 2)
                        for i in range(2):
                            rr = 2 * g - 2 + i
                            out = bank(4 + q % 2)[:, 32 * rr:32 * rr + 32]
                            mm(out, ck_t[:, rr % 4, 0, :], qs[:, 0, col], start=True, stop=False)
                            mm(out, ck_t[:, rr % 4, 1, :], qs[:, 1, col], start=False, stop=False)
                            last = mm(out, kr_tt[0:DR, rr % 4, :], qsr[0:DR, col], start=False, stop=True)
                    if g in before:
                        before[g]()
                last.then_inc(c_s, 1)

            def weigh(n, q):
                pe.wait_ge(c_p, n + 1)
                pe.wait_ge(c_acc, n + 1)
                for c in range(2):
                    for rr in range(PG):
                        last = mm(bank(7)[:, 32 * c:32 * c + 32], ck[q][:, rr, P * c:P * c + P],
                                  p_exp[q % 2][:, 32 * rr:32 * rr + 32], start=(rr == 0), stop=(rr == PG - 1))
                last.then_inc(c_pv, 1)

            turn_score(0, 0, 1, slice(0, 32), {})

            def batch(i, last_batch):
                for q in range(4):
                    n = 4 * i + q
                    parts = {1: lambda n=n: max_turn(n), 3: lambda n=n: max_spread(n)}
                    if q < 3:
                        turn_score(n + 1, q + 1, i + 1, bass.ds(32 * i, 32), parts)
                    elif not last_batch:
                        turn_score(n + 1, 0, i + 2, bass.ds(32 * i + 32, 32), parts)
                    else:
                        parts[1]()
                        parts[3]()
                    weigh(n, q)

            with pe.Fori(0, NB - 1) as i:
                batch(i, False)
            batch(NB - 1, True)
            pe.wait_ge(c_acc, NCH + 1)
            mm(bank(6)[:, 0:256], ones, l_all, start=True, stop=True).then_inc(n_pe, 1)
            pe.wait_ge(n_dve, 5)
            for h in range(H):
                for c in range(2):
                    last = mm(bank(0, 2)[0:RS, DV * h:DV * h + DV], o_lat[:, c, RS * h:RS * h + RS],
                              w_uv_sb[:, c, DV * h:DV * h + DV], start=(c == 0), stop=(c == 1))
            last.then_inc(n_pe, 1)
            pe.wait_ge(n_act, 2)
            stage_end(pe, 3)

            pe.wait_ge(wo_in, 16)

            def merge(n, s, r, wst):
                pe.wait_ge(v_n, n + 1)
                pe.wait_ge(sgu_ok, n + 1)
                for g in range(KD):
                    last = mm(bank(0, 2)[0:r, P * g:P * g + P], wst[0:r, g, 0:r], zt[s][0:r, D + P * g:D + P * g + P],
                              start=True, stop=True)
                last.then_inc(mix_mm, 1)
                pe.wait_ge(mrg_ok, n + 1)
                pe.wait_ge(ot_ev, n + 1)
                for k in range(KD):
                    last = tr(bank(2, 2)[:, P * k:P * k + r], zt[s][0:r, P * k:P * k + P], ident[0:r, 0:r])
                last.then_inc(mt_mm, 1)
                pe.wait_ge(mt_ev, n + 1)
                for half in range(2):
                    for k in range(KD):
                        last = mm(bank(4 + half)[0:r, :], m_t[:, k, 0:r], w_o_sb[:, k, 512 * half:512 * half + 512],
                                  start=(k == 0), stop=(k == KD - 1))
                last.then_inc(y_mm, 1)
                pe.wait_ge(o_n, n + 1)
                for k in range(KD):
                    last = tr(bank(2, 2)[:, P * k:P * k + r], xo[s][0:r, P * k:P * k + P], ident[0:r, 0:r])
                last.then_inc(ot_mm, 1)
                pe.wait_ge(ot_ev, n + 2)
                pe.wait_ge(lg_ok, n + 1)
                for k in range(KD):
                    last = mm(bank(6)[0:r, 0:72], x2_t[:, k, 0:r], w_router[:, k, :], start=(k == 0), stop=(k == KD - 1))
                last.then_inc(lg_mm, 1)

            with pe.Fori(0, 4) as i:
                for s in range(2):
                    merge(2 * i + s, s, P, ws_t)
            merge(8, 0, RS, ws_ts)
            pe.wait_ge(lg_ok, NT + 1)
            stage_end(pe, 4)

            pe.wait_ge(r_dve, 1)
            for t in range(NT):
                out = bank(t // 8)[:, NE * (t % 8):NE * (t % 8) + NE]
                mm(out, const("before"), mask[:, t, :], start=True, stop=False)
                mm(out, ones, cum[:, t, :], start=False, stop=True)
            mm(bank(1)[:, NE:2 * NE], ones, rank[:, 0, :], start=True, stop=True).then_inc(r_pe, 1)
            pe.wait_ge(r_dve, 2)
            for c in range(2):
                last = tr(bank(2)[:, P * c:P * c + NBLK], slot_f.rearrange("p (r c) -> p c r", c=2)[0:NBLK, c, :],
                          ident[0:NBLK, 0:NBLK])
            last.then_inc(r_pe, 1)
            pe.wait_ge(slots_ok, 1)

            def expert(n, sw, s, i_w, i_x):
                g, u, dn = w_e[sw]
                pe.wait_ge(e_x[s], 16 * i_x)
                for k in range(KD):
                    last = tr(bank(0, 2)[:, P * k:P * k + P], xg[s].rearrange("p (n k) -> p k n", k=KD)[:, k, :], ident)
                last.then_inc(e_xt, 1)
                pe.wait_ge(e_w[sw], 48 * i_w)
                pe.wait_ge(e_xe, 2 * n + 2)
                for k in range(KD):
                    last = mm(bank(2)[:, 0:DE], xg_t[:, k, :], g[:, k, :], start=(k == 0), stop=(k == KD - 1))
                last.then_inc(e_g, 1)
                for k in range(KD):
                    last = mm(bank(3)[:, 0:DE], xg_t[:, k, :], u[:, k, :], start=(k == 0), stop=(k == KD - 1))
                last.then_inc(e_u, 1)
                pe.wait_ge(e_h, n + 1)
                for f in range(2):
                    last = tr(bank(4)[:, P * f:P * f + P], h_n.rearrange("p (n f) -> p f n", f=2)[:, f, :], ident)
                last.then_inc(e_ht, 1)
                pe.wait_ge(e_he, n + 1)
                for half in range(2):
                    pe.wait_ge(e_ye[half], n + 1)
                    for f in range(2):
                        last = mm(bank(5 + half), h_t[:, f, :], dn[:, f, 512 * half:512 * half + 512],
                                  start=(f == 0), stop=(f == 1))
                    last.then_inc(e_y[half], 1)

            with pe.Fori(0, 16) as i:
                for s in range(4):
                    expert(4 * i + s, s, s % 2, i + 1, 2 * i + s // 2 + 1)
            total = pe.value_load(ovf_id[0:1, NOVF:NOVF + 1], min_val=0, max_val=NOVF)
            with pe.Fori(0, NOVF) as j:
                with pe.If(total > j):
                    expert(NE + j, 0, 0, 17 + j, 33 + j)

        @block.scalar
        def _(act):
            A = nc.scalar.activation
            act.sem_inc(xt_ev[0], 2)
            act.sem_inc(c_ea, 2)
            act.sem_inc(ot_ev, 1)
            act.sem_inc(e_ye[0], 1)
            for u in range(2):
                act.sem_inc(z_stored[u], 16)
            act.wait_ge(tab_in, 16)
            act.wait_ge(small_zero, 1)

            for u in range(4):
                act.wait_ge(setup_mm, u + 1)
                nc.scalar.copy(w_uk_t[:, 2 * u:2 * u + 2, :].rearrange("p h c -> p (h c)"), bank(6 + u % 2)).then_inc(setup_ev, 1)
            for u in range(2):
                act.wait_ge(setup_mm, 5 + u)
                nc.scalar.copy(ws_t[:, 4 * u:4 * u + 4, :].rearrange("p g i -> p (g i)"), bank(6 + u)).then_inc(setup_ev, 1)
            act.wait_ge(setup_mm, 7)
            nc.scalar.copy(ws_ts[0:RS, :, :].rearrange("p g i -> p (g i)"), bank(6)[0:RS, 0:RS * KD]).then_inc(setup_ev, 1)

            def square_x(n, s, r, i_l):
                act.wait_ge(x_loaded[s], 16 * i_l)
                A(junk1[0:r, :], x_in[s][0:r, :], ACT.Square, scale=D ** -0.5, accum_out=small[0:r, s:s + 1]).then_inc(x_sq, 1)
                act.wait_ge(x_sq, n + 1)
                A(small[0:r, 2 + s:3 + s], small[0:r, s:s + 1], ACT.Sqrt, bias=eps[0:r]).then_inc(x_rstd, 1)

            def copy_x(n, s, r, dst):
                act.wait_ge(xt_mm, n + 1)
                nc.scalar.copy(dst, bank(2 * s).rearrange("p (k n) -> p k n", k=4)[:, :, 0:r]).then_inc(xt_ev[0], 1)

            with act.Fori(0, 4) as i:
                for s in range(2):
                    square_x(2 * i + s, s, P, i + 1)
                    copy_x(2 * i + s, s, P, xn_t[:, 0:4, bass.ds(2 * P * i + P * s, P)])
            square_x(8, 0, RS, 5)
            copy_x(8, 0, RS, xn_t[:, 0:4, SEQ:TOK])

            def take_z(n, s):
                for t in range(NT):
                    r = rows_of(t)
                    u = (s * NT + t) % 2
                    act.wait_ge(z_mm, NT * n + t + 1)
                    nc.scalar.copy(z0[0:r, t, 352 * s:352 * s + 352], bank(4 + u)[0:r, 0:352]).then_inc(z_ev, 1)

            take_z(0, 0)
            take_z(1, 1)

            def take_pair(i, func):
                for s in range(2):
                    for t in range(NT):
                        r = rows_of(t)
                        u = (s * NT + t) % 2
                        act.wait_ge(z_mm, 2 * NT * i + 2 * NT + s * NT + t + 1)
                        act.wait_ge(z_stored[u], 16 * NT * i + 16 * ((s * NT + t) // 2) + 16)
                        A(zst[u][0:r, :], bank(4 + u)[0:r, :], func).then_inc(z_ev, 1)

            with act.Fori(0, 2) as i:
                take_pair(i, ACT.Gelu_apprx_tanh)
            with act.Fori(2, 4) as i:
                take_pair(i, ACT.Sigmoid)
            act.wait_ge(p_sq, 1)
            A(stat, stat, ACT.Sqrt, bias=eps).then_inc(p_rs, 1)
            for u in range(2):
                act.wait_ge(z_stored[u], 16 * (8 * NT // 2) + 16)
            stage_end(act, 1)

            got = 0
            for what, n in sched:
                if what == "Q":
                    t, r, s = n, rows_of(n), n % 2

                    def from0(dst, src):
                        nonlocal got
                        got += 1
                        act.wait_ge(b_mm[0], got)
                        nc.scalar.copy(dst, src).then_inc(b_ev[0], 1)

                    b0 = bank(0).rearrange("p (i n) -> p i n", i=4)
                    got += 1
                    act.wait_ge(b_mm[0], got)
                    nc.scalar.copy(kr_t[0:DR, t * P:t * P + r], b0[0:DR, 3, 0:r])
                    nc.scalar.copy(cq_t[:, :, 0:r], b0[:, 0:3, 0:r]).then_inc(b_ev[0], 1)
                    from0(qn_t[:, 0:4, 0:r], b0[:, :, 0:r])
                    from0(qr_n[0:r, :], bank(0)[0:r, :])
                    act.wait_ge(b_ev[0], got)
                    act.sem_inc(qrn_ready, 1)
                    for h in (2, 6):
                        from0(ql_t[s][:, h:h + 2, :, 0:r].rearrange("p h c n -> p (h c) n"), b0[:, :, 0:r])
                    from0(qr_t[s][0:DR, 4:8, 0:r], b0[0:DR, :, 0:r])
                elif what == "S":
                    t, h = units[n]
                    w = P * (t + 1)
                    act.wait_ge(s_nm, n + 1)
                    A(prob[n % 2][:, 0:w], bank(2 + 2 * (n % 2), 2)[:, 0:w], ACT.Exp, bias=negmax[:, n:n + 1], scale=SCALE,
                      accum_out=psumq[:, n:n + 1]).then_inc(s_exp, 1)
                elif what == "T":
                    t, h = units[n]
                    w = P * min(t + 1, 4)
                    act.wait_ge(t_mm[0], n + 1)
                    nc.scalar.copy(prob_t[n % 2][:, 0:w // P, :].rearrange("p j n -> p (j n)"), bank(6)[:, 0:w]).then_inc(t_ev[0], 1)
                elif what != "prep" and n % 2 == 0:
                    t, h = units[n]
                    got += 1
                    act.wait_ge(b_mm[0], got)
                    if what == "PV":
                        nc.scalar.copy(pv_t[0].rearrange("p c n -> p (c n)"), bank(0)[:, 0:2 * P]).then_inc(b_ev[0], 1)
                    else:
                        act.wait_ge(s_rinv, n + 1)
                        A(attn[:, t, DV * h:DV * h + DV], bank(0)[:, 0:DV], ACT.Copy, scale=rinv[:, n:n + 1]).then_inc(b_ev[0], 1)
            stage_end(act, 2)

            act.wait_ge(n_dve, 3)
            act.wait_ge(c_sub, 1)
            A(p_new[0:RS, :], s_new[0:RS, :], ACT.Exp, scale=SCALE).then_inc(n_act, 1)
            act.wait_ge(n_dve, 4)

            def turned(n, parts):
                for g in range(PG // 2):
                    act.wait_ge(c_tr, 8 * n + g + 1)
                    nc.scalar.copy(ck_t[:, 2 * (g % 2):2 * (g % 2) + 2, :, :].rearrange("p r c n -> p (r c n)"), bank(2 * (g % 2))).then_inc(c_ea, 1)
                    if g in parts:
                        parts[g]()

            def exps(n, q):
                act.wait_ge(c_sub, n + 2)
                A(alpha, m_dif, ACT.Exp, scale=SCALE).then_inc(c_al, 1)
                A(p_exp[q % 2], p_sub, ACT.Exp, scale=SCALE).then_inc(c_p, 1)

            turned(0, {})

            def batch(i, last_batch):
                for q in range(4):
                    n = 4 * i + q
                    if q < 3 or not last_batch:
                        turned(n + 1, {5: lambda n=n, q=q: exps(n, q)})
                    else:
                        exps(n, q)

            with act.Fori(0, NB - 1) as i:
                batch(i, False)
            batch(NB - 1, True)
            act.wait_ge(n_pe, 6)
            nc.scalar.copy(attn[0:RS, NTP, :], bank(0, 2)[0:RS, :]).then_inc(n_act, 1)
            stage_end(act, 3)

            def merge(n, s, r, i_in):
                act.wait_ge(z_in[s], 32 * i_in)
                A(junk5[0:r, :], zt[s][0:r, D:2 * D], ACT.Square, scale=D ** -0.5, accum_out=stat5[s][0:r, 0:1]).then_inc(v_sq, 1)
                act.wait_ge(v_sq, n + 1)
                A(stat5[s][0:r, 0:1], stat5[s][0:r, 0:1], ACT.Sqrt, bias=eps[0:r]).then_inc(v_rs, 1)
                act.wait_ge(mt_mm, n + 1)
                nc.scalar.copy(m_t[:, :, 0:r], bank(2, 2).rearrange("p (k n) -> p k n", k=KD)[:, :, 0:r]).then_inc(mt_ev, 1)
                act.wait_ge(x2_ok, n + 1)
                A(junk5[0:r, :], xr[s][0:r, :], ACT.Square, scale=D ** -0.5, accum_out=stat5[s][0:r, 2:3]).then_inc(o_sq, 1)
                act.wait_ge(o_sq, n + 1)
                A(stat5[s][0:r, 2:3], stat5[s][0:r, 2:3], ACT.Sqrt, bias=eps[0:r]).then_inc(o_rs, 1)
                act.wait_ge(ot_mm, n + 1)
                nc.scalar.copy(x2_t[:, :, 0:r], bank(2, 2).rearrange("p (k n) -> p k n", k=KD)[:, :, 0:r]).then_inc(ot_ev, 1)

            with act.Fori(0, 4) as i:
                for s in range(2):
                    merge(2 * i + s, s, P, i + 1)
            merge(8, 0, RS, 5)
            stage_end(act, 4)

            act.wait_ge(r_sub, 1)
            A(g_exp, g_sub, ACT.Exp)
            A(d_exp, d_sub, ACT.Exp).then_inc(r_exp, 1)

            def expert(n):
                act.wait_ge(e_xt, n + 1)
                nc.scalar.copy(xg_t[:, 0:4, :].rearrange("p k n -> p (k n)"), bank(0)).then_inc(e_xe, 1)
                act.wait_ge(e_g, n + 1)
                A(h_s, bank(2)[:, 0:DE], ACT.Silu).then_inc(e_si, 1)

            def expert_out(n, s, i_s):
                act.wait_ge(e_y[0], n + 1)
                act.wait_ge(yo_free[s], i_s)
                nc.scalar.copy(yo[s][:, 0:512], bank(5)).then_inc(e_ye[0], 1)

            with act.Fori(0, 16) as i:
                for s in range(4):
                    expert(4 * i + s)
                    expert_out(4 * i + s, s % 2, 2 * i + s // 2 + 1)
            total = act.value_load(ovf_id[0:1, NOVF:NOVF + 1], min_val=0, max_val=NOVF)
            with act.Fori(0, NOVF) as j:
                with act.If(total > j):
                    expert(NE + j)
                    expert_out(NE + j, 0, 33 + j)

            def last_norm(n, s, r):
                act.wait_ge(f_sum, n + 1)
                A(junk8[0:r, :], fin[s][0:r, :], ACT.Square, scale=D ** -0.5, accum_out=stat8[s][0:r, 0:1]).then_inc(f_sq, 1)
                act.wait_ge(f_sq, n + 1)
                A(stat8[s][0:r, 0:1], stat8[s][0:r, 0:1], ACT.Sqrt, bias=eps[0:r]).then_inc(f_rs, 1)

            with act.Fori(0, 4) as i:
                for s in range(2):
                    last_norm(2 * i + s, s, P)
            last_norm(8, 0, RS)

        @block.gpsimd
        def _(pool):
            G = nc.gpsimd
            step = Count(pool, pool_c)
            for u in range(2):
                pool.sem_inc(yo_free[u], 1)
                pool.sem_inc(xt_st[u], 16)
                pool.sem_inc(f_st[u], 16)

            G.memset(ws_ns[0:RS, :, :], 0.0).then_inc(ws_zero, 1)
            pool.wait_ge(tab_in, 16)
            pool.wait_ge(pt_in, 16 * PG)
            step(G.tensor_copy(page_idx, page_raw))
            G.tensor_scalar(page_int, page_idx, 8.0, const("p_mod"), ALU.mult, ALU.add).then_inc(idx_ready, 1)
            pool.wait_ge(ws_ready, 16 * (1 + NB))
            for g in range(KD):
                G.tensor_tensor(ws_n[:, g, :], ws_n[:, g, :], const("keep"), ALU.mult)
                last = G.tensor_tensor(ws_ns[0:RS, g, :], ws_ns[0:RS, g, :], const("keep_s")[0:RS, :], ALU.mult)
            last.then_inc(wsm_ready, 1)
            stage_end(pool, 1)

            for what, t in sched:
                r = rows_of(t) if what in ("prep", "Q") else 0
                if what == "prep":
                    c, sn = cos[0:r, t, :], sin[0:r, t, :]
                    x1, x2_ = z0[0:r, t, QL + KVL:QL + KVL + 32], z0[0:r, t, QL + KVL + 32:ZL]
                    G.tensor_tensor(kr_tmp[0:r, 0:32], x1, c, ALU.mult)
                    G.tensor_tensor(kr_tmp[0:r, 32:64], x2_, sn, ALU.mult)
                    G.tensor_tensor(kr_tmp[0:r, 64:96], x2_, c, ALU.mult)
                    step(G.tensor_tensor(kr_tmp[0:r, 96:128], x1, sn, ALU.mult))
                    G.tensor_tensor(kr_n[0:r, t, 0:32], kr_tmp[0:r, 0:32], kr_tmp[0:r, 32:64], ALU.subtract)
                    step(G.tensor_tensor(kr_n[0:r, t, 32:64], kr_tmp[0:r, 64:96], kr_tmp[0:r, 96:128], ALU.add))
                    pool.sem_inc(p_kr, 1)
                    if t == NTP:
                        pool.sem_inc(lat_ready, 1)
                elif what == "Q":
                    pool.wait_ge(qrn_ready, t + 1)
                    v = [x.rearrange("p (h f) -> p h f", h=H) for x in (qr_n, qr_r)]
                    x1, x2_ = v[0][0:r, :, 0:32], v[0][0:r, :, 32:64]
                    tmp = qr_tmp.rearrange("p (a h f) -> p a h f", a=4, h=H)
                    cb = cos[0:r, t, :].unsqueeze(1).broadcast_to([r, H, 32])
                    sb = sin[0:r, t, :].unsqueeze(1).broadcast_to([r, H, 32])
                    G.tensor_tensor(tmp[0:r, 0], x1, cb, ALU.mult)
                    G.tensor_tensor(tmp[0:r, 1], x2_, sb, ALU.mult)
                    G.tensor_tensor(tmp[0:r, 2], x2_, cb, ALU.mult)
                    step(G.tensor_tensor(tmp[0:r, 3], x1, sb, ALU.mult))
                    G.tensor_tensor(v[1][0:r, :, 0:32], tmp[0:r, 0], tmp[0:r, 1], ALU.subtract)
                    G.tensor_tensor(v[1][0:r, :, 32:64], tmp[0:r, 2], tmp[0:r, 3], ALU.add).then_inc(qrope_done, 1)
            stage_end(pool, 2)

            ckv_g = cache_ckv[0].rearrange("n (a r) c -> (n a) (r c)", r=PG)
            kr_g = cache_krope[0].rearrange("n (a r) c -> (n a) (r c)", r=PG)

            def gather(q, n, col):
                step_g = G.tensor_copy(idx_now[q], page_int[:, col].bitcast(U32))
                return step_g

            def fetch(q):
                off = bass.IndirectOffsetOnAxis(ap=idx_now[q], axis=0)
                pool.indirect_dma_start(ck[q].rearrange("p r c -> p (r c)"), None, ckv_g, off).then_inc(c_in[q], 16)
                pool.indirect_dma_start(kr[q].rearrange("p r c -> p (r c)"), None, kr_g, off).then_inc(c_in[q], 16)

            for q in range(4):
                gather(q, q, slice(q, q + 1)).then_inc(idx_step, 1)
                pool.wait_ge(idx_step, q + 1)
                fetch(q)
            with pool.Fori(0, NB - 1) as i:
                for q in range(4):
                    pool.wait_ge(c_pv, 4 * i + q + 1)
                    gather(q, None, bass.ds(4 * i + q + 4, 1)).then_inc(idx_step, 1)
                    pool.wait_ge(idx_step, 4 * i + q + 5)
                    pool.sem_inc(marks, 1)
                    fetch(q)
            stage_end(pool, 3)

            def merge(n, s, r, attn_rows, x2_rows, i_in):
                pool.wait_ge(z_in[s], 32 * i_in)
                G.tensor_tensor(zt[s][0:r, 2 * D:3 * D], zt[s][0:r, 2 * D:3 * D], attn_rows, ALU.mult).then_inc(at_ok, 1)
                pool.wait_ge(x2_ok, n + 1)
                G.tensor_copy(x2_rows, xr[s][0:r, :]).then_inc(x2_cp, 1)

            with pool.Fori(0, 4) as i:
                for s in range(2):
                    t = 2 * i + s
                    merge(t, s, P, attn.rearrange("p t n -> p (t n)")[:, bass.ds(2 * D * i + D * s, D)],
                          x2.rearrange("p t n -> p (t n)")[:, bass.ds(2 * D * i + D * s, D)], i + 1)
            merge(8, 0, RS, attn[0:RS, NTP, :], x2[0:RS, NTP, :], 5)
            stage_end(pool, 4)

            G.memset(fill.bitcast(I32), 1 << 29).then_inc(fill_ok, 1)
            pool.wait_ge(fill_in, 16)
            pool.wait_ge(r_pos, 1)
            ids_v = ids_sb.rearrange("p (n c) -> p n c", c=2)
            for n in range(2 * NT):
                pool.indirect_dma_start(slot_rows, bass.IndirectOffsetOnAxis(ap=pos_i[:, n:n + 1], axis=0),
                                        ids_v[:, n, :], None, bounds_check=NBLK * P - 1, oob_is_err=False).then_inc(scat_in, 16)
            pool.wait_ge(slots_ok, 1)
            for s in range(2):
                last = G.memset(xg[s], 0.0)
            last.then_inc(xg_zero, 1)
            pool.wait_ge(xg_zero, 1)
            for u in range(2):
                pool.wait_ge(xt_st[u], 16 * (6 - u))

            last_tok, last_slot = pool.to_reg(TOK - 1), pool.to_reg(2 * TOK - 1)

            def rows_in(s, n, k):
                G.tensor_copy(idx_row[s], slot_idx[:, n, 0:1] if isinstance(n, int) else slot_idx[:, bass.ds(n, 1), 0])
                G.tensor_copy(idx_tok[s], slot_idx[:, n, 1:2] if isinstance(n, int) else slot_idx[:, bass.ds(n, 1), 1]).then_inc(x_idx, 1)
                pool.wait_ge(x_idx, k + 1)
                pool.sem_inc(marks, 1)
                pool.indirect_dma_start(xg[s], None, xt_rows, bass.IndirectOffsetOnAxis(ap=idx_tok[s], axis=0),
                                        bounds_check=last_tok, oob_is_err=False).then_inc(e_x[s], 16)

            def rows_out(s, n):
                pool.wait_ge(e_ye[0], n + 2)
                pool.wait_ge(e_ye[1], n + 2)
                pool.sem_inc(marks, 1)
                pool.indirect_dma_start(y_rows, bass.IndirectOffsetOnAxis(ap=idx_row[s], axis=0), yo[s], None,
                                        bounds_check=last_slot, oob_is_err=False).then_inc(e_sc[s], 16)

            rows_in(0, 0, 0)
            rows_in(1, 1, 1)
            with pool.Fori(0, 31) as i:
                for s in range(2):
                    rows_out(s, 2 * i + s)
                    pool.wait_ge(e_sc[s], 16 * i + 16)
                    pool.sem_inc(yo_free[s], 1)
                    rows_in(s, 2 * i + s + 2, 2 * i + s + 2)
            rows_out(0, 62)
            rows_out(1, 63)
            for s in range(2):
                pool.wait_ge(e_sc[s], 16 * 32)
                pool.sem_inc(yo_free[s], 1)
            total = pool.value_load(ovf_id[0:1, NOVF:NOVF + 1], min_val=0, max_val=NOVF)
            with pool.Fori(0, NOVF) as j:
                with pool.If(total > j):
                    rows_in(0, NE + j, NE + j)
                    rows_out(0, NE + j)
                    pool.wait_ge(e_sc[0], 16 * (33 + j))
                    pool.sem_inc(yo_free[0], 1)
            pool.sem_inc(moe_end, 1)


        @block.vector
        def _(dve):
            V = nc.vector
            copy, tt, ts, stt, red = V.tensor_copy, V.tensor_tensor, V.tensor_scalar, V.scalar_tensor_tensor, V.tensor_reduce
            step = Count(dve, dve_c)
            dve.sem_inc(xt_ev[1], 2)
            dve.sem_inc(c_ed, 2)
            dve.sem_inc(c_acc, 1)
            dve.sem_inc(sgu_ok, 1)
            dve.sem_inc(lg_ok, 1)
            dve.sem_inc(e_ye[1], 1)
            V.memset(logits, 0.0)
            step(V.memset(small, 0.0))
            dve.sem_inc(small_zero, 1)
            dve.wait_ge(small_in, 16 * (9 + NB))

            def norm_x(n, s, r, dst):
                dve.wait_ge(x_rstd, n + 1)
                V.reciprocal(small[0:r, 4 + s:5 + s], small[0:r, 2 + s:3 + s]).then_inc(x_inv, 1)
                dve.wait_ge(x_inv, n + 1)
                stt(xn[s][0:r, :], x_in[s][0:r, :], small[0:r, 4 + s:5 + s], g1[0:r, :], ALU.mult, ALU.mult).then_inc(xn_ready, 1)
                dve.wait_ge(xt_mm, n + 1)
                ts(dst, bank(2 * s + 1).rearrange("p (k n) -> p k n", k=4)[:, :, 0:r], 1.0, None, ALU.mult).then_inc(xt_ev[1], 1)

            with dve.Fori(0, 4) as i:
                for s in range(2):
                    norm_x(2 * i + s, s, P, xn_t[:, 4:8, bass.ds(2 * P * i + P * s, P)])
            norm_x(8, 0, RS, xn_t[:, 4:8, SEQ:TOK])
            for t in range(NT):
                r = rows_of(t)
                dve.wait_ge(z_ev, NT + t + 1)
                for c, (a0, w) in enumerate(((0, QL), (QL, KVL))):
                    step(stt(junk2[0:r, c * QL:c * QL + w], z0[0:r, t, a0:a0 + w], 1.0 / w, z0[0:r, t, a0:a0 + w], ALU.mult,
                             ALU.mult, accum_out=stat[0:r, t, c:c + 1]))
            dve.sem_inc(p_sq, 1)
            dve.wait_ge(p_rs, 1)
            step(V.reciprocal(rstd, stat))
            stage_end(dve, 1)

            got = 0
            for what, n in sched:
                if what == "prep":
                    t, r = n, rows_of(n)
                    if t >= 1:
                        dve.wait_ge(b_mm[0], cq_read)
                    stt(cq[0:r, :], z0[0:r, t, 0:QL], rstd[0:r, t, 0:1], gq[0:r, :], ALU.mult, ALU.mult)
                    last = stt(ckv_n[0:r, t, :], z0[0:r, t, QL:QL + KVL], rstd[0:r, t, 1:2], gkv[0:r, :], ALU.mult, ALU.mult)
                    last.then_inc(p_cn, 1)
                    if t == NTP:
                        dve.wait_ge(p_cn, NT)
                        dve.sem_inc(lat_ready, 1)
                elif what == "Q":
                    t, r, s = n, rows_of(n), n % 2
                    b1 = bank(1).rearrange("p (i n) -> p i n", i=4)

                    def from1(dst, src):
                        nonlocal got
                        got += 1
                        dve.wait_ge(b_mm[1], got)
                        copy(dst, src).then_inc(b_ev[1], 1)

                    from1(ckv_t[:, :, t * P:t * P + r], b1[:, 0:2, 0:r])
                    from1(qn_t[:, 4:8, 0:r], b1[:, :, 0:r])
                    for h in (0, 4):
                        from1(ql_t[s][:, h:h + 2, :, 0:r].rearrange("p h c n -> p (h c) n"), b1[:, :, 0:r])
                    from1(qr_t[s][0:DR, 0:4, 0:r], b1[0:DR, :, 0:r])
                    cq_read = q_units(sched, t)
                elif what == "S":
                    t, h = units[n]
                    w = P * (t + 1)
                    dve.wait_ge(s_mm, n + 1)
                    step(red(rinv[:, n:n + 1], bank(2 + 2 * (n % 2), 2)[:, 0:w], AX.X, ALU.max))
                    ts(negmax[:, n:n + 1], rinv[:, n:n + 1], -SCALE, None, ALU.mult).then_inc(s_nm, 1)
                    dve.wait_ge(s_exp, n + 1)
                    V.reciprocal(rinv[:, n:n + 1], psumq[:, n:n + 1]).then_inc(s_rinv, 1)
                elif what == "T":
                    t, h = units[n]
                    if t >= 4:
                        dve.wait_ge(t_mm[1], n - 4 * H + 1)
                        copy(prob_t[n % 2][:, 4:t + 1, :].rearrange("p j n -> p (j n)"), bank(7)[:, 0:P * (t - 3)]).then_inc(t_ev[1], 1)
                elif n % 2 == 1:
                    t, h = units[n]
                    got += 1
                    dve.wait_ge(b_mm[1], got)
                    if what == "PV":
                        copy(pv_t[1].rearrange("p c n -> p (c n)"), bank(1)[:, 0:2 * P]).then_inc(b_ev[1], 1)
                    else:
                        dve.wait_ge(s_rinv, n + 1)
                        ts(attn[:, t, DV * h:DV * h + DV], bank(1)[:, 0:DV], rinv[:, n:n + 1], None, ALU.mult).then_inc(b_ev[1], 1)
            dve.wait_ge(b_ev[0], bank0_units)
            for c in range(2):
                copy(qs[:, c, :].rearrange("p (b h t) -> p b h t", b=NB, h=H),
                     ql_t[0][:, :, c, 0:RS].rearrange("p h (b t) -> p b h t", b=NB))
            copy(qsr[0:DR, :].rearrange("p (b h t) -> p b h t", b=NB, h=H),
                 qr_t[0][0:DR, :, 0:RS].rearrange("p h (b t) -> p b h t", b=NB)).then_inc(n_dve, 1)
            stage_end(dve, 2)

            dve.wait_ge(n_pe, 1)
            dve.wait_ge(lat_stored, 64)
            step(tt(s_new[0:RS, :], bank(6)[0:RS, 0:256], const("mask_new")[0:RS, :], ALU.add))
            dve.sem_inc(n_dve, 1)
            dve.wait_ge(n_pe, 2)
            step(red(m_col2, bank(7)[:, 0:64].rearrange("p (g n) -> p g n", g=2), AX.X, ALU.max))
            for g in range(2):
                last = ts(m_diag2[:, P * g:P * g + P], ident, m_col2[:, g:g + 1], None, ALU.mult)
            last.then_inc(n_dve, 1)
            dve.wait_ge(n_pe, 3)
            step(copy(m_all, bank(6)[:, 0:256]))
            tt(s_new[0:RS, :], s_new[0:RS, :], m_all[0:RS, :], ALU.subtract).then_inc(c_sub, 1)
            step(V.memset(l_all, 0.0))
            dve.wait_ge(n_act, 1)
            copy(l_all[0:RS, :], p_new[0:RS, :])
            dve.wait_ge(n_pe, 4)
            step(copy(acc.rearrange("p c n -> p (c n)"), bank(7)))
            dve.sem_inc(n_dve, 1)

            PER = 6
            chain0 = step.n

            def turned(n, parts):
                for g in range(PG // 2):
                    dve.wait_ge(c_tr, 8 * n + g + 1)
                    copy(kr_tt[0:DR, 2 * (g % 2):2 * (g % 2) + 2, :].rearrange("p r n -> p (r n)"), bank(2 * (g % 2) + 1)[0:DR, 0:256]).then_inc(c_ed, 1)
                    if g in parts:
                        parts[g]()

            def softmax(n, q, col):
                ch = Count(dve, dve_c, chain0 + PER * n)
                sc = bank(4 + q % 2)

                def part_max():
                    dve.wait_ge(c_s, n + 1)
                    red(m_part, sc.rearrange("p (r n) -> p n r", r=PG), AX.X, ALU.max).then_inc(c_mpart, 1)

                def diagonal():
                    dve.wait_ge(c_mt, n + 1)
                    ch(red(m_col[0:32, 0:1], bank(6)[0:32, 0:P], AX.X, ALU.max))
                    ts(m_diag[0:32, :], ident[0:32, 0:32], m_col[0:32, 0:1], None, ALU.mult).then_inc(c_md, 1)

                def shift():
                    dve.wait_ge(c_mb, n + 1)
                    ch(tt(m_new, m_all[:, col], bank(6)[:, P:P + 32], ALU.max))
                    tt(m_dif, m_all[:, col], m_new, ALU.subtract)
                    ch(tt(p_sub.rearrange("p (r n) -> p r n", r=PG), sc.rearrange("p (r n) -> p r n", r=PG),
                          m_new.unsqueeze(1).broadcast_to([P, PG, 32]), ALU.subtract))
                    ts(m_all[:, col], m_new, 1.0, None, ALU.mult).then_inc(c_sub, 1)

                def sums():
                    dve.wait_ge(c_p, n + 1)
                    red(l_add, p_exp[q % 2].rearrange("p (r n) -> p n r", r=PG), AX.X, ALU.add)
                    ch(tt(l_all[:, col], l_all[:, col], alpha, ALU.mult))
                    tt(l_all[:, col], l_all[:, col], l_add, ALU.add)
                    ch(tt(acc[:, :, col], acc[:, :, col], alpha.unsqueeze(1).broadcast_to([P, 2, 32]), ALU.mult))
                    dve.wait_ge(c_pv, n + 1)
                    ch(tt(acc[:, :, col], acc[:, :, col], bank(7)[:, 0:64].rearrange("p (c n) -> p c n", c=2), ALU.add))
                    dve.sem_inc(c_acc, 1)
                    assert ch.n == PER, ch.n

                return part_max, diagonal, shift, sums

            turned(0, {})

            def batch(i, last_batch):
                for q in range(4):
                    n = 4 * i + q
                    part_max, diagonal, shift, sums = softmax(n, q, bass.ds(32 * i, 32))
                    part_max()
                    if q < 3 or not last_batch:
                        turned(n + 1, {1: diagonal, 3: shift})
                    else:
                        diagonal()
                        shift()
                    sums()

            with dve.Fori(0, NB - 1) as i:
                batch(i, False)
            batch(NB - 1, True)
            step.n += PER * NCH
            dve.wait_ge(n_pe, 5)
            step(V.reciprocal(l_inv, bank(6)[:, 0:256]))
            for c in range(2):
                last = tt(o_lat[:, c, :].rearrange("p (h b t) -> p b h t", h=H, b=NB),
                          acc[:, c, :].rearrange("p (b h t) -> p b h t", h=H, b=NB),
                          l_inv.rearrange("p (b h t) -> p b h t", h=H, b=NB), ALU.mult)
            last.then_inc(n_dve, 1)
            stage_end(dve, 3)

            chain5 = step.n
            PER5 = 2

            def merge(n, s, r, bs, lg_rows, k):
                ch = Count(dve, dve_c, chain5 + PER5 * n)
                u, v, ga, gb = (zt[s][0:r, D * x:D * x + D] for x in range(4))
                dve.wait_ge(v_rs, n + 1)
                V.reciprocal(stat5[s][0:r, 1:2], stat5[s][0:r, 0:1]).then_inc(v_inv, 1)
                dve.wait_ge(v_inv, n + 1)
                stt(v, v, stat5[s][0:r, 1:2], gv[0:r, :], ALU.mult, ALU.mult).then_inc(v_n, 1)
                dve.wait_ge(mix_mm, n + 1)
                for g in range(KD):
                    last = stt(u[:, P * g:P * g + P], bank(0, 2)[0:r, P * g:P * g + P], bs[0:r, g:g + 1],
                               u[:, P * g:P * g + P], ALU.add, ALU.mult)
                last.then_inc(sgu_ok, 1)
                dve.wait_ge(sgu_ok, n + 2)
                ch(tt(u, u, gb, ALU.mult))
                dve.wait_ge(at_ok, n + 1)
                tt(u, u, ga, ALU.add).then_inc(mrg_ok, 1)
                dve.wait_ge(y_mm, n + 1)
                tt(xr[s][0:r, :], xr[s][0:r, :], bank(4, 2)[0:r, :], ALU.add).then_inc(x2_ok, 1)
                dve.wait_ge(o_rs, n + 1)
                V.reciprocal(stat5[s][0:r, 3:4], stat5[s][0:r, 2:3]).then_inc(o_inv, 1)
                dve.wait_ge(o_inv, n + 1)
                dve.wait_ge(xt_st[s], 16 * k + 16)
                ch(stt(xo[s][0:r, :], xr[s][0:r, :], stat5[s][0:r, 3:4], g2[0:r, :], ALU.mult, ALU.mult))
                dve.sem_inc(o_n, 1)
                dve.wait_ge(lg_mm, n + 1)
                tt(lg_rows, bank(6)[0:r, 0:72], rbias[0:r, :], ALU.add).then_inc(lg_ok, 1)
                assert ch.n == PER5

            dve.wait_ge(late_in, 48)
            lg_flat = logits.rearrange("p t n -> p (t n)")
            with dve.Fori(0, 4) as i:
                for s in range(2):
                    merge(2 * i + s, s, P, bs_t, lg_flat[:, bass.ds(144 * i + 72 * s, 72)], i)
            merge(8, 0, RS, bs_ts, logits[0:RS, NTP, :], 4)
            step.n += PER5 * NT
            for u in range(2):
                dve.wait_ge(xt_st[u], 16 * (6 - u))
            dve.wait_ge(v_st, 16)
            stage_end(dve, 4)

            def wide(x, n):
                return x.unsqueeze(len(x.shape)).broadcast_to(list(x.shape) + [n])

            for t in range(NT):
                last = V.max(g_top[:, t, :], logits[:, t, 0:NG])
            step(last)
            for t in range(NT):
                last = V.max_index(g_ind[:, t, :], g_top[:, t, :], logits[:, t, 0:NG])
            step(last)
            step(copy(g_f, g_ind[:, :, 0]))
            iota = const("iota")
            step(tt(pen, iota[:, 0:NG].unsqueeze(1).broadcast_to([P, NT, NG]), wide(g_f, NG), ALU.is_equal))
            step(ts(pen, pen, -NEG, NEG, ALU.mult, ALU.add))
            step(tt(e_log.rearrange("p t (g e) -> p t g e", g=NG), logits[:, :, NG:].rearrange("p t (g e) -> p t g e", g=NG),
                    wide(pen, 8), ALU.add))
            for t in range(NT):
                last = V.max(e_top[:, t, :], e_log[:, t, :])
            step(last)
            for t in range(NT):
                last = V.max_index(e_ind[:, t, :], e_top[:, t, :], e_log[:, t, :])
            tt(g_sub, logits[:, :, 0:NG], g_top[:, :, 0:1].broadcast_to([P, NT, NG]), ALU.subtract)
            step(tt(d_sub, e_top[:, :, 1], e_top[:, :, 0], ALU.subtract))
            dve.sem_inc(r_sub, 1)
            step(copy(e_f, e_ind[:, :, 0:2]))
            step(tt(e_f, e_f, wide(const("pad"), 2), ALU.add))
            step(tt(hot.rearrange("p t c n -> p (t c) n"), iota.unsqueeze(1).broadcast_to([P, 2 * NT, NE]),
                    wide(e_f.rearrange("p t c -> p (t c)"), NE), ALU.is_equal))
            step(tt(mask, hot[:, :, 0, :], hot[:, :, 1, :], ALU.add))
            step(V.memset(cum[:, 0, :], 0.0))
            for t in range(1, NT):
                step(tt(cum[:, t, :], cum[:, t - 1, :], mask[:, t - 1, :], ALU.add))
            step(tt(rank[:, 0, :], cum[:, NT - 1, :], mask[:, NT - 1, :], ALU.add))
            dve.sem_inc(r_dve, 1)
            dve.wait_ge(r_exp, 1)
            step(red(g_den, g_exp, AX.X, ALU.add))
            step(ts(d_sub, d_exp, 1.0, None, ALU.add))
            step(tt(g_den, g_den, d_sub, ALU.mult))
            step(V.reciprocal(gates[:, :, 0], g_den))
            step(tt(gates[:, :, 1], gates[:, :, 0], d_exp, ALU.mult))
            dve.wait_ge(r_pe, 1)
            step(copy(cnt[0], bank(1)[:, NE:2 * NE]))
            prod8 = prod.rearrange("p t c n -> p (t c n)")
            big = prod8[:, 0:NE * CAP_STEPS].rearrange("p (e s) -> p e s", s=CAP_STEPS)
            step(tt(big, wide(cnt[0], CAP_STEPS), const("steps").unsqueeze(1).broadcast_to([P, NE, CAP_STEPS]), ALU.is_gt))
            step(red(cnt[1], big, AX.X, ALU.add))
            step(V.tensor_tensor_scan(cnt[2], ones[:, 0:NE], cnt[1], 0.0, ALU.mult, ALU.add))
            step(tt(cnt[3], cnt[2], cnt[1], ALU.subtract))
            big = prod8[:, 0:NE * NOVF].rearrange("p (j e) -> p j e", j=NOVF)
            step(tt(big, cnt[2].unsqueeze(1).broadcast_to([P, NOVF, NE]), wide(const("blocks"), NE), ALU.is_le))
            step(red(cnt[0][:, 0:NOVF], big, AX.X, ALU.add))
            ts(ovf_id[:, 0:NOVF], cnt[0][:, 0:NOVF], NE - 1.0, None, ALU.min)
            copy(ovf_id[:, NOVF:NOVF + 1], cnt[2][:, NE - 1:NE])
            step(copy(rank[:, 0:8, :].rearrange("p t n -> p (t n)"), bank(0)))
            step(copy(rank[:, 8, :], bank(1)[:, 0:NE]))
            rk, xs_, q_, rem, b_, tmp_ = (x.rearrange("p t c -> p (t c)") for x in n_rt)
            ef = e_f.rearrange("p t c -> p (t c)")
            for c in range(2):
                last = tt(prod[:, :, c, :], hot[:, :, c, :], rank, ALU.mult)
            step(last)
            step(red(rk, prod.rearrange("p t c n -> p (t c) n"), AX.X, ALU.add))
            step(tt(prod.rearrange("p t c n -> p (t c) n"), hot.rearrange("p t c n -> p (t c) n"),
                    cnt[3].unsqueeze(1).broadcast_to([P, 2 * NT, NE]), ALU.mult))
            step(red(xs_, prod.rearrange("p t c n -> p (t c) n"), AX.X, ALU.add))
            big = prod8[:, 0:2 * NT * CAP_STEPS].rearrange("p (e s) -> p e s", s=CAP_STEPS)
            step(tt(big, wide(rk, CAP_STEPS), const("steps").unsqueeze(1).broadcast_to([P, 2 * NT, CAP_STEPS]), ALU.is_ge))
            step(red(q_, big, AX.X, ALU.add))
            step(stt(rem, q_, -float(P), rk, ALU.mult, ALU.add))
            step(stt(b_, q_, NE - 1.0, xs_, ALU.add, ALU.add))
            step(tt(b_, b_, ef, ALU.subtract))
            step(ts(tmp_, q_, 1.0, None, ALU.min))
            step(tt(b_, b_, tmp_, ALU.mult))
            step(tt(b_, b_, ef, ALU.add))
            step(stt(pos_i, b_, float(P), rem, ALU.mult, ALU.add))
            dve.sem_inc(r_pos, 1)
            dve.wait_ge(slots_in, 16)
            step(copy(slot_f[0:NBLK, :], fill[0:NBLK, :].bitcast(I32)))
            dve.sem_inc(r_dve, 1)
            dve.wait_ge(r_pe, 2)
            for c in range(2):
                last = copy(slot_idx[:, :, c], bank(2)[:, P * c:P * c + NBLK])
            step(last)
            dve.sem_inc(slots_ok, 1)

            def expert(n):
                dve.wait_ge(e_xt, n + 1)
                copy(xg_t[:, 4:8, :].rearrange("p k n -> p (k n)"), bank(1)).then_inc(e_xe, 1)
                dve.wait_ge(e_u, n + 1)
                dve.wait_ge(e_si, n + 1)
                tt(h_n, h_s, bank(3)[:, 0:DE], ALU.mult).then_inc(e_h, 1)
                dve.wait_ge(e_ht, n + 1)
                copy(h_t.rearrange("p f n -> p (f n)"), bank(4)[:, 0:DE]).then_inc(e_he, 1)

            def expert_out(n, s, i_s):
                dve.wait_ge(e_y[1], n + 1)
                dve.wait_ge(yo_free[s], i_s)
                copy(yo[s][:, 512:D], bank(6)).then_inc(e_ye[1], 1)

            with dve.Fori(0, 16) as i:
                for s in range(4):
                    expert(4 * i + s)
                    expert_out(4 * i + s, s % 2, 2 * i + s // 2 + 1)
            total = dve.value_load(ovf_id[0:1, NOVF:NOVF + 1], min_val=0, max_val=NOVF)
            with dve.Fori(0, NOVF) as j:
                with dve.If(total > j):
                    expert(NE + j)
                    expert_out(NE + j, 0, 33 + j)

            for t in range(NT):
                s, r = t % 2, rows_of(t)
                dve.wait_ge(f_in[s], 16 * (t // 2 + 1))
                dve.wait_ge(f_st[s], 16 * (t // 2) + 16)
                step(stt(fin[s][0:r, :], y2[s][0:r, 0:D], gates[0:r, t, 0:1], x2[0:r, t, :], ALU.mult, ALU.add))
                stt(fin[s][0:r, :], y2[s][0:r, D:2 * D], gates[0:r, t, 1:2], fin[s][0:r, :], ALU.mult, ALU.add).then_inc(f_sum, 1)
                dve.wait_ge(f_rs, t + 1)
                V.reciprocal(stat8[s][0:r, 1:2], stat8[s][0:r, 0:1]).then_inc(f_inv, 1)
                dve.wait_ge(f_inv, t + 1)
                stt(fin[s][0:r, :], fin[s][0:r, :], stat8[s][0:r, 1:2], gf[0:r, :], ALU.mult, ALU.mult).then_inc(f_ok, 1)


_INS = ["x_prompt", "x_sample", "cache_ckv", "cache_krope", "page_table", "norm1_g", "w_in", "q_norm_g", "kv_norm_g",
        "w_uq", "w_qr", "w_uk", "w_uv", "sgu_norm_g", "w_s", "b_s", "w_o", "norm2_g", "w_rg", "b_rg", "w_re", "b_re",
        "w_gate", "w_up", "w_down", "norm_f_g"]
_OUTS = [(1, SEQ, D), (NB, TS, D), (1, 1, NTP, P, KVL), (1, 1, NTP, P, DR), (1, NB, TS, KVL), (1, NB, TS, DR),
         (1, NB, TS, D)]
_SCRATCH = [("z_act", [TOK, 4 * D], F32), ("xt_rows", [TOK, D], F32), ("slot_rows", [NBLK * P, 2], I32),
            ("y_rows", [2 * TOK, D], F32)]


def kernel(**inputs):
    import numpy as _np
    import concourse.bacc as _bacc
    from concourse import mybir as _mybir
    from concourse.bass_utils import run_bass_kernel_spmd as _run

    nc = _bacc.Bacc("TRN2", target_bir_lowering=False, num_devices=1)
    arrays, args = {}, []
    tables, ids = const_tables()
    for name, a in [(n, _np.ascontiguousarray(inputs[n])) for n in _INS] + [("tables", tables), ("ids", ids)]:
        arrays[f"in_{name}_dram"] = a
        args.append(nc.dram_tensor(f"in_{name}_dram", a.shape, _mybir.dt.from_np(a.dtype), kind="ExternalInput").ap())
    for i, shape in enumerate(_OUTS):
        args.append(nc.dram_tensor(f"out_{i}_dram", shape, _mybir.dt.float32, kind="ExternalOutput").ap())
    for name, shape, dt in _SCRATCH:
        args.append(nc.dram_tensor(name, shape, dt, kind="Internal").ap())
    build(nc, *args)
    r = _run(nc, [arrays], core_ids=[0])
    return tuple(r.results[0][f"out_{i}_dram"] for i in range(len(_OUTS)))
```

```python
from contextlib import ExitStack

import numpy as np

import concourse.bass as bass
from concourse import mybir

F32 = mybir.dt.float32
I32 = mybir.dt.int32
U32 = mybir.dt.uint32
ALU = mybir.AluOpType
ACT = mybir.ActivationFunctionType
AX = mybir.AxisListType

P = 128
D = 1024
KD = D // P
SEQ = 1024
NTP = SEQ // P
NB, TS = 8, 4
RS = NB * TS
NT = NTP + 1
TOK = SEQ + RS
H = 8
DN = 128
DR = 64
DV = 128
QL, KVL = 384, 256
ZL = QL + KVL + DR
NG = 8
NE = 64
DE = 256
EPS = 1e-6
SCALE = float(np.float32((DN + DR) ** -0.5))
NEG = -1e30
PAST = 8192
PAGES = PAST // P
PG = 16
NCH = NB * PAGES // PG
NOVF = 2 * TOK // P
NBLK = NE + NOVF
PAD = 1e6
CAP_STEPS = (TOK + P - 1) // P - 1
QB = 2 * H * P


def rows_of(t):
    return P if t < NTP else RS


def const_layout():
    at, off = {}, 0
    for name, n in (("ident", P), ("negmask", P), ("before", P), ("ones", P), ("keep", P), ("keep_s", RS),
                    ("cos", NT * 32), ("sin", NT * 32), ("iota", NE), ("steps", CAP_STEPS),
                    ("pad", NT), ("blocks", NOVF), ("mask_new", NB * RS), ("same_q", P), ("p_mod", 1), ("eps", 1)):
        at[name] = (off, n)
        off += n
    return at, off


def const_tables():
    at, n = const_layout()
    k = np.zeros((P, n), np.float32)

    def put(name, a):
        o, w = at[name]
        k[:a.shape[0], o:o + w] = a.reshape(a.shape[0], w)

    i = np.arange(P)
    put("ident", np.eye(P, dtype=np.float32))
    put("negmask", np.where(i[None, :] <= i[:, None], 0, NEG).astype(np.float32))
    put("before", (i[:, None] < i[None, :]).astype(np.float32))
    put("ones", np.ones((P, P), np.float32))
    put("keep", (i[None, :] <= i[:, None]).astype(np.float32))
    r = np.arange(RS)
    same = r[None, :] // TS == r[:, None] // TS
    put("keep_s", (same & (r[None, :] <= r[:, None])).astype(np.float32))
    half = DR // 2
    freq = (10000.0 ** (-np.arange(half) / half)).astype(np.float32)
    pos = np.zeros((P, NT), np.float32)
    for t in range(NTP):
        pos[:, t] = t * P + i
    pos[:RS, NTP] = PAST + r % TS
    ang = (pos[:, :, None] * freq[None, None, :]).astype(np.float64)
    put("cos", np.cos(ang).astype(np.float32))
    put("sin", np.sin(ang).astype(np.float32))
    put("iota", np.tile(np.arange(NE, dtype=np.float32), (P, 1)))
    put("steps", np.tile(P * np.arange(1, CAP_STEPS + 1, dtype=np.float32), (P, 1)))
    pad = np.zeros((P, NT), np.float32)
    pad[RS:, NTP] = PAD + i[RS:]
    put("pad", pad)
    put("blocks", np.tile(np.arange(NOVF, dtype=np.float32), (P, 1)))
    col = np.arange(NB * RS)
    cb, ck_ = col // RS, col % RS
    ok = (ck_ // TS == cb)[None, :] & (ck_[None, :] % TS <= r[:, None] % TS)
    put("mask_new", np.where(ok, 0, NEG).astype(np.float32))
    put("same_q", (i[:, None] % RS == i[None, :] % RS).astype(np.float32))
    put("p_mod", (i % 8).astype(np.float32)[:, None])
    put("eps", np.full((P, 1), EPS, np.float32))
    ids = np.zeros((P, NT, 2, 2), np.int32)
    for t in range(NT):
        for c in range(2):
            ids[:, t, c, 0] = (t * P + i) * 2 + c
            ids[:, t, c, 1] = t * P + i
    return k, ids.reshape(P, NT * 4)


def q_units(sched, tile):
    n = 0
    for what, k in sched:
        if what == "Q" and k == tile:
            return n + 1
        n += 6 if what == "Q" else int(what in ("PV", "UV") and k % 2 == 0)


class Count:

    def __init__(self, eng, sem, base=0):
        self.eng, self.sem, self.base, self.n = eng, sem, base, 0

    def __call__(self, ins):
        self.n += 1
        ins.then_inc(self.sem, 1)
        self.eng.wait_ge(self.sem, self.base + self.n)


def attention_schedule():
    units = [(t, h) for t in range(NTP) for h in range(H)]
    todo = [("prep", 0), ("Q", 0), ("S", 0)]
    for n, (t, h) in enumerate(units):
        if n + 1 < len(units):
            if h == 1:
                todo.append(("prep", t + 1))
            if h == 3:
                todo.append(("Q", t + 1))
            todo.append(("S", n + 1))
        todo.append(("T", n))
        if t == NTP - 1 and h == 1:
            todo.append(("prep", NTP))
        if t == NTP - 1 and h == 3:
            todo.append(("Q", NTP))
        if n >= 1:
            todo.append(("PV", n - 1))
        if n >= 2:
            todo.append(("UV", n - 2))
    last = len(units) - 1
    todo += [("PV", last), ("UV", last - 1), ("UV", last)]
    out = []
    for x in todo:
        if x not in out:
            out.append(x)
    return units, out


def build(nc, x_prompt, x_sample, cache_ckv, cache_krope, page_table, norm1_g, w_in, q_norm_g, kv_norm_g,
          w_uq, w_qr, w_uk, w_uv, sgu_norm_g, w_s, b_s, w_o, norm2_g, w_rg, b_rg, w_re, b_re,
          w_gate, w_up, w_down, norm_f_g, tables, ids,
          y_prompt, y_sample, ckv_prompt, kr_prompt, ckv_sample, kr_sample, v_sample,
          z_act, xt_rows, slot_rows, y_rows):
    with ExitStack() as ctx:
        def sem(name):
            return ctx.enter_context(nc.semaphore(name))

        SIZE = 53200
        arena = ctx.enter_context(nc.sbuf_tensor("arena", [P, SIZE], F32))
        psum = ctx.enter_context(nc.psum_tensor("psum", [P, 8 * 512], F32))
        top = [0]
        end = [SIZE]

        def take(n, where=None, dt=F32):
            where = where or top
            v = arena[:, where[0]:where[0] + n]
            where[0] += n
            assert where[0] <= end[0], (where, n)
            return v

        def bank(b, n=1):
            return psum[:, 512 * b:512 * (b + n)]

        at, n_const = const_layout()
        K = take(n_const)

        def const(name):
            o, w = at[name]
            return K[:, o:o + w]

        ident, ones, eps = const("ident"), const("ones"), const("eps")
        cos, sin = (const(x).rearrange("p (t f) -> p t f", t=NT) for x in ("cos", "sin"))
        ids_sb = take(NT * 4).bitcast(I32)
        gains_base = top[0]
        g1, g2, gf, gv = take(D), take(D), take(D), take(D)
        gq, gkv = take(QL), take(KVL)
        rbias = take(NG + NE)
        w_router = take(KD * (NG + NE)).rearrange("p (k n) -> p k n", k=KD)
        ws_t = take(KD * P).rearrange("p (g i) -> p g i", g=KD)
        ws_ts = take(KD * RS).rearrange("p (g i) -> p g i", g=KD)
        bs_t, bs_ts = take(KD), take(KD)
        logits = take(NT * 72).rearrange("p (t n) -> p t n", t=NT)
        small = take(64)
        stat = small[:, 8:8 + 2 * NT].rearrange("p (t n) -> p t n", t=NT)
        rstd = small[:, 30:30 + 2 * NT].rearrange("p (t n) -> p t n", t=NT)
        page_idx = take(NCH)
        page_int = take(NCH).bitcast(I32)
        page_raw = take(NCH).bitcast(I32)
        x2_at = [SIZE - NT * D]
        x2 = arena[:, x2_at[0]:SIZE].rearrange("p (t n) -> p t n", t=NT)

        attn_base = top[0]
        attn = take(NT * D).rearrange("p (t n) -> p t n", t=NT)
        kv_base = top[0]
        ckv_n = take(NT * KVL).rearrange("p (t n) -> p t n", t=NT)
        kr_n = take(NT * DR).rearrange("p (t n) -> p t n", t=NT)
        ckv_t = take(2 * TOK).rearrange("p (c n) -> p c n", c=2)
        kr_t = take(TOK)
        w_uv_sb = take(2 * H * DV).rearrange("p (c n) -> p c n", c=2)
        qs = take(2 * NB * H * TS).rearrange("p (c n) -> p c n", c=2)
        qsr = take(NB * H * TS)
        z0_base = top[0]
        z0 = take(NT * ZL).rearrange("p (t n) -> p t n", t=NT)
        w_uq_sb = take(3 * H * DN).rearrange("p (r n) -> p r n", r=3)
        w_qr_sb = take(3 * H * DR).rearrange("p (r n) -> p r n", r=3)
        w_uk_t = take(H * KVL).rearrange("p (h c) -> p h c", h=H)
        o_base = top[0]

        o, kv = [o_base], [kv_base]
        xn_t = take(KD * TOK, o).rearrange("p (k n) -> p k n", k=KD)
        w_blk = [take(KD * 512, x).rearrange("p (k n) -> p k n", k=KD) for x in (o, kv)]
        zst = [take(512, kv) for _ in range(2)]
        a = [attn_base]
        x_in = [take(D, a) for _ in range(2)]
        xn = [take(D, a) for _ in range(2)]
        junk1 = take(D, a)
        junk2 = take(QL + KVL, a)
        w_uk_n = take(2 * H * DN, a).rearrange("p (c h d) -> p c h d", c=2, h=H)
        ws_n = take(KD * P, a).rearrange("p (g j) -> p g j", g=KD)
        ws_ns = take(KD * RS, a).rearrange("p (g j) -> p g j", g=KD)

        o = [o_base]
        cq = take(QL, o)
        cq_t = take(3 * P, o).rearrange("p (r n) -> p r n", r=3)
        early = [gains_base]
        qr_tmp = take(H * 32 * 4, early)
        qn_t = take(H * P, early).rearrange("p (h n) -> p h n", h=H)
        qr_n, qr_r = take(H * DR, o), take(H * DR, o)
        ql_t = [take(QB, o).rearrange("p (h c n) -> p h c n", h=H, c=2) for _ in range(2)]
        qr_t = [take(H * P, o).rearrange("p (h n) -> p h n", h=H) for _ in range(2)]
        prob = [take(SEQ, o) for _ in range(2)]
        prob_t = [take(SEQ, early).rearrange("p (j n) -> p j n", j=8) for _ in range(2)]
        pv_t = [take(2 * P, o).rearrange("p (c n) -> p c n", c=2) for _ in range(2)]
        kr_tmp = take(DR * 2, o)
        negmax, psumq, rinv = take(64, o), take(64, o), take(64, o)

        o = [z0_base]
        ck = [take(PG * KVL, o).rearrange("p (r n) -> p r n", r=PG) for _ in range(4)]
        kr = [take(PG * DR, o).rearrange("p (r n) -> p r n", r=PG) for _ in range(4)]
        ck_t = take(2 * 4 * 512, o).rearrange("p (c j n) -> p c j n", c=2, j=4)
        kr_tt = take(2 * 512, o).rearrange("p (g n) -> p g n", g=2)
        early = [gains_base]
        p_exp = take(512, early)
        p_t = take(512, early).rearrange("p (k n) -> p k n", k=4)
        s_new, p_new, p_new_t = (take(NB * RS, early) for _ in range(3))
        o_lat = take(512, early).rearrange("p (c n) -> p c n", c=2)
        q_now = take(2 * RS, early).rearrange("p (c n) -> p c n", c=2)
        qr_now = take(RS, early)
        m_all, l_all, w_all, w_dif, l_w, l_inv = (take(NB, early) for _ in range(6))
        m_now = take(5, early)
        m_part, neg_m, alpha, l_add = (take(1, early) for _ in range(4))
        m8, m8b = take(RS, early), take(P, early)
        idx_now = [take(1, early).bitcast(U32) for _ in range(4)]
        old = [kv_base]
        acc = take(NB * KVL, old).rearrange("p (b c) -> p b c", b=NB)
        assert old[0] <= kv_base + NTP * KVL and early[0] <= gains_base + 4 * D

        o = [kv_base]
        w_o_sb = take(KD * D, o).rearrange("p (k n) -> p k n", k=KD)
        zt = [take(4 * D, o) for _ in range(2)]
        xr = [take(D, o) for _ in range(2)]
        m_t = take(KD * P, o).rearrange("p (k n) -> p k n", k=KD)
        x2_t = take(KD * P, o).rearrange("p (k n) -> p k n", k=KD)
        xo = [take(D, o) for _ in range(2)]
        junk5 = take(D, o)
        stat5 = [take(4, o) for _ in range(2)]
        assert o[0] <= x2_at[0], (o, x2_at)

        o = [attn_base]
        w_e = [(take(KD * DE, o).rearrange("p (k n) -> p k n", k=KD),
                take(KD * DE, o).rearrange("p (k n) -> p k n", k=KD),
                take(2 * D, o).rearrange("p (f n) -> p f n", f=2)) for _ in range(4)]
        xg = [take(D, o) for _ in range(2)]
        xg_t = take(KD * P, o).rearrange("p (k n) -> p k n", k=KD)
        h_n, h_t = take(DE, o), take(DE, o).rearrange("p (f n) -> p f n", f=2)
        h_s = take(DE, o)
        yo = [take(D, o) for _ in range(2)]
        slot_idx = take(2 * NBLK, o).bitcast(U32).rearrange("p (b c) -> p b c", c=2)
        idx_tok, idx_row = [take(1, o).bitcast(U32) for _ in range(2)], [take(1, o).bitcast(U32) for _ in range(2)]
        ovf_id = take(NOVF + 1, o).bitcast(I32)
        gates = take(NT * 2, o).rearrange("p (t c) -> p t c", t=NT)
        rt_base = o[0]
        g_top = take(NT * 8, o).rearrange("p (t n) -> p t n", t=NT)
        g_ind = take(NT * 8, o).bitcast(U32).rearrange("p (t n) -> p t n", t=NT)
        g_f = take(NT, o)
        pen = take(NT * 8, o).rearrange("p (t n) -> p t n", t=NT)
        e_top = take(NT * 8, o).rearrange("p (t n) -> p t n", t=NT)
        e_ind = take(NT * 8, o).bitcast(U32).rearrange("p (t n) -> p t n", t=NT)
        e_f = take(NT * 2, o).rearrange("p (t c) -> p t c", t=NT)
        n_rt = [take(NT * 2, o).rearrange("p (t c) -> p t c", t=NT) for _ in range(6)]
        cnt = [take(NE, o) for _ in range(4)]
        g_sub, g_exp = (take(NT * 8, o).rearrange("p (t n) -> p t n", t=NT) for _ in range(2))
        d_sub, d_exp, g_den, w_one, w_two = (take(NT, o) for _ in range(5))
        pos_i = take(NT * 2, o).bitcast(U32)
        assert o[0] <= x2_at[0], (o, x2_at)
        o2 = [attn_base + 4 * 6144]
        e_log = take(NT * NE, o2).rearrange("p (t n) -> p t n", t=NT)
        hot = take(NT * 2 * NE, o2).rearrange("p (t c n) -> p t c n", t=NT, c=2)
        mask = take(NT * NE, o2).rearrange("p (t n) -> p t n", t=NT)
        rank = take(NT * NE, o2).rearrange("p (t n) -> p t n", t=NT)
        assert o2[0] <= attn_base + 4 * 6144 + 2 * D + KD * P + 3 * DE + 2 * D
        o3 = [x2_at[0] - 2700]
        assert o[0] <= o3[0], (o, o3)
        cum = take(NT * NE, o3).rearrange("p (t n) -> p t n", t=NT)
        prod = take(NT * 2 * NE, o3).rearrange("p (t c n) -> p t c n", t=NT, c=2)
        slot_f = take(256, o3)
        fill = take(256, o3)
        o = [attn_base]
        y2 = [take(2 * D, o) for _ in range(2)]
        fin = [take(D, o) for _ in range(2)]
        junk8 = take(D, o)
        stat8 = [take(2, o) for _ in range(2)]

        tab_in, small_in, wuk_in, wuq_in, uv_in, wo_in = (sem(n) for n in (
            "tables_in", "small_in", "wuk_in", "wuq_in", "wuv_in", "wo_in"))
        ws_zero, ws_ready, wsm_ready = sem("ws_zeroed"), sem("ws_loaded"), sem("ws_masked")
        setup_mm, setup_ev = sem("setup_turned"), sem("setup_copied")
        x_loaded = [sem(f"x_loaded{i}") for i in range(2)]
        x_sq, x_rstd, xn_ready = sem("x_squared"), sem("x_rstd"), sem("xn_ready")
        xt_mm = sem("xn_turned")
        xt_ev = [sem("xn_copied_act"), sem("xn_copied_dve")]
        w_loaded = [sem(f"w_in_loaded{i}") for i in range(2)]
        z_mm, z_ev = sem("z_summed"), sem("z_taken")
        z_stored = [sem(f"z_stored{i}") for i in range(2)]
        lat_stored = sem("latent_stored")
        lat_ready = sem("latent_ready")
        p_sq, p_rs, p_cn, p_kr = sem("latent_squared"), sem("latent_rstd"), sem("latent_normed"), sem("krope_ready")
        b_mm = [sem(f"bank{i}_written") for i in range(2)]
        b_ev = [sem(f"bank{i}_taken") for i in range(2)]
        qrope_done = sem("qrope_done")
        s_mm, s_nm, s_exp, s_rinv = sem("scores_ready"), sem("negmax_ready"), sem("probs_ready"), sem("rinv_ready")
        t_mm = [sem("probs_turned_lo"), sem("probs_turned_hi")]
        t_ev = [sem("probs_t_lo"), sem("probs_t_hi")]
        act_c, dve_c, pool_c = sem("act_steps"), sem("dve_steps"), sem("pool_steps")
        ends = sem("stage_ends")
        done = {"n": 0}
        idx_ready = sem("page_index_ready")
        pt_in = sem("page_table_in")
        c_in = [sem(f"cache_in{i}") for i in range(4)]
        c_tr = sem("cache_turned")
        kt_in = [sem("turned_by_act"), sem("turned_by_dve")]
        c_s, c_neg, c_p, c_pt, c_ptc = (sem(n) for n in (
            "cache_scores", "cache_negmax", "cache_probs", "cache_probs_turned", "cache_probs_t"))
        c_sub, c_pv, c_acc, q_ready = sem("shifted"), sem("pv_ready"), sem("acc_done"), sem("batch_queries")
        late_in = sem("late_gains_in")
        n_pe, n_dve, n_act = sem("new_pe"), sem("new_dve"), sem("new_act")
        z_in = [sem(f"z_in{i}") for i in range(2)]
        v_sq, v_rs, v_n = sem("v_squared"), sem("v_rstd"), sem("v_normed")
        mix_mm, sgu_ok, mrg_ok, at_ok = sem("mixed"), sem("sgu_ready"), sem("merged"), sem("gated_attn")
        mt_mm, mt_ev, y_mm, x2_ok = sem("merged_turned"), sem("merged_t"), sem("wo_summed"), sem("x2_ready")
        o_sq, o_rs, o_n, ot_mm, ot_ev = (sem(n) for n in ("x2_squared", "x2_rstd", "x2_normed", "x2n_turned", "x2n_t"))
        lg_mm, lg_ok = sem("logits_summed"), sem("logits_ready")
        xt_st = [sem(f"xt_stored{i}") for i in range(2)]
        v_st = sem("v_stored")
        r_pe, r_dve, r_sub, r_exp = sem("route_pe"), sem("route_dve"), sem("route_exp_in"), sem("route_exp_out")
        r_pos = sem("slot_positions")
        x_inv, v_inv, o_inv, f_inv = sem("x_inv"), sem("v_inv"), sem("x2_inv"), sem("f_inv")
        small_zero = sem("stats_zeroed")
        x2_cp = sem("x2_kept")
        fill_ok = sem("fill_ready")
        qrn_ready, idx_step, x_idx = sem("qrope_copied"), sem("page_index_steps"), sem("slot_index_steps")
        fill_in, scat_in, slots_in, slots_ok = sem("slots_filled"), sem("slots_scattered"), sem("slots_in"), sem("slot_index")
        e_w = [sem(f"expert_w{i}") for i in range(4)]
        e_x = [sem(f"expert_rows{i}") for i in range(2)]
        xg_zero = sem("rows_zeroed")
        e_xt, e_xe, e_g, e_u, e_si, e_h, e_ht, e_he = (sem(n) for n in (
            "rows_turned", "rows_t", "gate_summed", "up_summed", "gate_silu", "hidden", "hidden_turned", "hidden_t"))
        e_y = [sem("y_lo"), sem("y_hi")]
        e_ye = [sem("y_lo_copied"), sem("y_hi_copied")]
        e_sc = [sem(f"y_scattered{i}") for i in range(2)]
        yo_free = [sem(f"y_slot_free{i}") for i in range(2)]
        marks = sem("marks")
        moe_end = sem("experts_done")
        f_in = [sem(f"y_rows_in{i}") for i in range(2)]
        f_sum, f_sq, f_rs, f_ok = sem("f_summed"), sem("f_squared"), sem("f_rstd"), sem("f_ready")
        f_st = [sem(f"out_stored{i}") for i in range(2)]

        xp = x_prompt.rearrange("b s d -> (b s) d")
        xs = x_sample.rearrange("b s d -> (b s) d")
        yp = y_prompt.rearrange("b s d -> (b s) d")
        ys = y_sample.rearrange("b s d -> (b s) d")
        w_in_v = w_in[0].rearrange("(k p) n -> p k n", p=P)
        units, sched = attention_schedule()
        bank0_units = 6 * NT + NTP * H
        block = ctx.enter_context(nc.Block())

        turn_units = [("c", 0, 0), ("c", 0, 1), ("r", 0, 0), ("c", 1, 0), ("c", 1, 1),
                      ("c", 2, 0), ("c", 2, 1), ("r", 1, 0), ("c", 3, 0), ("c", 3, 1)]
        NU = len(turn_units)

        def key_row(j, kk):
            return 8 * (j // 2) + 2 * kk + j % 2

        def turned_at(u):
            kind, j, c = turn_units[u]
            return ck_t[:, c, j, :] if kind == "c" else kr_tt[:, j, :]

        def stage_end(eng, k):
            eng.drain().then_inc(ends, 1)
            eng.wait_ge(ends, 4 * k)

        @block.sync
        def _(sp):
            sp.dma_start(K, tables).then_inc(tab_in, 16)

            def x_load(t, s, rows, src):
                sp.dma_start(x_in[s][0:rows, :], src).then_inc(x_loaded[s], 16)

            x_load(0, 0, P, xp[0:P, :])
            x_load(1, 1, P, xp[P:2 * P, :])
            sp.dma_start(g1, norm1_g[0].partition_broadcast(P)).then_inc(small_in, 16)
            sp.dma_start(w_blk[0][:, :, 0:352], w_in_v[:, :, 0:352]).then_inc(w_loaded[0], 16)
            for dst, src in ((gq, q_norm_g[0]),
                             (gkv, kv_norm_g[0]), (rbias[:, 0:NG], b_rg[0]), (rbias[:, NG:], b_re[0])):
                sp.dma_start(dst, src.partition_broadcast(P)).then_inc(small_in, 16)
            sp.dma_start(ids_sb, ids).then_inc(small_in, 16)
            with nc.allow_non_contiguous_dma(reason="small tables"):
                sp.dma_start(w_router[:, :, 0:NG], w_rg[0].rearrange("(k p) n -> p k n", p=P)).then_inc(small_in, 16)
                sp.dma_start(w_router[:, :, NG:], w_re[0].rearrange("(k p) n -> p k n", p=P)).then_inc(small_in, 16)
                sp.dma_start(bs_t, b_s[0].rearrange("g i -> i g")).then_inc(small_in, 16)
                for b in range(NB):
                    sp.dma_start(bs_ts[TS * b:TS * b + TS, :], b_s[0, :, 0:TS].rearrange("g i -> i g")).then_inc(small_in, 16)
                pt = page_table.rearrange("b (c g) -> g (b c)", g=PG)
                for g in range(PG):
                    sp.dma_start(page_raw[8 * g:8 * g + 8, :], pt[g].partition_broadcast(8)).then_inc(pt_in, 16)
                sp.dma_start(w_uk_n, w_uk[0].rearrange("(c p) h d -> p c h d", p=P)).then_inc(wuk_in, 16)
                sp.dma_start(ws_n, w_s[0].rearrange("g i j -> i g j")).then_inc(ws_ready, 16)
                sp.wait_ge(ws_zero, 1)
                for b in range(NB):
                    sp.dma_start(ws_ns[TS * b:TS * b + TS, :, TS * b:TS * b + TS],
                                 w_s[0, :, 0:TS, 0:TS].rearrange("g i j -> i g j")).then_inc(ws_ready, 16)
            sp.dma_start(w_blk[1][:, :, 0:352], w_in_v[:, :, 352:704]).then_inc(w_loaded[1], 16)
            sp.dma_start(w_uq_sb, w_uq[0].rearrange("(r p) h d -> p r (h d)", p=P)).then_inc(wuq_in, 16)
            sp.dma_start(w_qr_sb, w_qr[0].rearrange("(r p) h d -> p r (h d)", p=P)).then_inc(wuq_in, 16)
            sp.dma_start(w_uv_sb, w_uv[0].rearrange("(c p) h d -> p c (h d)", p=P)).then_inc(uv_in, 16)
            with sp.Fori(0, 3) as i:
                for s in range(2):
                    sp.wait_ge(xn_ready, 2 * i + s + 1)
                    x_load(None, s, P, xp[bass.ds(2 * P * i + (s + 2) * P, P), :])
            sp.wait_ge(xn_ready, 7)
            x_load(8, 0, RS, xs)

            sp.wait_ge(z_mm, NT)
            sp.dma_start(w_blk[0], w_in_v[:, :, ZL:ZL + 512]).then_inc(w_loaded[0], 16)

            def block_moves(b, s, load):
                if load:
                    sp.wait_ge(z_mm, NT * 2 + NT * b)
                    sp.dma_start(w_blk[1 - s], w_in_v[:, :, bass.ds(512 * b + ZL + 512, 512)]).then_inc(w_loaded[1 - s], 16)
                cols = [z_act[t * P:t * P + rows_of(t), bass.ds(512 * b, 512)] for t in range(NT)]
                for t in range(NT):
                    u = (s * NT + t) % 2
                    r = rows_of(t)
                    sp.wait_ge(z_ev, NT * 2 + NT * b + t + 1)
                    sp.sem_inc(marks, 1)
                    sp.dma_start(cols[t], zst[u][0:r, :]).then_inc(z_stored[u], 16)

            with sp.Fori(0, 3) as i:
                block_moves(2 * i, 0, True)
                block_moves(2 * i + 1, 1, True)
            block_moves(6, 0, True)
            block_moves(7, 1, False)

            sp.wait_ge(lat_ready, 2)
            sp.dma_start(ckv_prompt.rearrange("l b t p c -> p (l b t) c"), ckv_n[:, 0:NTP, :]).then_inc(lat_stored, 16)
            sp.dma_start(kr_prompt.rearrange("l b t p c -> p (l b t) c"), kr_n[:, 0:NTP, :]).then_inc(lat_stored, 16)
            sp.dma_start(ckv_sample.rearrange("l b t c -> (l b t) c"), ckv_n[0:RS, NTP, :]).then_inc(lat_stored, 16)
            sp.dma_start(kr_sample.rearrange("l b t c -> (l b t) c"), kr_n[0:RS, NTP, :]).then_inc(lat_stored, 16)
            sp.wait_ge(lat_stored, 64)

            sp.wait_ge(ends, 12)
            for dst, src in ((g2, norm2_g[0]), (gf, norm_f_g), (gv, sgu_norm_g[0])):
                sp.dma_start(dst, src.partition_broadcast(P)).then_inc(late_in, 16)
            for u in range(2):
                sp.wait_ge(z_stored[u], 16 * (8 * NT // 2) + 16)

            def z_load(s, r, z_src, x_src):
                sp.dma_start(zt[s][0:r, :], z_src).then_inc(z_in[s], 16)
                sp.dma_start(xr[s][0:r, :], x_src).then_inc(z_in[s], 16)

            z_load(0, P, z_act[0:P, :], xp[0:P, :])
            sp.dma_start(w_o_sb, w_o[0].rearrange("(k p) n -> p k n", p=P)).then_inc(wo_in, 16)
            z_load(1, P, z_act[P:2 * P, :], xp[P:2 * P, :])
            with sp.Fori(0, 3) as i:
                for s in range(2):
                    sp.wait_ge(o_n, 2 * i + s + 1)
                    sp.wait_ge(x2_cp, 2 * i + s + 1)
                    z_load(s, P, z_act[bass.ds(2 * P * i + (s + 2) * P, P), :], xp[bass.ds(2 * P * i + (s + 2) * P, P), :])
                    sp.dma_start(xt_rows[bass.ds(2 * P * i + s * P, P), :], xo[s]).then_inc(xt_st[s], 16)
            sp.wait_ge(o_n, 7)
            sp.wait_ge(x2_cp, 7)
            z_load(0, RS, z_act[8 * P:TOK, :], xs)
            for t in range(6, NT):
                sp.wait_ge(o_n, t + 1)
                r = rows_of(t)
                sp.dma_start(xt_rows[t * P:t * P + r, :], xo[t % 2][0:r, :]).then_inc(xt_st[t % 2], 16)
            sp.wait_ge(v_n, NT)
            sp.dma_start(v_sample.rearrange("l b t c -> (l b t) c"), zt[0][0:RS, D:2 * D]).then_inc(v_st, 16)
            sp.wait_ge(v_st, 16)

            sp.wait_ge(fill_ok, 1)
            slots_v = slot_rows.rearrange("(b r) c -> b (r c)", r=P)
            sp.dma_start(slots_v, fill[0:NBLK, :].bitcast(I32)).then_inc(fill_in, 16)

            def w_load(s, e):
                g, u, dn = w_e[s]
                for dst, src, k in ((g, w_gate, KD), (u, w_up, KD), (dn, w_down, 2)):
                    sp.dma_start(dst.rearrange("p k n -> p (k n)"),
                                 src[0, bass.ds(e, 1)].rearrange("e (p k) n -> p (e k n)", p=P)).then_inc(e_w[s], 16)

            sp.wait_ge(ends, 16)
            for s in range(4):
                w_load(s, s)
            sp.wait_ge(scat_in, 16 * 2 * NT)
            sp.dma_start(fill[0:NBLK, :].bitcast(I32), slots_v).then_inc(slots_in, 16)
            with sp.Fori(0, 15) as i:
                for s in range(4):
                    sp.wait_ge(e_y[1], 4 * i + s + 1)
                    w_load(s, 4 * i + s + 4)
            sp.wait_ge(slots_ok, 1)
            total = sp.value_load(ovf_id[0:1, NOVF:NOVF + 1], min_val=0, max_val=NOVF)
            sp.wait_ge(e_y[1], NE)
            with sp.Fori(0, NOVF) as j:
                with sp.If(total > j):
                    e = sp.value_load(ovf_id[0:1, bass.ds(j, 1)], min_val=0, max_val=NE - 1)
                    sp.wait_ge(e_y[1], NE + j)
                    w_load(0, e)

            sp.wait_ge(moe_end, 1)
            yr = y_rows.rearrange("(n c) d -> n (c d)", c=2)
            sp.dma_start(y2[0], yr[0:P, :]).then_inc(f_in[0], 16)
            sp.dma_start(y2[1], yr[P:2 * P, :]).then_inc(f_in[1], 16)
            with sp.Fori(0, 3) as i:
                for s in range(2):
                    sp.wait_ge(f_sum, 2 * i + s + 1)
                    sp.dma_start(y2[s], yr[bass.ds(2 * P * i + (s + 2) * P, P), :]).then_inc(f_in[s], 16)
                    sp.wait_ge(f_ok, 2 * i + s + 1)
                    sp.dma_start(yp[bass.ds(2 * P * i + s * P, P), :], fin[s]).then_inc(f_st[s], 16)
            sp.wait_ge(f_sum, 7)
            sp.dma_start(y2[0][0:RS, :], yr[8 * P:TOK, :]).then_inc(f_in[0], 16)
            for t in range(6, NT):
                sp.wait_ge(f_ok, t + 1)
                if t < NTP:
                    sp.dma_start(yp[t * P:(t + 1) * P, :], fin[t % 2]).then_inc(f_st[t % 2], 16)
                else:
                    sp.dma_start(ys, fin[0][0:RS, :]).then_inc(f_st[0], 16)
            sp.wait_ge(f_st[0], 16 * 6)
            sp.wait_ge(f_st[1], 16 * 5)

        @block.tensor
        def _(pe):
            mm, tr = nc.tensor.matmul, nc.tensor.transpose
            pe.wait_ge(tab_in, 16)
            pe.wait_ge(wuk_in, 16)
            for u in range(4):
                b = 6 + u % 2
                if u >= 2:
                    pe.wait_ge(setup_ev, u - 1)
                for i in range(4):
                    h, c = 2 * u + i // 2, i % 2
                    last = tr(bank(b)[:, P * i:P * i + P], w_uk_n[:, c, h, :], ident)
                last.then_inc(setup_mm, 1)
            pe.wait_ge(wsm_ready, 1)
            for u in range(2):
                pe.wait_ge(setup_ev, 3 + u)
                for i in range(4):
                    last = tr(bank(6 + u)[:, P * i:P * i + P], ws_n[:, 4 * u + i, :], ident)
                last.then_inc(setup_mm, 1)
            pe.wait_ge(setup_ev, 5)
            for g in range(KD):
                last = tr(bank(6)[0:RS, RS * g:RS * g + RS], ws_ns[0:RS, g, :], ident[0:RS, 0:RS])
            last.then_inc(setup_mm, 1)

            def turn_x(n, s, r):
                pe.wait_ge(xn_ready, n + 1)
                pe.wait_ge(xt_ev[0], n + 1)
                pe.wait_ge(xt_ev[1], n + 1)
                for k in range(KD):
                    last = tr(bank(2 * s, 2)[:, P * k:P * k + r], xn[s][0:r, P * k:P * k + P], ident[0:r, 0:r])
                last.then_inc(xt_mm, 1)

            with pe.Fori(0, 4) as i:
                for s in range(2):
                    turn_x(2 * i + s, s, P)
            turn_x(8, 0, RS)
            pe.wait_ge(xt_ev[0], NT + 2)
            pe.wait_ge(xt_ev[1], NT + 2)

            def z_block(n, s, w, i_loaded, first=False):
                pe.wait_ge(w_loaded[s], 16 * i_loaded)
                for t in range(NT):
                    r = rows_of(t)
                    u = (s * NT + t) % 2
                    if not (first and t < 2):
                        pe.wait_ge(z_ev, NT * n + t - 1)
                    for k in range(KD):
                        last = mm(bank(4 + u)[0:r, 0:w], xn_t[:, k, t * P:t * P + r], w_blk[s][:, k, 0:w],
                                  start=(k == 0), stop=(k == KD - 1))
                    last.then_inc(z_mm, 1)

            z_block(0, 0, 352, 1, True)
            z_block(1, 1, 352, 1)
            with pe.Fori(0, 4) as i:
                z_block(2 * i + 2, 0, 512, i + 2)
                z_block(2 * i + 3, 1, 512, i + 2)
            pe.wait_ge(z_ev, 10 * NT)
            stage_end(pe, 1)

            pe.wait_ge(wuq_in, 32)
            pe.wait_ge(uv_in, 16)
            pe.wait_ge(setup_ev, 7)
            used = [0, 0]

            def open_bank(b):
                if used[b]:
                    pe.wait_ge(b_ev[b], used[b])
                used[b] += 1

            for what, n in sched:
                if what == "Q":
                    t, r, s = n, rows_of(n), n % 2
                    pe.wait_ge(p_cn, t + 1)
                    pe.wait_ge(p_kr, t + 1)
                    open_bank(0)
                    for i in range(3):
                        tr(bank(0)[:, P * i:P * i + r], cq[0:r, P * i:P * i + P], ident[0:r, 0:r])
                    tr(bank(0)[0:DR, 384:384 + r], kr_n[0:r, t, :], ident[0:r, 0:r]).then_inc(b_mm[0], 1)
                    open_bank(1)
                    for c in range(2):
                        last = tr(bank(1)[:, P * c:P * c + r], ckv_n[0:r, t, P * c:P * c + P], ident[0:r, 0:r])
                    last.then_inc(b_mm[1], 1)
                    pe.wait_ge(b_ev[0], used[0])
                    for u in range(2):
                        open_bank(u)
                        for i in range(4):
                            h = 4 * u + i
                            for c in range(3):
                                last = mm(bank(u)[:, P * i:P * i + r], w_uq_sb[:, c, P * h:P * h + P], cq_t[:, c, 0:r],
                                          start=(c == 0), stop=(c == 2))
                        last.then_inc(b_mm[u], 1)
                    open_bank(0)
                    for c in range(3):
                        last = mm(bank(0)[0:r, :], cq_t[:, c, 0:r], w_qr_sb[:, c, :], start=(c == 0), stop=(c == 2))
                    last.then_inc(b_mm[0], 1)
                    for u in range(4):
                        b = 1 - u % 2
                        open_bank(b)
                        for i in range(4):
                            h, c = 2 * u + i // 2, i % 2
                            last = mm(bank(b)[:, P * i:P * i + r], w_uk_t[:, h, P * c:P * c + P], qn_t[:, h, 0:r],
                                      start=True, stop=True)
                        last.then_inc(b_mm[b], 1)
                    pe.wait_ge(qrope_done, t + 1)
                    for u in range(2):
                        b = 1 - u
                        open_bank(b)
                        for i in range(4):
                            h = 4 * u + i
                            last = tr(bank(b)[0:DR, P * i:P * i + r], qr_r[0:r, DR * h:DR * h + DR], ident[0:r, 0:r])
                        last.then_inc(b_mm[b], 1)
                    pe.wait_ge(b_ev[0], used[0])
                    pe.wait_ge(b_ev[1], used[1])
                elif what == "S":
                    t, h = units[n]
                    s, sl = t % 2, n % 2
                    if n >= 2:
                        pe.wait_ge(s_exp, n - 1)
                    for c0 in range(0, P * (t + 1), 512):
                        w = min(512, P * (t + 1) - c0)
                        out = bank(2 + 2 * sl, 2)[:, c0:c0 + w]
                        mm(out, ql_t[s][:, h, 0, :], ckv_t[:, 0, c0:c0 + w], start=True, stop=False)
                        mm(out, ql_t[s][:, h, 1, :], ckv_t[:, 1, c0:c0 + w], start=False, stop=False)
                        diag = c0 <= P * t < c0 + w
                        last = mm(out, qr_t[s][0:DR, h, :], kr_t[0:DR, c0:c0 + w], start=False, stop=True)
                        if diag:
                            last = mm(bank(2 + 2 * sl, 2)[:, P * t:P * t + P], ident, const("negmask"),
                                      start=False, stop=True, skip_group_check=True)
                    last.then_inc(s_mm, 1)
                elif what == "T":
                    t, h = units[n]
                    pe.wait_ge(s_exp, n + 1)
                    for half in range(2):
                        js = range(4 * half, min(4 * half + 4, t + 1))
                        if not js:
                            continue
                        k = n if half == 0 else n - 4 * H
                        if k >= 1:
                            pe.wait_ge(t_ev[half], k)
                        for j in js:
                            last = tr(bank(6 + half)[:, P * (j % 4):P * (j % 4) + P], prob[n % 2][:, P * j:P * j + P], ident)
                        last.then_inc(t_mm[half], 1)
                elif what == "PV":
                    t, h = units[n]
                    b = n % 2
                    pe.wait_ge(t_ev[0], n + 1)
                    if t >= 4:
                        pe.wait_ge(t_ev[1], n - 4 * H + 1)
                    open_bank(b)
                    for c in range(2):
                        for j in range(t + 1):
                            last = mm(bank(b)[:, P * c:P * c + P], ckv_n[:, j, P * c:P * c + P], prob_t[b][:, j, :],
                                      start=(j == 0), stop=(j == t))
                    last.then_inc(b_mm[b], 1)
                elif what == "UV":
                    t, h = units[n]
                    b = n % 2
                    open_bank(b)
                    for c in range(2):
                        last = mm(bank(b)[:, 0:DV], pv_t[b][:, c, :], w_uv_sb[:, c, DV * h:DV * h + DV],
                                  start=(c == 0), stop=(c == 1))
                    last.then_inc(b_mm[b], 1)
            pe.wait_ge(b_ev[0], used[0])
            pe.wait_ge(b_ev[1], used[1])
            stage_end(pe, 2)

            pe.wait_ge(n_dve, 1)
            for b in range(NB):
                new, cols = bank(5)[0:RS, RS * b:RS * b + RS], slice(RS * b, RS * b + RS)
                mm(new, qs[:, 0, cols], ckv_t[:, 0, SEQ:TOK], start=True, stop=False)
                mm(new, qs[:, 1, cols], ckv_t[:, 1, SEQ:TOK], start=False, stop=False)
                last = mm(new, qsr[0:DR, cols], kr_t[0:DR, SEQ:TOK], start=False, stop=True)
            last.then_inc(n_pe, 1)
            pe.wait_ge(n_act, 1)
            for b in range(NB):
                last = tr(bank(6)[0:RS, RS * b:RS * b + RS], p_new[0:RS, RS * b:RS * b + RS], ident[0:RS, 0:RS])
            last.then_inc(n_pe, 1)
            pe.wait_ge(n_dve, 2)
            for b in range(NB):
                last = mm(bank(0, 4)[0:RS, KVL * b:KVL * b + KVL], p_new_t[0:RS, RS * b:RS * b + RS], ckv_n[0:RS, NTP, :],
                          start=True, stop=True)
            last.then_inc(n_pe, 1)
            pe.wait_ge(n_dve, 3)

            def turn(n, q, us, first=False):
                for u in us:
                    if u >= 5:
                        pe.wait_ge(kt_in[(u - 5) % 2], 5 * n + (u - 5) // 2 + 1)
                    elif not first:
                        pe.wait_ge(kt_in[(u + 5) % 2], 5 * n - 5 + (u + 5) // 2 + 1)
                    kind, j, c = turn_units[u]
                    for kk in range(4):
                        if kind == "c":
                            src = ck[q][:, key_row(j, kk), P * c:P * c + P]
                        else:
                            src = kr[q][:, 8 * j + 2 * kk:8 * j + 2 * kk + 2, :].rearrange("p r n -> p (r n)")
                        last = tr(bank(u % 5)[:, P * kk:P * kk + P], src, ident)
                    last.then_inc(c_tr, 1)

            def score(n):
                for e in range(2):
                    pe.wait_ge(kt_in[e], 5 * n + 5)
                for c in range(3):
                    for j in range(4):
                        half = slice(DR * (j % 2), DR * (j % 2) + DR)
                        last = mm(bank(5)[RS * j:RS * j + RS, :], q_now[:, c, :] if c < 2 else qr_now[half, :],
                                  ck_t[:, c, j, :] if c < 2 else kr_tt[half, j // 2, :], start=(c == 0), stop=(c == 2))
                last.then_inc(c_s, 1)

            def turn_probs(n):
                pe.wait_ge(c_p, n + 1)
                for kk in range(4):
                    last = tr(bank(6)[:, P * kk:P * kk + P], p_exp[:, P * kk:P * kk + P], ident)
                last.then_inc(c_pt, 1)

            def weigh(n, q):
                pe.wait_ge(c_ptc, n + 1)
                pe.wait_ge(c_acc, n + 1)
                for kk in range(4):
                    for j in range(4):
                        last = mm(bank(7)[RS * j:RS * j + RS, 0:KVL], p_t[:, kk, RS * j:RS * j + RS],
                                  ck[q][:, key_row(j, kk), :], start=(kk == 0), stop=(kk == 3))
                last.then_inc(c_pv, 1)

            pe.wait_ge(c_in[0], 32)
            turn(0, 0, range(NU), first=True)
            pe.wait_ge(q_ready, 1)
            score(0)

            def batch(i, last_batch):
                for q in range(4):
                    n = 4 * i + q
                    more = q < 3 or not last_batch
                    if more:
                        pe.wait_ge(c_in[(q + 1) % 4], 32 * i + (32 if q < 3 else 64))
                        turn(n + 1, (q + 1) % 4, range(6))
                    turn_probs(n)
                    if more:
                        turn(n + 1, (q + 1) % 4, range(6, NU))
                    weigh(n, q)
                    if more:
                        if q == 3:
                            pe.wait_ge(q_ready, i + 2)
                        score(n + 1)

            with pe.Fori(0, NB - 1) as i:
                batch(i, False)
            batch(NB - 1, True)
            pe.wait_ge(n_dve, 4)
            tr(bank(6)[0:NB, 0:P], m_all, ident).then_inc(n_pe, 1)
            pe.wait_ge(n_dve, 5)
            tr(bank(6)[:, P:P + NB], m8b[0:NB, :], ident[0:NB, 0:NB]).then_inc(n_pe, 1)
            pe.wait_ge(n_dve, 6)
            mm(bank(6)[:, 2 * P:2 * P + NB], const("same_q"), l_w, start=True, stop=True).then_inc(n_pe, 1)
            pe.wait_ge(n_dve, 7)
            for c in range(2):
                for b in range(NB):
                    last = mm(bank(7)[:, NB * RS * c + RS * b:NB * RS * c + RS * b + RS], acc[:, b, P * c:P * c + P],
                              const("same_q")[:, 0:RS], start=True, stop=True)
            last.then_inc(n_pe, 1)
            pe.wait_ge(n_dve, 8)
            for h in range(H):
                for c in range(2):
                    last = mm(bank(0, 2)[0:RS, DV * h:DV * h + DV], o_lat[:, c, RS * h:RS * h + RS],
                              w_uv_sb[:, c, DV * h:DV * h + DV], start=(c == 0), stop=(c == 1))
            last.then_inc(n_pe, 1)
            pe.wait_ge(n_act, 3)
            stage_end(pe, 3)

            pe.wait_ge(wo_in, 16)

            def merge(n, s, r, wst):
                pe.wait_ge(v_n, n + 1)
                pe.wait_ge(sgu_ok, n + 1)
                for g in range(KD):
                    last = mm(bank(0, 2)[0:r, P * g:P * g + P], wst[0:r, g, 0:r], zt[s][0:r, D + P * g:D + P * g + P],
                              start=True, stop=True)
                last.then_inc(mix_mm, 1)
                pe.wait_ge(mrg_ok, n + 1)
                pe.wait_ge(ot_ev, n + 1)
                for k in range(KD):
                    last = tr(bank(2, 2)[:, P * k:P * k + r], zt[s][0:r, P * k:P * k + P], ident[0:r, 0:r])
                last.then_inc(mt_mm, 1)
                pe.wait_ge(mt_ev, n + 1)
                for half in range(2):
                    for k in range(KD):
                        last = mm(bank(4 + half)[0:r, :], m_t[:, k, 0:r], w_o_sb[:, k, 512 * half:512 * half + 512],
                                  start=(k == 0), stop=(k == KD - 1))
                last.then_inc(y_mm, 1)
                pe.wait_ge(o_n, n + 1)
                for k in range(KD):
                    last = tr(bank(2, 2)[:, P * k:P * k + r], xo[s][0:r, P * k:P * k + P], ident[0:r, 0:r])
                last.then_inc(ot_mm, 1)
                pe.wait_ge(ot_ev, n + 2)
                pe.wait_ge(lg_ok, n + 1)
                for k in range(KD):
                    last = mm(bank(6)[0:r, 0:72], x2_t[:, k, 0:r], w_router[:, k, :], start=(k == 0), stop=(k == KD - 1))
                last.then_inc(lg_mm, 1)

            with pe.Fori(0, 4) as i:
                for s in range(2):
                    merge(2 * i + s, s, P, ws_t)
            merge(8, 0, RS, ws_ts)
            pe.wait_ge(lg_ok, NT + 1)
            stage_end(pe, 4)

            pe.wait_ge(r_dve, 1)
            for t in range(NT):
                out = bank(t // 8)[:, NE * (t % 8):NE * (t % 8) + NE]
                mm(out, const("before"), mask[:, t, :], start=True, stop=False)
                mm(out, ones, cum[:, t, :], start=False, stop=True)
            mm(bank(1)[:, NE:2 * NE], ones, rank[:, 0, :], start=True, stop=True).then_inc(r_pe, 1)
            pe.wait_ge(r_dve, 2)
            for c in range(2):
                last = tr(bank(2)[:, P * c:P * c + NBLK], slot_f.rearrange("p (r c) -> p c r", c=2)[0:NBLK, c, :],
                          ident[0:NBLK, 0:NBLK])
            last.then_inc(r_pe, 1)
            pe.wait_ge(slots_ok, 1)

            def expert(n, sw, s, i_w, i_x):
                g, u, dn = w_e[sw]
                pe.wait_ge(e_x[s], 16 * i_x)
                for k in range(KD):
                    last = tr(bank(0, 2)[:, P * k:P * k + P], xg[s].rearrange("p (n k) -> p k n", k=KD)[:, k, :], ident)
                last.then_inc(e_xt, 1)
                pe.wait_ge(e_w[sw], 48 * i_w)
                pe.wait_ge(e_xe, 2 * n + 2)
                for k in range(KD):
                    last = mm(bank(2)[:, 0:DE], xg_t[:, k, :], g[:, k, :], start=(k == 0), stop=(k == KD - 1))
                last.then_inc(e_g, 1)
                for k in range(KD):
                    last = mm(bank(3)[:, 0:DE], xg_t[:, k, :], u[:, k, :], start=(k == 0), stop=(k == KD - 1))
                last.then_inc(e_u, 1)
                pe.wait_ge(e_h, n + 1)
                for f in range(2):
                    last = tr(bank(4)[:, P * f:P * f + P], h_n.rearrange("p (n f) -> p f n", f=2)[:, f, :], ident)
                last.then_inc(e_ht, 1)
                pe.wait_ge(e_he, n + 1)
                for half in range(2):
                    pe.wait_ge(e_ye[half], n + 1)
                    for f in range(2):
                        last = mm(bank(5 + half), h_t[:, f, :], dn[:, f, 512 * half:512 * half + 512],
                                  start=(f == 0), stop=(f == 1))
                    last.then_inc(e_y[half], 1)

            with pe.Fori(0, 16) as i:
                for s in range(4):
                    expert(4 * i + s, s, s % 2, i + 1, 2 * i + s // 2 + 1)
            total = pe.value_load(ovf_id[0:1, NOVF:NOVF + 1], min_val=0, max_val=NOVF)
            with pe.Fori(0, NOVF) as j:
                with pe.If(total > j):
                    expert(NE + j, 0, 0, 17 + j, 33 + j)

        @block.scalar
        def _(act):
            A = nc.scalar.activation
            act.sem_inc(xt_ev[0], 2)
            act.sem_inc(ot_ev, 1)
            act.sem_inc(e_ye[0], 1)
            for u in range(2):
                act.sem_inc(z_stored[u], 16)
            act.wait_ge(tab_in, 16)
            act.wait_ge(small_zero, 1)

            for u in range(4):
                act.wait_ge(setup_mm, u + 1)
                nc.scalar.copy(w_uk_t[:, 2 * u:2 * u + 2, :].rearrange("p h c -> p (h c)"), bank(6 + u % 2)).then_inc(setup_ev, 1)
            for u in range(2):
                act.wait_ge(setup_mm, 5 + u)
                nc.scalar.copy(ws_t[:, 4 * u:4 * u + 4, :].rearrange("p g i -> p (g i)"), bank(6 + u)).then_inc(setup_ev, 1)
            act.wait_ge(setup_mm, 7)
            nc.scalar.copy(ws_ts[0:RS, :, :].rearrange("p g i -> p (g i)"), bank(6)[0:RS, 0:RS * KD]).then_inc(setup_ev, 1)

            def square_x(n, s, r, i_l):
                act.wait_ge(x_loaded[s], 16 * i_l)
                A(junk1[0:r, :], x_in[s][0:r, :], ACT.Square, scale=D ** -0.5, accum_out=small[0:r, s:s + 1]).then_inc(x_sq, 1)
                act.wait_ge(x_sq, n + 1)
                A(small[0:r, 2 + s:3 + s], small[0:r, s:s + 1], ACT.Sqrt, bias=eps[0:r]).then_inc(x_rstd, 1)

            def copy_x(n, s, r, dst):
                act.wait_ge(xt_mm, n + 1)
                nc.scalar.copy(dst, bank(2 * s).rearrange("p (k n) -> p k n", k=4)[:, :, 0:r]).then_inc(xt_ev[0], 1)

            with act.Fori(0, 4) as i:
                for s in range(2):
                    square_x(2 * i + s, s, P, i + 1)
                    copy_x(2 * i + s, s, P, xn_t[:, 0:4, bass.ds(2 * P * i + P * s, P)])
            square_x(8, 0, RS, 5)
            copy_x(8, 0, RS, xn_t[:, 0:4, SEQ:TOK])

            def take_z(n, s):
                for t in range(NT):
                    r = rows_of(t)
                    u = (s * NT + t) % 2
                    act.wait_ge(z_mm, NT * n + t + 1)
                    nc.scalar.copy(z0[0:r, t, 352 * s:352 * s + 352], bank(4 + u)[0:r, 0:352]).then_inc(z_ev, 1)

            take_z(0, 0)
            take_z(1, 1)

            def take_pair(i, func):
                for s in range(2):
                    for t in range(NT):
                        r = rows_of(t)
                        u = (s * NT + t) % 2
                        act.wait_ge(z_mm, 2 * NT * i + 2 * NT + s * NT + t + 1)
                        act.wait_ge(z_stored[u], 16 * NT * i + 16 * ((s * NT + t) // 2) + 16)
                        A(zst[u][0:r, :], bank(4 + u)[0:r, :], func).then_inc(z_ev, 1)

            with act.Fori(0, 2) as i:
                take_pair(i, ACT.Gelu_apprx_tanh)
            with act.Fori(2, 4) as i:
                take_pair(i, ACT.Sigmoid)
            act.wait_ge(p_sq, 1)
            A(stat, stat, ACT.Sqrt, bias=eps).then_inc(p_rs, 1)
            for u in range(2):
                act.wait_ge(z_stored[u], 16 * (8 * NT // 2) + 16)
            stage_end(act, 1)

            got = 0
            for what, n in sched:
                if what == "Q":
                    t, r, s = n, rows_of(n), n % 2

                    def from0(dst, src):
                        nonlocal got
                        got += 1
                        act.wait_ge(b_mm[0], got)
                        nc.scalar.copy(dst, src).then_inc(b_ev[0], 1)

                    b0 = bank(0).rearrange("p (i n) -> p i n", i=4)
                    got += 1
                    act.wait_ge(b_mm[0], got)
                    nc.scalar.copy(kr_t[0:DR, t * P:t * P + r], b0[0:DR, 3, 0:r])
                    nc.scalar.copy(cq_t[:, :, 0:r], b0[:, 0:3, 0:r]).then_inc(b_ev[0], 1)
                    from0(qn_t[:, 0:4, 0:r], b0[:, :, 0:r])
                    from0(qr_n[0:r, :], bank(0)[0:r, :])
                    act.wait_ge(b_ev[0], got)
                    act.sem_inc(qrn_ready, 1)
                    for h in (2, 6):
                        from0(ql_t[s][:, h:h + 2, :, 0:r].rearrange("p h c n -> p (h c) n"), b0[:, :, 0:r])
                    from0(qr_t[s][0:DR, 4:8, 0:r], b0[0:DR, :, 0:r])
                elif what == "S":
                    t, h = units[n]
                    w = P * (t + 1)
                    act.wait_ge(s_nm, n + 1)
                    A(prob[n % 2][:, 0:w], bank(2 + 2 * (n % 2), 2)[:, 0:w], ACT.Exp, bias=negmax[:, n:n + 1], scale=SCALE,
                      accum_out=psumq[:, n:n + 1]).then_inc(s_exp, 1)
                elif what == "T":
                    t, h = units[n]
                    w = P * min(t + 1, 4)
                    act.wait_ge(t_mm[0], n + 1)
                    nc.scalar.copy(prob_t[n % 2][:, 0:w // P, :].rearrange("p j n -> p (j n)"), bank(6)[:, 0:w]).then_inc(t_ev[0], 1)
                elif what != "prep" and n % 2 == 0:
                    t, h = units[n]
                    got += 1
                    act.wait_ge(b_mm[0], got)
                    if what == "PV":
                        nc.scalar.copy(pv_t[0].rearrange("p c n -> p (c n)"), bank(0)[:, 0:2 * P]).then_inc(b_ev[0], 1)
                    else:
                        act.wait_ge(s_rinv, n + 1)
                        A(attn[:, t, DV * h:DV * h + DV], bank(0)[:, 0:DV], ACT.Copy, scale=rinv[:, n:n + 1]).then_inc(b_ev[0], 1)
            stage_end(act, 2)

            act.wait_ge(c_sub, 1)
            A(p_new[0:RS, :], s_new[0:RS, :], ACT.Exp, scale=SCALE).then_inc(n_act, 1)

            def turned(n, us):
                for u in us:
                    act.wait_ge(c_tr, NU * n + u + 1)
                    nc.scalar.copy(turned_at(u), bank(u % 5)).then_inc(kt_in[0], 1)

            act.wait_ge(n_dve, 3)
            turned(0, range(0, NU, 2))

            def batch(i, last_batch):
                for q in range(4):
                    n = 4 * i + q
                    more = q < 3 or not last_batch
                    if more:
                        turned(n + 1, (0,))
                    act.wait_ge(c_neg, n + 1)
                    A(alpha, m_now[:, q:q + 1], ACT.Exp, bias=neg_m, scale=SCALE)
                    A(p_exp, bank(5), ACT.Exp, bias=neg_m, scale=SCALE, accum_out=l_add).then_inc(c_p, 1)
                    if more:
                        turned(n + 1, (2, 4))
                    act.wait_ge(c_pt, n + 1)
                    nc.scalar.copy(p_t.rearrange("p k n -> p (k n)"), bank(6)).then_inc(c_ptc, 1)
                    if more:
                        turned(n + 1, (6, 8))

            with act.Fori(0, NB - 1) as i:
                batch(i, False)
            batch(NB - 1, True)
            act.wait_ge(c_sub, 2)
            A(w_all, w_dif, ACT.Exp, scale=SCALE).then_inc(n_act, 1)
            act.wait_ge(n_pe, 8)
            nc.scalar.copy(attn[0:RS, NTP, :], bank(0, 2)[0:RS, :]).then_inc(n_act, 1)
            stage_end(act, 3)

            def merge(n, s, r, i_in):
                act.wait_ge(z_in[s], 32 * i_in)
                A(junk5[0:r, :], zt[s][0:r, D:2 * D], ACT.Square, scale=D ** -0.5, accum_out=stat5[s][0:r, 0:1]).then_inc(v_sq, 1)
                act.wait_ge(v_sq, n + 1)
                A(stat5[s][0:r, 0:1], stat5[s][0:r, 0:1], ACT.Sqrt, bias=eps[0:r]).then_inc(v_rs, 1)
                act.wait_ge(mt_mm, n + 1)
                nc.scalar.copy(m_t[:, :, 0:r], bank(2, 2).rearrange("p (k n) -> p k n", k=KD)[:, :, 0:r]).then_inc(mt_ev, 1)
                act.wait_ge(x2_ok, n + 1)
                A(junk5[0:r, :], xr[s][0:r, :], ACT.Square, scale=D ** -0.5, accum_out=stat5[s][0:r, 2:3]).then_inc(o_sq, 1)
                act.wait_ge(o_sq, n + 1)
                A(stat5[s][0:r, 2:3], stat5[s][0:r, 2:3], ACT.Sqrt, bias=eps[0:r]).then_inc(o_rs, 1)
                act.wait_ge(ot_mm, n + 1)
                nc.scalar.copy(x2_t[:, :, 0:r], bank(2, 2).rearrange("p (k n) -> p k n", k=KD)[:, :, 0:r]).then_inc(ot_ev, 1)

            with act.Fori(0, 4) as i:
                for s in range(2):
                    merge(2 * i + s, s, P, i + 1)
            merge(8, 0, RS, 5)
            stage_end(act, 4)

            act.wait_ge(r_sub, 1)
            A(g_exp, g_sub, ACT.Exp)
            A(d_exp, d_sub, ACT.Exp).then_inc(r_exp, 1)

            def expert(n):
                act.wait_ge(e_xt, n + 1)
                nc.scalar.copy(xg_t[:, 0:4, :].rearrange("p k n -> p (k n)"), bank(0)).then_inc(e_xe, 1)
                act.wait_ge(e_g, n + 1)
                A(h_s, bank(2)[:, 0:DE], ACT.Silu).then_inc(e_si, 1)

            def expert_out(n, s, i_s):
                act.wait_ge(e_y[0], n + 1)
                act.wait_ge(yo_free[s], i_s)
                nc.scalar.copy(yo[s][:, 0:512], bank(5)).then_inc(e_ye[0], 1)

            with act.Fori(0, 16) as i:
                for s in range(4):
                    expert(4 * i + s)
                    expert_out(4 * i + s, s % 2, 2 * i + s // 2 + 1)
            total = act.value_load(ovf_id[0:1, NOVF:NOVF + 1], min_val=0, max_val=NOVF)
            with act.Fori(0, NOVF) as j:
                with act.If(total > j):
                    expert(NE + j)
                    expert_out(NE + j, 0, 33 + j)

            def last_norm(n, s, r):
                act.wait_ge(f_sum, n + 1)
                A(junk8[0:r, :], fin[s][0:r, :], ACT.Square, scale=D ** -0.5, accum_out=stat8[s][0:r, 0:1]).then_inc(f_sq, 1)
                act.wait_ge(f_sq, n + 1)
                A(stat8[s][0:r, 0:1], stat8[s][0:r, 0:1], ACT.Sqrt, bias=eps[0:r]).then_inc(f_rs, 1)

            with act.Fori(0, 4) as i:
                for s in range(2):
                    last_norm(2 * i + s, s, P)
            last_norm(8, 0, RS)

        @block.gpsimd
        def _(pool):
            G = nc.gpsimd
            step = Count(pool, pool_c)
            for u in range(2):
                pool.sem_inc(yo_free[u], 1)
                pool.sem_inc(xt_st[u], 16)
                pool.sem_inc(f_st[u], 16)

            G.memset(ws_ns[0:RS, :, :], 0.0).then_inc(ws_zero, 1)
            pool.wait_ge(tab_in, 16)
            pool.wait_ge(pt_in, 16 * PG)
            step(G.tensor_copy(page_idx, page_raw))
            G.tensor_scalar(page_int, page_idx, 8.0, const("p_mod"), ALU.mult, ALU.add).then_inc(idx_ready, 1)
            pool.wait_ge(ws_ready, 16 * (1 + NB))
            for g in range(KD):
                G.tensor_tensor(ws_n[:, g, :], ws_n[:, g, :], const("keep"), ALU.mult)
                last = G.tensor_tensor(ws_ns[0:RS, g, :], ws_ns[0:RS, g, :], const("keep_s")[0:RS, :], ALU.mult)
            last.then_inc(wsm_ready, 1)
            stage_end(pool, 1)

            for what, t in sched:
                r = rows_of(t) if what in ("prep", "Q") else 0
                if what == "prep":
                    c, sn = cos[0:r, t, :], sin[0:r, t, :]
                    x1, x2_ = z0[0:r, t, QL + KVL:QL + KVL + 32], z0[0:r, t, QL + KVL + 32:ZL]
                    G.tensor_tensor(kr_tmp[0:r, 0:32], x1, c, ALU.mult)
                    G.tensor_tensor(kr_tmp[0:r, 32:64], x2_, sn, ALU.mult)
                    G.tensor_tensor(kr_tmp[0:r, 64:96], x2_, c, ALU.mult)
                    step(G.tensor_tensor(kr_tmp[0:r, 96:128], x1, sn, ALU.mult))
                    G.tensor_tensor(kr_n[0:r, t, 0:32], kr_tmp[0:r, 0:32], kr_tmp[0:r, 32:64], ALU.subtract)
                    step(G.tensor_tensor(kr_n[0:r, t, 32:64], kr_tmp[0:r, 64:96], kr_tmp[0:r, 96:128], ALU.add))
                    pool.sem_inc(p_kr, 1)
                    if t == NTP:
                        pool.sem_inc(lat_ready, 1)
                elif what == "Q":
                    pool.wait_ge(qrn_ready, t + 1)
                    v = [x.rearrange("p (h f) -> p h f", h=H) for x in (qr_n, qr_r)]
                    x1, x2_ = v[0][0:r, :, 0:32], v[0][0:r, :, 32:64]
                    tmp = qr_tmp.rearrange("p (a h f) -> p a h f", a=4, h=H)
                    cb = cos[0:r, t, :].unsqueeze(1).broadcast_to([r, H, 32])
                    sb = sin[0:r, t, :].unsqueeze(1).broadcast_to([r, H, 32])
                    G.tensor_tensor(tmp[0:r, 0], x1, cb, ALU.mult)
                    G.tensor_tensor(tmp[0:r, 1], x2_, sb, ALU.mult)
                    G.tensor_tensor(tmp[0:r, 2], x2_, cb, ALU.mult)
                    step(G.tensor_tensor(tmp[0:r, 3], x1, sb, ALU.mult))
                    G.tensor_tensor(v[1][0:r, :, 0:32], tmp[0:r, 0], tmp[0:r, 1], ALU.subtract)
                    G.tensor_tensor(v[1][0:r, :, 32:64], tmp[0:r, 2], tmp[0:r, 3], ALU.add).then_inc(qrope_done, 1)
            stage_end(pool, 2)

            ckv_g = cache_ckv[0].rearrange("n (a r) c -> (n a) (r c)", r=PG)
            kr_g = cache_krope[0].rearrange("n (a r) c -> (n a) (r c)", r=PG)

            def gather(q, n, col):
                step_g = G.tensor_copy(idx_now[q], page_int[:, col].bitcast(U32))
                return step_g

            def fetch(q):
                off = bass.IndirectOffsetOnAxis(ap=idx_now[q], axis=0)
                pool.indirect_dma_start(ck[q].rearrange("p r c -> p (r c)"), None, ckv_g, off).then_inc(c_in[q], 16)
                pool.indirect_dma_start(kr[q].rearrange("p r c -> p (r c)"), None, kr_g, off).then_inc(c_in[q], 16)

            for q in range(4):
                gather(q, q, slice(q, q + 1)).then_inc(idx_step, 1)
                pool.wait_ge(idx_step, q + 1)
                fetch(q)
            with pool.Fori(0, NB - 1) as i:
                for q in range(4):
                    pool.wait_ge(c_pv, 4 * i + q + 1)
                    gather(q, None, bass.ds(4 * i + q + 4, 1)).then_inc(idx_step, 1)
                    pool.wait_ge(idx_step, 4 * i + q + 5)
                    pool.sem_inc(marks, 1)
                    fetch(q)
            stage_end(pool, 3)

            def merge(n, s, r, attn_rows, x2_rows, i_in):
                pool.wait_ge(z_in[s], 32 * i_in)
                G.tensor_tensor(zt[s][0:r, 2 * D:3 * D], zt[s][0:r, 2 * D:3 * D], attn_rows, ALU.mult).then_inc(at_ok, 1)
                pool.wait_ge(x2_ok, n + 1)
                G.tensor_copy(x2_rows, xr[s][0:r, :]).then_inc(x2_cp, 1)

            with pool.Fori(0, 4) as i:
                for s in range(2):
                    t = 2 * i + s
                    merge(t, s, P, attn.rearrange("p t n -> p (t n)")[:, bass.ds(2 * D * i + D * s, D)],
                          x2.rearrange("p t n -> p (t n)")[:, bass.ds(2 * D * i + D * s, D)], i + 1)
            merge(8, 0, RS, attn[0:RS, NTP, :], x2[0:RS, NTP, :], 5)
            stage_end(pool, 4)

            G.memset(fill.bitcast(I32), 1 << 29).then_inc(fill_ok, 1)
            pool.wait_ge(fill_in, 16)
            pool.wait_ge(r_pos, 1)
            ids_v = ids_sb.rearrange("p (n c) -> p n c", c=2)
            for n in range(2 * NT):
                pool.indirect_dma_start(slot_rows, bass.IndirectOffsetOnAxis(ap=pos_i[:, n:n + 1], axis=0),
                                        ids_v[:, n, :], None, bounds_check=NBLK * P - 1, oob_is_err=False).then_inc(scat_in, 16)
            pool.wait_ge(slots_ok, 1)
            for s in range(2):
                last = G.memset(xg[s], 0.0)
            last.then_inc(xg_zero, 1)
            pool.wait_ge(xg_zero, 1)
            for u in range(2):
                pool.wait_ge(xt_st[u], 16 * (6 - u))

            last_tok, last_slot = pool.to_reg(TOK - 1), pool.to_reg(2 * TOK - 1)

            def rows_in(s, n, k):
                G.tensor_copy(idx_row[s], slot_idx[:, n, 0:1] if isinstance(n, int) else slot_idx[:, bass.ds(n, 1), 0])
                G.tensor_copy(idx_tok[s], slot_idx[:, n, 1:2] if isinstance(n, int) else slot_idx[:, bass.ds(n, 1), 1]).then_inc(x_idx, 1)
                pool.wait_ge(x_idx, k + 1)
                pool.sem_inc(marks, 1)
                pool.indirect_dma_start(xg[s], None, xt_rows, bass.IndirectOffsetOnAxis(ap=idx_tok[s], axis=0),
                                        bounds_check=last_tok, oob_is_err=False).then_inc(e_x[s], 16)

            def rows_out(s, n):
                pool.wait_ge(e_ye[0], n + 2)
                pool.wait_ge(e_ye[1], n + 2)
                pool.sem_inc(marks, 1)
                pool.indirect_dma_start(y_rows, bass.IndirectOffsetOnAxis(ap=idx_row[s], axis=0), yo[s], None,
                                        bounds_check=last_slot, oob_is_err=False).then_inc(e_sc[s], 16)

            rows_in(0, 0, 0)
            rows_in(1, 1, 1)
            with pool.Fori(0, 31) as i:
                for s in range(2):
                    rows_out(s, 2 * i + s)
                    pool.wait_ge(e_sc[s], 16 * i + 16)
                    pool.sem_inc(yo_free[s], 1)
                    rows_in(s, 2 * i + s + 2, 2 * i + s + 2)
            rows_out(0, 62)
            rows_out(1, 63)
            for s in range(2):
                pool.wait_ge(e_sc[s], 16 * 32)
                pool.sem_inc(yo_free[s], 1)
            total = pool.value_load(ovf_id[0:1, NOVF:NOVF + 1], min_val=0, max_val=NOVF)
            with pool.Fori(0, NOVF) as j:
                with pool.If(total > j):
                    rows_in(0, NE + j, NE + j)
                    rows_out(0, NE + j)
                    pool.wait_ge(e_sc[0], 16 * (33 + j))
                    pool.sem_inc(yo_free[0], 1)
            pool.sem_inc(moe_end, 1)


        @block.vector
        def _(dve):
            V = nc.vector
            copy, tt, ts, stt, red = V.tensor_copy, V.tensor_tensor, V.tensor_scalar, V.scalar_tensor_tensor, V.tensor_reduce
            step = Count(dve, dve_c)
            dve.sem_inc(xt_ev[1], 2)
            dve.sem_inc(c_acc, 1)
            dve.sem_inc(sgu_ok, 1)
            dve.sem_inc(lg_ok, 1)
            dve.sem_inc(e_ye[1], 1)
            V.memset(logits, 0.0)
            step(V.memset(small, 0.0))
            dve.sem_inc(small_zero, 1)
            dve.wait_ge(small_in, 16 * (9 + NB))

            def norm_x(n, s, r, dst):
                dve.wait_ge(x_rstd, n + 1)
                V.reciprocal(small[0:r, 4 + s:5 + s], small[0:r, 2 + s:3 + s]).then_inc(x_inv, 1)
                dve.wait_ge(x_inv, n + 1)
                stt(xn[s][0:r, :], x_in[s][0:r, :], small[0:r, 4 + s:5 + s], g1[0:r, :], ALU.mult, ALU.mult).then_inc(xn_ready, 1)
                dve.wait_ge(xt_mm, n + 1)
                ts(dst, bank(2 * s + 1).rearrange("p (k n) -> p k n", k=4)[:, :, 0:r], 1.0, None, ALU.mult).then_inc(xt_ev[1], 1)

            with dve.Fori(0, 4) as i:
                for s in range(2):
                    norm_x(2 * i + s, s, P, xn_t[:, 4:8, bass.ds(2 * P * i + P * s, P)])
            norm_x(8, 0, RS, xn_t[:, 4:8, SEQ:TOK])
            for t in range(NT):
                r = rows_of(t)
                dve.wait_ge(z_ev, NT + t + 1)
                for c, (a0, w) in enumerate(((0, QL), (QL, KVL))):
                    step(stt(junk2[0:r, c * QL:c * QL + w], z0[0:r, t, a0:a0 + w], 1.0 / w, z0[0:r, t, a0:a0 + w], ALU.mult,
                             ALU.mult, accum_out=stat[0:r, t, c:c + 1]))
            dve.sem_inc(p_sq, 1)
            dve.wait_ge(p_rs, 1)
            step(V.reciprocal(rstd, stat))
            stage_end(dve, 1)

            got = 0
            for what, n in sched:
                if what == "prep":
                    t, r = n, rows_of(n)
                    if t >= 1:
                        dve.wait_ge(b_mm[0], cq_read)
                    stt(cq[0:r, :], z0[0:r, t, 0:QL], rstd[0:r, t, 0:1], gq[0:r, :], ALU.mult, ALU.mult)
                    last = stt(ckv_n[0:r, t, :], z0[0:r, t, QL:QL + KVL], rstd[0:r, t, 1:2], gkv[0:r, :], ALU.mult, ALU.mult)
                    last.then_inc(p_cn, 1)
                    if t == NTP:
                        dve.wait_ge(p_cn, NT)
                        dve.sem_inc(lat_ready, 1)
                elif what == "Q":
                    t, r, s = n, rows_of(n), n % 2
                    b1 = bank(1).rearrange("p (i n) -> p i n", i=4)

                    def from1(dst, src):
                        nonlocal got
                        got += 1
                        dve.wait_ge(b_mm[1], got)
                        copy(dst, src).then_inc(b_ev[1], 1)

                    from1(ckv_t[:, :, t * P:t * P + r], b1[:, 0:2, 0:r])
                    from1(qn_t[:, 4:8, 0:r], b1[:, :, 0:r])
                    for h in (0, 4):
                        from1(ql_t[s][:, h:h + 2, :, 0:r].rearrange("p h c n -> p (h c) n"), b1[:, :, 0:r])
                    from1(qr_t[s][0:DR, 0:4, 0:r], b1[0:DR, :, 0:r])
                    cq_read = q_units(sched, t)
                elif what == "S":
                    t, h = units[n]
                    w = P * (t + 1)
                    dve.wait_ge(s_mm, n + 1)
                    step(red(rinv[:, n:n + 1], bank(2 + 2 * (n % 2), 2)[:, 0:w], AX.X, ALU.max))
                    ts(negmax[:, n:n + 1], rinv[:, n:n + 1], -SCALE, None, ALU.mult).then_inc(s_nm, 1)
                    dve.wait_ge(s_exp, n + 1)
                    V.reciprocal(rinv[:, n:n + 1], psumq[:, n:n + 1]).then_inc(s_rinv, 1)
                elif what == "T":
                    t, h = units[n]
                    if t >= 4:
                        dve.wait_ge(t_mm[1], n - 4 * H + 1)
                        copy(prob_t[n % 2][:, 4:t + 1, :].rearrange("p j n -> p (j n)"), bank(7)[:, 0:P * (t - 3)]).then_inc(t_ev[1], 1)
                elif n % 2 == 1:
                    t, h = units[n]
                    got += 1
                    dve.wait_ge(b_mm[1], got)
                    if what == "PV":
                        copy(pv_t[1].rearrange("p c n -> p (c n)"), bank(1)[:, 0:2 * P]).then_inc(b_ev[1], 1)
                    else:
                        dve.wait_ge(s_rinv, n + 1)
                        ts(attn[:, t, DV * h:DV * h + DV], bank(1)[:, 0:DV], rinv[:, n:n + 1], None, ALU.mult).then_inc(b_ev[1], 1)
            dve.wait_ge(b_ev[0], bank0_units)
            for c in range(2):
                copy(qs[:, c, :].rearrange("p (b h t) -> p b h t", b=NB, h=H),
                     ql_t[0][:, :, c, 0:RS].rearrange("p h (b t) -> p b h t", b=NB))
            copy(qsr[0:DR, :].rearrange("p (b h t) -> p b h t", b=NB, h=H),
                 qr_t[0][0:DR, :, 0:RS].rearrange("p h (b t) -> p b h t", b=NB))
            copy(qsr[DR:P, :].rearrange("p (b h t) -> p b h t", b=NB, h=H),
                 qr_t[0][0:DR, :, 0:RS].rearrange("p h (b t) -> p b h t", b=NB)).then_inc(n_dve, 1)
            stage_end(dve, 2)

            dve.wait_ge(n_dve, 1)
            for c in range(2):
                copy(q_now[:, c, :], qs[:, c, 0:RS])
            copy(qr_now, qsr[:, 0:RS]).then_inc(q_ready, 1)
            dve.wait_ge(lat_stored, 64)
            V.memset(acc, 0.0)
            V.memset(l_all, 0.0)
            step(V.memset(m_all, NEG))
            dve.wait_ge(n_pe, 1)
            keys = s_new[0:RS, :].rearrange("p (b k) -> p b k", b=NB)
            step(tt(s_new[0:RS, :], bank(5)[0:RS, 0:NB * RS], const("mask_new")[0:RS, :], ALU.add))
            step(red(m_all[0:RS, :], keys, AX.X, ALU.max))
            tt(keys, keys, m_all[0:RS, :].unsqueeze(2).broadcast_to([RS, NB, RS]), ALU.subtract).then_inc(c_sub, 1)
            copy(m_now[:, 0:1], m_all[:, 0:1])
            dve.wait_ge(n_act, 1)
            red(l_all[0:RS, :], p_new[0:RS, :].rearrange("p (b k) -> p b k", b=NB), AX.X, ALU.add)
            dve.wait_ge(n_pe, 2)
            copy(p_new_t[0:RS, :], bank(6)[0:RS, 0:NB * RS]).then_inc(n_dve, 1)
            dve.wait_ge(n_pe, 3)
            step(copy(acc[0:RS, :, :].rearrange("p b c -> p (b c)"), bank(0, 4)[0:RS, :]))
            dve.sem_inc(n_dve, 1)

            PER4 = 18
            chain4 = step.n

            def turned(n, us):
                for u in us:
                    dve.wait_ge(c_tr, NU * n + u + 1)
                    copy(turned_at(u), bank(u % 5)).then_inc(kt_in[1], 1)

            turned(0, range(1, NU, 2))
            acc_flat = acc.rearrange("p b c -> p (b c)")

            def batch(i, last_batch):
                ch = Count(dve, dve_c, chain4 + PER4 * i)
                acc_b, l_b, m_b = acc_flat[:, bass.ds(KVL * i, KVL)], l_all[:, bass.ds(i, 1)], m_all[:, bass.ds(i, 1)]
                for q in range(4):
                    n = 4 * i + q
                    more = q < 3 or not last_batch
                    dve.wait_ge(c_s, n + 1)
                    ch(red(m_part, bank(5), AX.X, ALU.max))
                    ch(tt(m_now[:, q + 1:q + 2], m_now[:, q:q + 1], m_part, ALU.max))
                    ts(neg_m, m_now[:, q + 1:q + 2], -SCALE, None, ALU.mult).then_inc(c_neg, 1)
                    if q == 3 and more:
                        for c in range(2):
                            ts(q_now[:, c, :], qs[:, c, bass.ds(RS * i + RS, RS)], 1.0, None, ALU.mult)
                        ts(qr_now, qsr[:, bass.ds(RS * i + RS, RS)], 1.0, None, ALU.mult).then_inc(q_ready, 1)
                    if more:
                        turned(n + 1, range(1, NU, 2))
                    dve.wait_ge(c_p, n + 1)
                    ch(stt(l_b, l_b, alpha, l_add, ALU.mult, ALU.add))
                    dve.wait_ge(c_pv, n + 1)
                    ch(stt(acc_b, acc_b, alpha, bank(7)[:, 0:KVL], ALU.mult, ALU.add))
                    dve.sem_inc(c_acc, 1)
                ch(ts(m_b, m_now[:, 4:5], 1.0, None, ALU.mult))
                if last_batch:
                    ch.n += 1
                else:
                    ch(ts(m_now[:, 0:1], m_all[:, bass.ds(i + 1, 1)], 1.0, None, ALU.mult))
                assert ch.n == PER4, ch.n

            with dve.Fori(0, NB - 1) as i:
                batch(i, False)
            batch(NB - 1, True)
            step.n += PER4 * NB - 1
            dve.sem_inc(n_dve, 1)
            dve.wait_ge(n_pe, 4)
            step(red(m8[0:NB, :], bank(6)[0:NB, 0:P].rearrange("p (j q) -> p q j", j=4), AX.X, ALU.max))
            copy(m8b[0:NB, :].rearrange("p (j q) -> p j q", j=4),
                 m8[0:NB, :].unsqueeze(1).broadcast_to([NB, 4, RS])).then_inc(n_dve, 1)
            dve.wait_ge(n_pe, 5)
            tt(w_dif, m_all, bank(6)[:, P:P + NB], ALU.subtract).then_inc(c_sub, 1)
            dve.wait_ge(n_act, 2)
            tt(l_w, l_all, w_all, ALU.mult).then_inc(n_dve, 1)
            dve.wait_ge(n_pe, 6)
            step(V.reciprocal(l_inv, bank(6)[:, 2 * P:2 * P + NB]))
            step(tt(l_inv, l_inv, w_all, ALU.mult))
            for b in range(NB):
                last = ts(acc[:, b, :], acc[:, b, :], l_inv[:, b:b + 1], None, ALU.mult)
            last.then_inc(n_dve, 1)
            dve.wait_ge(n_pe, 7)
            for c in range(2):
                last = copy(o_lat[:, c, :].rearrange("p (h b t) -> p b h t", h=H, b=NB),
                            bank(7)[:, NB * RS * c:NB * RS * c + NB * RS].rearrange("p (b h t) -> p b h t", h=H, b=NB))
            last.then_inc(n_dve, 1)
            stage_end(dve, 3)

            chain5 = step.n
            PER5 = 2

            def merge(n, s, r, bs, lg_rows, k):
                ch = Count(dve, dve_c, chain5 + PER5 * n)
                u, v, ga, gb = (zt[s][0:r, D * x:D * x + D] for x in range(4))
                dve.wait_ge(v_rs, n + 1)
                V.reciprocal(stat5[s][0:r, 1:2], stat5[s][0:r, 0:1]).then_inc(v_inv, 1)
                dve.wait_ge(v_inv, n + 1)
                stt(v, v, stat5[s][0:r, 1:2], gv[0:r, :], ALU.mult, ALU.mult).then_inc(v_n, 1)
                dve.wait_ge(mix_mm, n + 1)
                for g in range(KD):
                    last = stt(u[:, P * g:P * g + P], bank(0, 2)[0:r, P * g:P * g + P], bs[0:r, g:g + 1],
                               u[:, P * g:P * g + P], ALU.add, ALU.mult)
                last.then_inc(sgu_ok, 1)
                dve.wait_ge(sgu_ok, n + 2)
                ch(tt(u, u, gb, ALU.mult))
                dve.wait_ge(at_ok, n + 1)
                tt(u, u, ga, ALU.add).then_inc(mrg_ok, 1)
                dve.wait_ge(y_mm, n + 1)
                tt(xr[s][0:r, :], xr[s][0:r, :], bank(4, 2)[0:r, :], ALU.add).then_inc(x2_ok, 1)
                dve.wait_ge(o_rs, n + 1)
                V.reciprocal(stat5[s][0:r, 3:4], stat5[s][0:r, 2:3]).then_inc(o_inv, 1)
                dve.wait_ge(o_inv, n + 1)
                dve.wait_ge(xt_st[s], 16 * k + 16)
                ch(stt(xo[s][0:r, :], xr[s][0:r, :], stat5[s][0:r, 3:4], g2[0:r, :], ALU.mult, ALU.mult))
                dve.sem_inc(o_n, 1)
                dve.wait_ge(lg_mm, n + 1)
                tt(lg_rows, bank(6)[0:r, 0:72], rbias[0:r, :], ALU.add).then_inc(lg_ok, 1)
                assert ch.n == PER5

            dve.wait_ge(late_in, 48)
            lg_flat = logits.rearrange("p t n -> p (t n)")
            with dve.Fori(0, 4) as i:
                for s in range(2):
                    merge(2 * i + s, s, P, bs_t, lg_flat[:, bass.ds(144 * i + 72 * s, 72)], i)
            merge(8, 0, RS, bs_ts, logits[0:RS, NTP, :], 4)
            step.n += PER5 * NT
            for u in range(2):
                dve.wait_ge(xt_st[u], 16 * (6 - u))
            dve.wait_ge(v_st, 16)
            stage_end(dve, 4)

            def wide(x, n):
                return x.unsqueeze(len(x.shape)).broadcast_to(list(x.shape) + [n])

            for t in range(NT):
                last = V.max(g_top[:, t, :], logits[:, t, 0:NG])
            step(last)
            for t in range(NT):
                last = V.max_index(g_ind[:, t, :], g_top[:, t, :], logits[:, t, 0:NG])
            step(last)
            step(copy(g_f, g_ind[:, :, 0]))
            iota = const("iota")
            step(tt(pen, iota[:, 0:NG].unsqueeze(1).broadcast_to([P, NT, NG]), wide(g_f, NG), ALU.is_equal))
            step(ts(pen, pen, -NEG, NEG, ALU.mult, ALU.add))
            step(tt(e_log.rearrange("p t (g e) -> p t g e", g=NG), logits[:, :, NG:].rearrange("p t (g e) -> p t g e", g=NG),
                    wide(pen, 8), ALU.add))
            for t in range(NT):
                last = V.max(e_top[:, t, :], e_log[:, t, :])
            step(last)
            for t in range(NT):
                last = V.max_index(e_ind[:, t, :], e_top[:, t, :], e_log[:, t, :])
            tt(g_sub, logits[:, :, 0:NG], g_top[:, :, 0:1].broadcast_to([P, NT, NG]), ALU.subtract)
            step(tt(d_sub, e_top[:, :, 1], e_top[:, :, 0], ALU.subtract))
            dve.sem_inc(r_sub, 1)
            step(copy(e_f, e_ind[:, :, 0:2]))
            step(tt(e_f, e_f, wide(const("pad"), 2), ALU.add))
            step(tt(hot.rearrange("p t c n -> p (t c) n"), iota.unsqueeze(1).broadcast_to([P, 2 * NT, NE]),
                    wide(e_f.rearrange("p t c -> p (t c)"), NE), ALU.is_equal))
            step(tt(mask, hot[:, :, 0, :], hot[:, :, 1, :], ALU.add))
            step(V.memset(cum[:, 0, :], 0.0))
            for t in range(1, NT):
                step(tt(cum[:, t, :], cum[:, t - 1, :], mask[:, t - 1, :], ALU.add))
            step(tt(rank[:, 0, :], cum[:, NT - 1, :], mask[:, NT - 1, :], ALU.add))
            dve.sem_inc(r_dve, 1)
            dve.wait_ge(r_exp, 1)
            step(red(g_den, g_exp, AX.X, ALU.add))
            step(ts(d_sub, d_exp, 1.0, None, ALU.add))
            step(tt(g_den, g_den, d_sub, ALU.mult))
            step(V.reciprocal(gates[:, :, 0], g_den))
            step(tt(gates[:, :, 1], gates[:, :, 0], d_exp, ALU.mult))
            dve.wait_ge(r_pe, 1)
            step(copy(cnt[0], bank(1)[:, NE:2 * NE]))
            prod8 = prod.rearrange("p t c n -> p (t c n)")
            big = prod8[:, 0:NE * CAP_STEPS].rearrange("p (e s) -> p e s", s=CAP_STEPS)
            step(tt(big, wide(cnt[0], CAP_STEPS), const("steps").unsqueeze(1).broadcast_to([P, NE, CAP_STEPS]), ALU.is_gt))
            step(red(cnt[1], big, AX.X, ALU.add))
            step(V.tensor_tensor_scan(cnt[2], ones[:, 0:NE], cnt[1], 0.0, ALU.mult, ALU.add))
            step(tt(cnt[3], cnt[2], cnt[1], ALU.subtract))
            big = prod8[:, 0:NE * NOVF].rearrange("p (j e) -> p j e", j=NOVF)
            step(tt(big, cnt[2].unsqueeze(1).broadcast_to([P, NOVF, NE]), wide(const("blocks"), NE), ALU.is_le))
            step(red(cnt[0][:, 0:NOVF], big, AX.X, ALU.add))
            ts(ovf_id[:, 0:NOVF], cnt[0][:, 0:NOVF], NE - 1.0, None, ALU.min)
            copy(ovf_id[:, NOVF:NOVF + 1], cnt[2][:, NE - 1:NE])
            step(copy(rank[:, 0:8, :].rearrange("p t n -> p (t n)"), bank(0)))
            step(copy(rank[:, 8, :], bank(1)[:, 0:NE]))
            rk, xs_, q_, rem, b_, tmp_ = (x.rearrange("p t c -> p (t c)") for x in n_rt)
            ef = e_f.rearrange("p t c -> p (t c)")
            for c in range(2):
                last = tt(prod[:, :, c, :], hot[:, :, c, :], rank, ALU.mult)
            step(last)
            step(red(rk, prod.rearrange("p t c n -> p (t c) n"), AX.X, ALU.add))
            step(tt(prod.rearrange("p t c n -> p (t c) n"), hot.rearrange("p t c n -> p (t c) n"),
                    cnt[3].unsqueeze(1).broadcast_to([P, 2 * NT, NE]), ALU.mult))
            step(red(xs_, prod.rearrange("p t c n -> p (t c) n"), AX.X, ALU.add))
            big = prod8[:, 0:2 * NT * CAP_STEPS].rearrange("p (e s) -> p e s", s=CAP_STEPS)
            step(tt(big, wide(rk, CAP_STEPS), const("steps").unsqueeze(1).broadcast_to([P, 2 * NT, CAP_STEPS]), ALU.is_ge))
            step(red(q_, big, AX.X, ALU.add))
            step(stt(rem, q_, -float(P), rk, ALU.mult, ALU.add))
            step(stt(b_, q_, NE - 1.0, xs_, ALU.add, ALU.add))
            step(tt(b_, b_, ef, ALU.subtract))
            step(ts(tmp_, q_, 1.0, None, ALU.min))
            step(tt(b_, b_, tmp_, ALU.mult))
            step(tt(b_, b_, ef, ALU.add))
            step(stt(pos_i, b_, float(P), rem, ALU.mult, ALU.add))
            dve.sem_inc(r_pos, 1)
            dve.wait_ge(slots_in, 16)
            step(copy(slot_f[0:NBLK, :], fill[0:NBLK, :].bitcast(I32)))
            dve.sem_inc(r_dve, 1)
            dve.wait_ge(r_pe, 2)
            for c in range(2):
                last = copy(slot_idx[:, :, c], bank(2)[:, P * c:P * c + NBLK])
            step(last)
            dve.sem_inc(slots_ok, 1)

            def expert(n):
                dve.wait_ge(e_xt, n + 1)
                copy(xg_t[:, 4:8, :].rearrange("p k n -> p (k n)"), bank(1)).then_inc(e_xe, 1)
                dve.wait_ge(e_u, n + 1)
                dve.wait_ge(e_si, n + 1)
                tt(h_n, h_s, bank(3)[:, 0:DE], ALU.mult).then_inc(e_h, 1)
                dve.wait_ge(e_ht, n + 1)
                copy(h_t.rearrange("p f n -> p (f n)"), bank(4)[:, 0:DE]).then_inc(e_he, 1)

            def expert_out(n, s, i_s):
                dve.wait_ge(e_y[1], n + 1)
                dve.wait_ge(yo_free[s], i_s)
                copy(yo[s][:, 512:D], bank(6)).then_inc(e_ye[1], 1)

            with dve.Fori(0, 16) as i:
                for s in range(4):
                    expert(4 * i + s)
                    expert_out(4 * i + s, s % 2, 2 * i + s // 2 + 1)
            total = dve.value_load(ovf_id[0:1, NOVF:NOVF + 1], min_val=0, max_val=NOVF)
            with dve.Fori(0, NOVF) as j:
                with dve.If(total > j):
                    expert(NE + j)
                    expert_out(NE + j, 0, 33 + j)

            for t in range(NT):
                s, r = t % 2, rows_of(t)
                dve.wait_ge(f_in[s], 16 * (t // 2 + 1))
                dve.wait_ge(f_st[s], 16 * (t // 2) + 16)
                step(stt(fin[s][0:r, :], y2[s][0:r, 0:D], gates[0:r, t, 0:1], x2[0:r, t, :], ALU.mult, ALU.add))
                stt(fin[s][0:r, :], y2[s][0:r, D:2 * D], gates[0:r, t, 1:2], fin[s][0:r, :], ALU.mult, ALU.add).then_inc(f_sum, 1)
                dve.wait_ge(f_rs, t + 1)
                V.reciprocal(stat8[s][0:r, 1:2], stat8[s][0:r, 0:1]).then_inc(f_inv, 1)
                dve.wait_ge(f_inv, t + 1)
                stt(fin[s][0:r, :], fin[s][0:r, :], stat8[s][0:r, 1:2], gf[0:r, :], ALU.mult, ALU.mult).then_inc(f_ok, 1)


_INS = ["x_prompt", "x_sample", "cache_ckv", "cache_krope", "page_table", "norm1_g", "w_in", "q_norm_g", "kv_norm_g",
        "w_uq", "w_qr", "w_uk", "w_uv", "sgu_norm_g", "w_s", "b_s", "w_o", "norm2_g", "w_rg", "b_rg", "w_re", "b_re",
        "w_gate", "w_up", "w_down", "norm_f_g"]
_OUTS = [(1, SEQ, D), (NB, TS, D), (1, 1, NTP, P, KVL), (1, 1, NTP, P, DR), (1, NB, TS, KVL), (1, NB, TS, DR),
         (1, NB, TS, D)]
_SCRATCH = [("z_act", [TOK, 4 * D], F32), ("xt_rows", [TOK, D], F32), ("slot_rows", [NBLK * P, 2], I32),
            ("y_rows", [2 * TOK, D], F32)]


def kernel(**inputs):
    import numpy as _np
    import concourse.bacc as _bacc
    from concourse import mybir as _mybir
    from concourse.bass_utils import run_bass_kernel_spmd as _run

    nc = _bacc.Bacc("TRN2", target_bir_lowering=False, num_devices=1)
    arrays, args = {}, []
    tables, ids = const_tables()
    for name, a in [(n, _np.ascontiguousarray(inputs[n])) for n in _INS] + [("tables", tables), ("ids", ids)]:
        arrays[f"in_{name}_dram"] = a
        args.append(nc.dram_tensor(f"in_{name}_dram", a.shape, _mybir.dt.from_np(a.dtype), kind="ExternalInput").ap())
    for i, shape in enumerate(_OUTS):
        args.append(nc.dram_tensor(f"out_{i}_dram", shape, _mybir.dt.float32, kind="ExternalOutput").ap())
    for name, shape, dt in _SCRATCH:
        args.append(nc.dram_tensor(name, shape, dt, kind="Internal").ap())
    build(nc, *args)
    r = _run(nc, [arrays], core_ids=[0])
    return tuple(r.results[0][f"out_{i}_dram"] for i in range(len(_OUTS)))
```

```python
from contextlib import ExitStack

import numpy as np

import concourse.bass as bass
from concourse import mybir

F32 = mybir.dt.float32
I32 = mybir.dt.int32
U32 = mybir.dt.uint32
ALU = mybir.AluOpType
ACT = mybir.ActivationFunctionType
AX = mybir.AxisListType

P = 128
D = 1024
KD = D // P
SEQ = 1024
NTP = SEQ // P
NB, TS = 8, 4
RS = NB * TS
NT = NTP + 1
TOK = SEQ + RS
H = 8
DN = 128
DR = 64
DV = 128
QL, KVL = 384, 256
ZL = QL + KVL + DR
NG = 8
NE = 64
DE = 256
EPS = 1e-6
SCALE = float(np.float32((DN + DR) ** -0.5))
NEG = -1e30
PAST = 8192
PAGES = PAST // P
PG = 16
NCH = NB * PAGES // PG
NOVF = 2 * TOK // P
NBLK = NE + NOVF
PAD = 1e6
CAP_STEPS = (TOK + P - 1) // P - 1
QB = 2 * H * P


def rows_of(t):
    return P if t < NTP else RS


def const_layout():
    at, off = {}, 0
    for name, n in (("ident", P), ("negmask", P), ("before", P), ("ones", P), ("keep", P), ("keep_s", RS),
                    ("cos", NT * 32), ("sin", NT * 32), ("iota", NE), ("steps", CAP_STEPS),
                    ("pad", NT), ("blocks", NOVF), ("mask_new", NB * RS), ("same_q", P), ("p_mod", 1), ("eps", 1)):
        at[name] = (off, n)
        off += n
    return at, off


def const_tables():
    at, n = const_layout()
    k = np.zeros((P, n), np.float32)

    def put(name, a):
        o, w = at[name]
        k[:a.shape[0], o:o + w] = a.reshape(a.shape[0], w)

    i = np.arange(P)
    put("ident", np.eye(P, dtype=np.float32))
    put("negmask", np.where(i[None, :] <= i[:, None], 0, NEG).astype(np.float32))
    put("before", (i[:, None] < i[None, :]).astype(np.float32))
    put("ones", np.ones((P, P), np.float32))
    put("keep", (i[None, :] <= i[:, None]).astype(np.float32))
    r = np.arange(RS)
    same = r[None, :] // TS == r[:, None] // TS
    put("keep_s", (same & (r[None, :] <= r[:, None])).astype(np.float32))
    half = DR // 2
    freq = (10000.0 ** (-np.arange(half) / half)).astype(np.float32)
    pos = np.zeros((P, NT), np.float32)
    for t in range(NTP):
        pos[:, t] = t * P + i
    pos[:RS, NTP] = PAST + r % TS
    ang = (pos[:, :, None] * freq[None, None, :]).astype(np.float64)
    put("cos", np.cos(ang).astype(np.float32))
    put("sin", np.sin(ang).astype(np.float32))
    put("iota", np.tile(np.arange(NE, dtype=np.float32), (P, 1)))
    put("steps", np.tile(P * np.arange(1, CAP_STEPS + 1, dtype=np.float32), (P, 1)))
    pad = np.zeros((P, NT), np.float32)
    pad[RS:, NTP] = PAD + i[RS:]
    put("pad", pad)
    put("blocks", np.tile(np.arange(NOVF, dtype=np.float32), (P, 1)))
    col = np.arange(NB * RS)
    cb, ck_ = col // RS, col % RS
    ok = (ck_ // TS == cb)[None, :] & (ck_[None, :] % TS <= r[:, None] % TS)
    put("mask_new", np.where(ok, 0, NEG).astype(np.float32))
    put("same_q", (i[:, None] % RS == i[None, :] % RS).astype(np.float32))
    put("p_mod", (i % 8).astype(np.float32)[:, None])
    put("eps", np.full((P, 1), EPS, np.float32))
    ids = np.zeros((P, NT, 2, 2), np.int32)
    for t in range(NT):
        for c in range(2):
            ids[:, t, c, 0] = (t * P + i) * 2 + c
            ids[:, t, c, 1] = t * P + i
    return k, ids.reshape(P, NT * 4)


def q_units(sched, tile):
    n = 0
    for what, k in sched:
        if what == "Q" and k == tile:
            return n + 1
        n += 6 if what == "Q" else int(what in ("PV", "UV") and k % 2 == 0)


class Count:

    def __init__(self, eng, sem, base=0):
        self.eng, self.sem, self.base, self.n = eng, sem, base, 0

    def __call__(self, ins):
        self.n += 1
        ins.then_inc(self.sem, 1)
        self.eng.wait_ge(self.sem, self.base + self.n)


def attention_schedule():
    units = [(t, h) for t in range(NTP) for h in range(H)]
    todo = [("prep", 0), ("Q", 0), ("S", 0)]
    for n, (t, h) in enumerate(units):
        if n + 1 < len(units):
            if h == 1:
                todo.append(("prep", t + 1))
            if h == 3:
                todo.append(("Q", t + 1))
            todo.append(("S", n + 1))
        todo.append(("T", n))
        if t == NTP - 1 and h == 1:
            todo.append(("prep", NTP))
        if t == NTP - 1 and h == 3:
            todo.append(("Q", NTP))
        if n >= 1:
            todo.append(("PV", n - 1))
        if n >= 2:
            todo.append(("UV", n - 2))
    last = len(units) - 1
    todo += [("PV", last), ("UV", last - 1), ("UV", last)]
    out = []
    for x in todo:
        if x not in out:
            out.append(x)
    return units, out


def build(nc, x_prompt, x_sample, cache_ckv, cache_krope, page_table, norm1_g, w_in, q_norm_g, kv_norm_g,
          w_uq, w_qr, w_uk, w_uv, sgu_norm_g, w_s, b_s, w_o, norm2_g, w_rg, b_rg, w_re, b_re,
          w_gate, w_up, w_down, norm_f_g, tables, ids,
          y_prompt, y_sample, ckv_prompt, kr_prompt, ckv_sample, kr_sample, v_sample,
          z_act, xt_rows, slot_rows, y_rows):
    with ExitStack() as ctx:
        def sem(name):
            return ctx.enter_context(nc.semaphore(name))

        SIZE = 53200
        arena = ctx.enter_context(nc.sbuf_tensor("arena", [P, SIZE], F32))
        psum = ctx.enter_context(nc.psum_tensor("psum", [P, 8 * 512], F32))
        top = [0]
        end = [SIZE]

        def take(n, where=None, dt=F32):
            where = where or top
            v = arena[:, where[0]:where[0] + n]
            where[0] += n
            assert where[0] <= end[0], (where, n)
            return v

        def bank(b, n=1):
            return psum[:, 512 * b:512 * (b + n)]

        at, n_const = const_layout()
        K = take(n_const)

        def const(name):
            o, w = at[name]
            return K[:, o:o + w]

        ident, ones, eps = const("ident"), const("ones"), const("eps")
        cos, sin = (const(x).rearrange("p (t f) -> p t f", t=NT) for x in ("cos", "sin"))
        ids_sb = take(NT * 4).bitcast(I32)
        gains_base = top[0]
        g1, g2, gf, gv = take(D), take(D), take(D), take(D)
        gq, gkv = take(QL), take(KVL)
        rbias = take(NG + NE)
        w_router = take(KD * (NG + NE)).rearrange("p (k n) -> p k n", k=KD)
        ws_t = take(KD * P).rearrange("p (g i) -> p g i", g=KD)
        ws_ts = take(KD * RS).rearrange("p (g i) -> p g i", g=KD)
        bs_t, bs_ts = take(KD), take(KD)
        logits = take(NT * 72).rearrange("p (t n) -> p t n", t=NT)
        small = take(64)
        stat = small[:, 8:8 + 2 * NT].rearrange("p (t n) -> p t n", t=NT)
        rstd = small[:, 30:30 + 2 * NT].rearrange("p (t n) -> p t n", t=NT)
        page_idx = take(NCH)
        page_int = take(NCH).bitcast(I32)
        page_raw = take(NCH).bitcast(I32)
        x2_at = [SIZE - NT * D]
        x2 = arena[:, x2_at[0]:SIZE].rearrange("p (t n) -> p t n", t=NT)

        attn_base = top[0]
        attn = take(NT * D).rearrange("p (t n) -> p t n", t=NT)
        kv_base = top[0]
        ckv_n = take(NT * KVL).rearrange("p (t n) -> p t n", t=NT)
        kr_n = take(NT * DR).rearrange("p (t n) -> p t n", t=NT)
        ckv_t = take(2 * TOK).rearrange("p (c n) -> p c n", c=2)
        kr_t = take(TOK)
        w_uv_sb = take(2 * H * DV).rearrange("p (c n) -> p c n", c=2)
        qs = take(2 * NB * H * TS).rearrange("p (c n) -> p c n", c=2)
        qsr = take(NB * H * TS)
        z0_base = top[0]
        z0 = take(NT * ZL).rearrange("p (t n) -> p t n", t=NT)
        w_uq_sb = take(3 * H * DN).rearrange("p (r n) -> p r n", r=3)
        w_qr_sb = take(3 * H * DR).rearrange("p (r n) -> p r n", r=3)
        w_uk_t = take(H * KVL).rearrange("p (h c) -> p h c", h=H)
        o_base = top[0]

        o, kv = [o_base], [kv_base]
        xn_t = take(KD * TOK, o).rearrange("p (k n) -> p k n", k=KD)
        w_blk = [take(KD * 512, x).rearrange("p (k n) -> p k n", k=KD) for x in (o, kv)]
        zst = [take(512, kv) for _ in range(2)]
        a = [attn_base]
        x_in = [take(D, a) for _ in range(2)]
        xn = [take(D, a) for _ in range(2)]
        junk1 = take(D, a)
        junk2 = take(QL + KVL, a)
        w_uk_n = take(2 * H * DN, a).rearrange("p (c h d) -> p c h d", c=2, h=H)
        ws_n = take(KD * P, a).rearrange("p (g j) -> p g j", g=KD)
        ws_ns = take(KD * RS, a).rearrange("p (g j) -> p g j", g=KD)

        o = [o_base]
        cq = take(QL, o)
        cq_t = take(3 * P, o).rearrange("p (r n) -> p r n", r=3)
        early = [gains_base]
        qr_tmp = take(H * 32 * 4, early)
        qn_t = take(H * P, early).rearrange("p (h n) -> p h n", h=H)
        qr_n, qr_r = take(H * DR, o), take(H * DR, o)
        ql_t = [take(QB, o).rearrange("p (h c n) -> p h c n", h=H, c=2) for _ in range(2)]
        qr_t = [take(H * P, o).rearrange("p (h n) -> p h n", h=H) for _ in range(2)]
        prob = [take(SEQ, o) for _ in range(2)]
        prob_t = [take(SEQ, early).rearrange("p (j n) -> p j n", j=8) for _ in range(2)]
        pv_t = [take(2 * P, o).rearrange("p (c n) -> p c n", c=2) for _ in range(2)]
        kr_tmp = take(DR * 2, o)
        negmax, psumq, rinv = take(64, o), take(64, o), take(64, o)

        o = [z0_base]
        ck = [take(PG * KVL, o).rearrange("p (r n) -> p r n", r=PG) for _ in range(4)]
        kr = [take(PG * DR, o).rearrange("p (r n) -> p r n", r=PG) for _ in range(4)]
        ck_t = take(2 * 4 * 512, o).rearrange("p (c j n) -> p c j n", c=2, j=4)
        kr_tt = take(2 * 512, o).rearrange("p (g n) -> p g n", g=2)
        early = [gains_base]
        p_exp = take(512, early)
        p_t = take(512, early).rearrange("p (k n) -> p k n", k=4)
        s_new, p_new, p_new_t = (take(NB * RS, early) for _ in range(3))
        o_lat = take(512, early).rearrange("p (c n) -> p c n", c=2)
        q_now = take(2 * RS, early).rearrange("p (c n) -> p c n", c=2)
        qr_now = take(RS, early)
        m_all, l_all, w_all, w_dif, l_w, l_inv = (take(NB, early) for _ in range(6))
        m_now = take(5, early)
        m_part, neg_m, alpha, l_add = (take(1, early) for _ in range(4))
        m8, m8b = take(RS, early), take(P, early)
        idx_now = [take(1, early).bitcast(U32) for _ in range(4)]
        old = [kv_base]
        acc = take(NB * KVL, old).rearrange("p (b c) -> p b c", b=NB)
        assert old[0] <= kv_base + NTP * KVL and early[0] <= gains_base + 4 * D

        o = [kv_base]
        w_o_sb = take(KD * D, o).rearrange("p (k n) -> p k n", k=KD)
        zt = [take(4 * D, o) for _ in range(2)]
        xr = [take(D, o) for _ in range(2)]
        m_t = take(KD * P, o).rearrange("p (k n) -> p k n", k=KD)
        x2_t = take(KD * P, o).rearrange("p (k n) -> p k n", k=KD)
        xo = [take(D, o) for _ in range(2)]
        junk5 = take(D, o)
        stat5 = [take(4, o) for _ in range(2)]
        assert o[0] <= x2_at[0], (o, x2_at)

        o = [attn_base]
        w_e = [(take(KD * DE, o).rearrange("p (k n) -> p k n", k=KD),
                take(KD * DE, o).rearrange("p (k n) -> p k n", k=KD),
                take(2 * D, o).rearrange("p (f n) -> p f n", f=2)) for _ in range(4)]
        xg = [take(D, o) for _ in range(4)]
        xg_t = [take(KD * P, o).rearrange("p (k n) -> p k n", k=KD) for _ in range(2)]
        h_n, h_t = take(DE, o), take(DE, o).rearrange("p (f n) -> p f n", f=2)
        h_s = take(DE, o)
        old = [gains_base]
        yo = [take(D, x) for x in (o, o, old, old)]
        slot_idx = take(2 * NBLK, o).bitcast(U32).rearrange("p (b c) -> p b c", c=2)
        idx_tok, idx_row = ([take(1, o).bitcast(U32) for _ in range(4)] for _ in range(2))
        ovf_id = take(NOVF + 1, o).bitcast(I32)
        gates = take(NT * 2, o).rearrange("p (t c) -> p t c", t=NT)
        rt_base = o[0]
        g_top = take(NT * 8, o).rearrange("p (t n) -> p t n", t=NT)
        g_ind = take(NT * 8, o).bitcast(U32).rearrange("p (t n) -> p t n", t=NT)
        g_f = take(NT, o)
        pen = take(NT * 8, o).rearrange("p (t n) -> p t n", t=NT)
        e_top = take(NT * 8, o).rearrange("p (t n) -> p t n", t=NT)
        e_ind = take(NT * 8, o).bitcast(U32).rearrange("p (t n) -> p t n", t=NT)
        e_f = take(NT * 2, o).rearrange("p (t c) -> p t c", t=NT)
        n_rt = [take(NT * 2, o).rearrange("p (t c) -> p t c", t=NT) for _ in range(6)]
        cnt = [take(NE, o) for _ in range(4)]
        g_sub, g_exp = (take(NT * 8, o).rearrange("p (t n) -> p t n", t=NT) for _ in range(2))
        d_sub, d_exp, g_den, w_one, w_two = (take(NT, o) for _ in range(5))
        pos_i = take(NT * 2, o).bitcast(U32)
        assert o[0] <= x2_at[0], (o, x2_at)
        o2 = [attn_base + 4 * 6144]
        e_log = take(NT * NE, o2).rearrange("p (t n) -> p t n", t=NT)
        hot = take(NT * 2 * NE, o2).rearrange("p (t c n) -> p t c n", t=NT, c=2)
        mask = take(NT * NE, o2).rearrange("p (t n) -> p t n", t=NT)
        rank = take(NT * NE, o2).rearrange("p (t n) -> p t n", t=NT)
        cum = take(NT * NE, o2).rearrange("p (t n) -> p t n", t=NT)
        prod = take(NT * 2 * NE, o2).rearrange("p (t c n) -> p t c n", t=NT, c=2)
        slot_f = take(256, o2)
        fill = take(256, o2)
        assert o2[0] <= attn_base + 4 * 6144 + 4 * D + 2 * KD * P
        o = [attn_base]
        y2 = [take(2 * D, o) for _ in range(2)]
        fin = [take(D, o) for _ in range(2)]
        junk8 = take(D, o)
        stat8 = [take(2, o) for _ in range(2)]

        tab_in, small_in, wuk_in, wuq_in, uv_in, wo_in = (sem(n) for n in (
            "tables_in", "small_in", "wuk_in", "wuq_in", "wuv_in", "wo_in"))
        ws_zero, ws_ready, wsm_ready = sem("ws_zeroed"), sem("ws_loaded"), sem("ws_masked")
        setup_mm, setup_ev = sem("setup_turned"), sem("setup_copied")
        x_loaded = [sem(f"x_loaded{i}") for i in range(2)]
        x_sq, x_rstd, xn_ready = sem("x_squared"), sem("x_rstd"), sem("xn_ready")
        xt_mm = sem("xn_turned")
        xt_ev = [sem("xn_copied_act"), sem("xn_copied_dve")]
        w_loaded = [sem(f"w_in_loaded{i}") for i in range(2)]
        z_mm, z_ev = sem("z_summed"), sem("z_taken")
        z_stored = [sem(f"z_stored{i}") for i in range(2)]
        lat_stored = sem("latent_stored")
        lat_ready = sem("latent_ready")
        p_sq, p_rs, p_cn, p_kr = sem("latent_squared"), sem("latent_rstd"), sem("latent_normed"), sem("krope_ready")
        b_mm = [sem(f"bank{i}_written") for i in range(2)]
        b_ev = [sem(f"bank{i}_taken") for i in range(2)]
        qrope_done = sem("qrope_done")
        s_mm, s_nm, s_exp, s_rinv = sem("scores_ready"), sem("negmax_ready"), sem("probs_ready"), sem("rinv_ready")
        t_mm = [sem("probs_turned_lo"), sem("probs_turned_hi")]
        t_ev = [sem("probs_t_lo"), sem("probs_t_hi")]
        act_c, dve_c, pool_c = sem("act_steps"), sem("dve_steps"), sem("pool_steps")
        ends = sem("stage_ends")
        done = {"n": 0}
        idx_ready = sem("page_index_ready")
        pt_in = sem("page_table_in")
        c_in = [sem(f"cache_in{i}") for i in range(4)]
        c_tr = sem("cache_turned")
        kt_in = [sem("turned_by_act"), sem("turned_by_dve")]
        c_s, c_neg, c_p, c_pt, c_ptc = (sem(n) for n in (
            "cache_scores", "cache_negmax", "cache_probs", "cache_probs_turned", "cache_probs_t"))
        c_sub, c_pv, c_acc, q_ready = sem("shifted"), sem("pv_ready"), sem("acc_done"), sem("batch_queries")
        late_in = sem("late_gains_in")
        n_pe, n_dve, n_act = sem("new_pe"), sem("new_dve"), sem("new_act")
        z_in, xr_in = ([sem(f"{n}{i}") for i in range(2)] for n in ("z_in", "x_again_in"))
        sgu_gated = sem("sgu_gated")
        v_sq, v_rs, v_n = sem("v_squared"), sem("v_rstd"), sem("v_normed")
        mix_mm, sgu_ok, mrg_ok, at_ok = sem("mixed"), sem("sgu_ready"), sem("merged"), sem("gated_attn")
        mt_mm, mt_ev, y_mm, x2_ok = sem("merged_turned"), sem("merged_t"), sem("wo_summed"), sem("x2_ready")
        o_sq, o_rs, o_n, ot_mm, ot_ev = (sem(n) for n in ("x2_squared", "x2_rstd", "x2_normed", "x2n_turned", "x2n_t"))
        lg_mm, lg_ok = sem("logits_summed"), sem("logits_ready")
        xt_st = [sem(f"xt_stored{i}") for i in range(2)]
        v_st = sem("v_stored")
        r_pe, r_dve, r_sub, r_exp = sem("route_pe"), sem("route_dve"), sem("route_exp_in"), sem("route_exp_out")
        r_pos = sem("slot_positions")
        x_inv, v_inv, o_inv, f_inv = sem("x_inv"), sem("v_inv"), sem("x2_inv"), sem("f_inv")
        small_zero = sem("stats_zeroed")
        x2_cp = sem("x2_kept")
        fill_ok = sem("fill_ready")
        qrn_ready, idx_step, x_idx = sem("qrope_copied"), sem("page_index_steps"), sem("slot_index_steps")
        fill_in, scat_in, slots_in, slots_ok = sem("slots_filled"), sem("slots_scattered"), sem("slots_in"), sem("slot_index")
        e_w = [sem(f"gate_up_w{i}") for i in range(4)]
        e_wd = [sem(f"down_w{i}") for i in range(4)]
        e_x = [sem(f"expert_rows{i}") for i in range(4)]
        xg_zero = sem("rows_zeroed")
        e_xt, e_xe, e_gu, e_si, e_h, e_ht, e_he = (sem(n) for n in (
            "rows_turned", "rows_t", "gate_up_summed", "gate_silu", "hidden", "hidden_turned", "hidden_t"))
        e_y = [sem("y_lo"), sem("y_hi")]
        e_ye = [sem("y_lo_copied"), sem("y_hi_copied")]
        e_sc = [sem(f"y_scattered{i}") for i in range(4)]
        yo_free = [sem(f"y_slot_free{i}") for i in range(4)]
        marks = sem("marks")
        moe_end = sem("experts_done")
        f_in = [sem(f"y_rows_in{i}") for i in range(2)]
        f_sum, f_sq, f_rs, f_ok = sem("f_summed"), sem("f_squared"), sem("f_rstd"), sem("f_ready")
        f_st = [sem(f"out_stored{i}") for i in range(2)]

        xp = x_prompt.rearrange("b s d -> (b s) d")
        xs = x_sample.rearrange("b s d -> (b s) d")
        yp = y_prompt.rearrange("b s d -> (b s) d")
        ys = y_sample.rearrange("b s d -> (b s) d")
        w_in_v = w_in[0].rearrange("(k p) n -> p k n", p=P)
        units, sched = attention_schedule()
        bank0_units = 6 * NT + NTP * H
        block = ctx.enter_context(nc.Block())

        turn_units = [("c", 0, 0), ("c", 0, 1), ("r", 0, 0), ("c", 1, 0), ("c", 1, 1),
                      ("c", 2, 0), ("c", 2, 1), ("r", 1, 0), ("c", 3, 0), ("c", 3, 1)]
        NU = len(turn_units)

        def key_row(j, kk):
            return 8 * (j // 2) + 2 * kk + j % 2

        def turned_at(u):
            kind, j, c = turn_units[u]
            return ck_t[:, c, j, :] if kind == "c" else kr_tt[:, j, :]

        def stage_end(eng, k):
            eng.drain().then_inc(ends, 1)
            eng.wait_ge(ends, 4 * k)

        @block.sync
        def _(sp):
            sp.dma_start(K, tables).then_inc(tab_in, 16)

            def x_load(t, s, rows, src):
                sp.dma_start(x_in[s][0:rows, :], src).then_inc(x_loaded[s], 16)

            x_load(0, 0, P, xp[0:P, :])
            x_load(1, 1, P, xp[P:2 * P, :])
            sp.dma_start(g1, norm1_g[0].partition_broadcast(P)).then_inc(small_in, 16)
            sp.dma_start(w_blk[0][:, :, 0:352], w_in_v[:, :, 0:352]).then_inc(w_loaded[0], 16)
            for dst, src in ((gq, q_norm_g[0]),
                             (gkv, kv_norm_g[0]), (rbias[:, 0:NG], b_rg[0]), (rbias[:, NG:], b_re[0])):
                sp.dma_start(dst, src.partition_broadcast(P)).then_inc(small_in, 16)
            sp.dma_start(ids_sb, ids).then_inc(small_in, 16)
            with nc.allow_non_contiguous_dma(reason="small tables"):
                sp.dma_start(w_router[:, :, 0:NG], w_rg[0].rearrange("(k p) n -> p k n", p=P)).then_inc(small_in, 16)
                sp.dma_start(w_router[:, :, NG:], w_re[0].rearrange("(k p) n -> p k n", p=P)).then_inc(small_in, 16)
                sp.dma_start(bs_t, b_s[0].rearrange("g i -> i g")).then_inc(small_in, 16)
                for b in range(NB):
                    sp.dma_start(bs_ts[TS * b:TS * b + TS, :], b_s[0, :, 0:TS].rearrange("g i -> i g")).then_inc(small_in, 16)
                pt = page_table.rearrange("b (c g) -> g (b c)", g=PG)
                for g in range(PG):
                    sp.dma_start(page_raw[8 * g:8 * g + 8, :], pt[g].partition_broadcast(8)).then_inc(pt_in, 16)
                sp.dma_start(w_uk_n, w_uk[0].rearrange("(c p) h d -> p c h d", p=P)).then_inc(wuk_in, 16)
                sp.dma_start(ws_n, w_s[0].rearrange("g i j -> i g j")).then_inc(ws_ready, 16)
                sp.wait_ge(ws_zero, 1)
                for b in range(NB):
                    sp.dma_start(ws_ns[TS * b:TS * b + TS, :, TS * b:TS * b + TS],
                                 w_s[0, :, 0:TS, 0:TS].rearrange("g i j -> i g j")).then_inc(ws_ready, 16)
            sp.dma_start(w_blk[1][:, :, 0:352], w_in_v[:, :, 352:704]).then_inc(w_loaded[1], 16)
            sp.dma_start(w_uq_sb, w_uq[0].rearrange("(r p) h d -> p r (h d)", p=P)).then_inc(wuq_in, 16)
            sp.dma_start(w_qr_sb, w_qr[0].rearrange("(r p) h d -> p r (h d)", p=P)).then_inc(wuq_in, 16)
            sp.dma_start(w_uv_sb, w_uv[0].rearrange("(c p) h d -> p c (h d)", p=P)).then_inc(uv_in, 16)
            with sp.Fori(0, 3) as i:
                for s in range(2):
                    sp.wait_ge(xn_ready, 2 * i + s + 1)
                    x_load(None, s, P, xp[bass.ds(2 * P * i + (s + 2) * P, P), :])
            sp.wait_ge(xn_ready, 7)
            x_load(8, 0, RS, xs)

            sp.wait_ge(z_mm, NT)
            sp.dma_start(w_blk[0], w_in_v[:, :, ZL:ZL + 512]).then_inc(w_loaded[0], 16)

            def block_moves(b, s, load):
                if load:
                    sp.wait_ge(z_mm, NT * 2 + NT * b)
                    sp.dma_start(w_blk[1 - s], w_in_v[:, :, bass.ds(512 * b + ZL + 512, 512)]).then_inc(w_loaded[1 - s], 16)
                cols = [z_act[t * P:t * P + rows_of(t), bass.ds(512 * b, 512)] for t in range(NT)]
                for t in range(NT):
                    u = (s * NT + t) % 2
                    r = rows_of(t)
                    sp.wait_ge(z_ev, NT * 2 + NT * b + t + 1)
                    sp.sem_inc(marks, 1)
                    sp.dma_start(cols[t], zst[u][0:r, :]).then_inc(z_stored[u], 16)

            with sp.Fori(0, 3) as i:
                block_moves(2 * i, 0, True)
                block_moves(2 * i + 1, 1, True)
            block_moves(6, 0, True)
            block_moves(7, 1, False)

            sp.wait_ge(lat_ready, 2)
            sp.dma_start(ckv_prompt.rearrange("l b t p c -> p (l b t) c"), ckv_n[:, 0:NTP, :]).then_inc(lat_stored, 16)
            sp.dma_start(kr_prompt.rearrange("l b t p c -> p (l b t) c"), kr_n[:, 0:NTP, :]).then_inc(lat_stored, 16)
            sp.dma_start(ckv_sample.rearrange("l b t c -> (l b t) c"), ckv_n[0:RS, NTP, :]).then_inc(lat_stored, 16)
            sp.dma_start(kr_sample.rearrange("l b t c -> (l b t) c"), kr_n[0:RS, NTP, :]).then_inc(lat_stored, 16)
            sp.wait_ge(lat_stored, 64)

            sp.wait_ge(ends, 12)
            for dst, src in ((g2, norm2_g[0]), (gf, norm_f_g), (gv, sgu_norm_g[0])):
                sp.dma_start(dst, src.partition_broadcast(P)).then_inc(late_in, 16)
            for u in range(2):
                sp.wait_ge(z_stored[u], 16 * (8 * NT // 2) + 16)

            def z_load(s, r, z_src):
                sp.dma_start(zt[s][0:r, :], z_src).then_inc(z_in[s], 16)

            def x_again(s, r, x_src):
                sp.dma_start(xr[s][0:r, :], x_src).then_inc(xr_in[s], 16)

            z_load(0, P, z_act[0:P, :])
            z_load(1, P, z_act[P:2 * P, :])
            sp.dma_start(w_o_sb, w_o[0].rearrange("(k p) n -> p k n", p=P)).then_inc(wo_in, 16)
            x_again(0, P, xp[0:P, :])
            x_again(1, P, xp[P:2 * P, :])
            with sp.Fori(0, 3) as i:
                for s in range(2):
                    n = 2 * i + s
                    sp.wait_ge(mt_mm, n + 1)
                    z_load(s, P, z_act[bass.ds(2 * P * i + (s + 2) * P, P), :])
                    sp.wait_ge(o_n, n + 1)
                    sp.wait_ge(x2_cp, n + 1)
                    x_again(s, P, xp[bass.ds(2 * P * i + (s + 2) * P, P), :])
                    sp.dma_start(xt_rows[bass.ds(2 * P * i + s * P, P), :], xo[s]).then_inc(xt_st[s], 16)
            sp.wait_ge(mt_mm, 7)
            z_load(0, RS, z_act[8 * P:TOK, :])
            sp.wait_ge(o_n, 7)
            sp.wait_ge(x2_cp, 7)
            x_again(0, RS, xs)
            for t in range(6, NT):
                sp.wait_ge(o_n, t + 1)
                r = rows_of(t)
                sp.dma_start(xt_rows[t * P:t * P + r, :], xo[t % 2][0:r, :]).then_inc(xt_st[t % 2], 16)
            sp.wait_ge(v_n, NT)
            sp.dma_start(v_sample.rearrange("l b t c -> (l b t) c"), zt[0][0:RS, D:2 * D]).then_inc(v_st, 16)
            sp.wait_ge(v_st, 16)

            sp.wait_ge(fill_ok, 1)
            slots_v = slot_rows.rearrange("(b r) c -> b (r c)", r=P)
            sp.dma_start(slots_v, fill[0:NBLK, :].bitcast(I32)).then_inc(fill_in, 16)

            def w_load(s, e, parts=(0, 1, 2)):
                for x in parts:
                    sp.dma_start(w_e[s][x].rearrange("p k n -> p (k n)"),
                                 (w_gate, w_up, w_down)[x][0, bass.ds(e, 1)].rearrange("e (p k) n -> p (e k n)", p=P)
                                 ).then_inc(e_w[s] if x < 2 else e_wd[s], 16)

            sp.wait_ge(ends, 16)
            for s in range(4):
                w_load(s, s)
            sp.wait_ge(scat_in, 16 * 2 * NT)
            sp.dma_start(fill[0:NBLK, :].bitcast(I32), slots_v).then_inc(slots_in, 16)
            with sp.Fori(0, 15) as i:
                for s in range(4):
                    sp.wait_ge(e_gu, 4 * i + s + 1)
                    w_load(s, 4 * i + s + 4, (0, 1))
                    sp.wait_ge(e_y[1], 4 * i + s + 1)
                    w_load(s, 4 * i + s + 4, (2,))
            sp.wait_ge(slots_ok, 1)
            total = sp.value_load(ovf_id[0:1, NOVF:NOVF + 1], min_val=0, max_val=NOVF)
            sp.wait_ge(e_y[1], NE)
            with sp.Fori(0, NOVF) as j:
                with sp.If(total > j):
                    e = sp.value_load(ovf_id[0:1, bass.ds(j, 1)], min_val=0, max_val=NE - 1)
                    sp.wait_ge(e_y[1], NE + j)
                    w_load(0, e)

            sp.wait_ge(moe_end, 1)
            yr = y_rows.rearrange("(n c) d -> n (c d)", c=2)
            sp.dma_start(y2[0], yr[0:P, :]).then_inc(f_in[0], 16)
            sp.dma_start(y2[1], yr[P:2 * P, :]).then_inc(f_in[1], 16)
            with sp.Fori(0, 3) as i:
                for s in range(2):
                    sp.wait_ge(f_sum, 2 * i + s + 1)
                    sp.dma_start(y2[s], yr[bass.ds(2 * P * i + (s + 2) * P, P), :]).then_inc(f_in[s], 16)
                    sp.wait_ge(f_ok, 2 * i + s + 1)
                    sp.dma_start(yp[bass.ds(2 * P * i + s * P, P), :], fin[s]).then_inc(f_st[s], 16)
            sp.wait_ge(f_sum, 7)
            sp.dma_start(y2[0][0:RS, :], yr[8 * P:TOK, :]).then_inc(f_in[0], 16)
            for t in range(6, NT):
                sp.wait_ge(f_ok, t + 1)
                if t < NTP:
                    sp.dma_start(yp[t * P:(t + 1) * P, :], fin[t % 2]).then_inc(f_st[t % 2], 16)
                else:
                    sp.dma_start(ys, fin[0][0:RS, :]).then_inc(f_st[0], 16)
            sp.wait_ge(f_st[0], 16 * 6)
            sp.wait_ge(f_st[1], 16 * 5)

        @block.tensor
        def _(pe):
            mm, tr = nc.tensor.matmul, nc.tensor.transpose
            pe.wait_ge(tab_in, 16)
            pe.wait_ge(wuk_in, 16)
            for u in range(4):
                b = 6 + u % 2
                if u >= 2:
                    pe.wait_ge(setup_ev, u - 1)
                for i in range(4):
                    h, c = 2 * u + i // 2, i % 2
                    last = tr(bank(b)[:, P * i:P * i + P], w_uk_n[:, c, h, :], ident)
                last.then_inc(setup_mm, 1)
            pe.wait_ge(wsm_ready, 1)
            for u in range(2):
                pe.wait_ge(setup_ev, 3 + u)
                for i in range(4):
                    last = tr(bank(6 + u)[:, P * i:P * i + P], ws_n[:, 4 * u + i, :], ident)
                last.then_inc(setup_mm, 1)
            pe.wait_ge(setup_ev, 5)
            for g in range(KD):
                last = tr(bank(6)[0:RS, RS * g:RS * g + RS], ws_ns[0:RS, g, :], ident[0:RS, 0:RS])
            last.then_inc(setup_mm, 1)

            def turn_x(n, s, r):
                pe.wait_ge(xn_ready, n + 1)
                pe.wait_ge(xt_ev[0], n + 1)
                pe.wait_ge(xt_ev[1], n + 1)
                for k in range(KD):
                    last = tr(bank(2 * s, 2)[:, P * k:P * k + r], xn[s][0:r, P * k:P * k + P], ident[0:r, 0:r])
                last.then_inc(xt_mm, 1)

            with pe.Fori(0, 4) as i:
                for s in range(2):
                    turn_x(2 * i + s, s, P)
            turn_x(8, 0, RS)
            pe.wait_ge(xt_ev[0], NT + 2)
            pe.wait_ge(xt_ev[1], NT + 2)

            def z_block(n, s, w, i_loaded, first=False):
                pe.wait_ge(w_loaded[s], 16 * i_loaded)
                for t in range(NT):
                    r = rows_of(t)
                    u = (s * NT + t) % 2
                    if not (first and t < 2):
                        pe.wait_ge(z_ev, NT * n + t - 1)
                    for k in range(KD):
                        last = mm(bank(4 + u)[0:r, 0:w], xn_t[:, k, t * P:t * P + r], w_blk[s][:, k, 0:w],
                                  start=(k == 0), stop=(k == KD - 1))
                    last.then_inc(z_mm, 1)

            z_block(0, 0, 352, 1, True)
            z_block(1, 1, 352, 1)
            with pe.Fori(0, 4) as i:
                z_block(2 * i + 2, 0, 512, i + 2)
                z_block(2 * i + 3, 1, 512, i + 2)
            pe.wait_ge(z_ev, 10 * NT)
            stage_end(pe, 1)

            pe.wait_ge(wuq_in, 32)
            pe.wait_ge(uv_in, 16)
            pe.wait_ge(setup_ev, 7)
            used = [0, 0]

            def open_bank(b):
                if used[b]:
                    pe.wait_ge(b_ev[b], used[b])
                used[b] += 1

            for what, n in sched:
                if what == "Q":
                    t, r, s = n, rows_of(n), n % 2
                    pe.wait_ge(p_cn, t + 1)
                    pe.wait_ge(p_kr, t + 1)
                    open_bank(0)
                    for i in range(3):
                        tr(bank(0)[:, P * i:P * i + r], cq[0:r, P * i:P * i + P], ident[0:r, 0:r])
                    tr(bank(0)[0:DR, 384:384 + r], kr_n[0:r, t, :], ident[0:r, 0:r]).then_inc(b_mm[0], 1)
                    open_bank(1)
                    for c in range(2):
                        last = tr(bank(1)[:, P * c:P * c + r], ckv_n[0:r, t, P * c:P * c + P], ident[0:r, 0:r])
                    last.then_inc(b_mm[1], 1)
                    pe.wait_ge(b_ev[0], used[0])
                    for u in range(2):
                        open_bank(u)
                        for i in range(4):
                            h = 4 * u + i
                            for c in range(3):
                                last = mm(bank(u)[:, P * i:P * i + r], w_uq_sb[:, c, P * h:P * h + P], cq_t[:, c, 0:r],
                                          start=(c == 0), stop=(c == 2))
                        last.then_inc(b_mm[u], 1)
                    open_bank(0)
                    for c in range(3):
                        last = mm(bank(0)[0:r, :], cq_t[:, c, 0:r], w_qr_sb[:, c, :], start=(c == 0), stop=(c == 2))
                    last.then_inc(b_mm[0], 1)
                    for u in range(4):
                        b = 1 - u % 2
                        open_bank(b)
                        for i in range(4):
                            h, c = 2 * u + i // 2, i % 2
                            last = mm(bank(b)[:, P * i:P * i + r], w_uk_t[:, h, P * c:P * c + P], qn_t[:, h, 0:r],
                                      start=True, stop=True)
                        last.then_inc(b_mm[b], 1)
                    pe.wait_ge(qrope_done, t + 1)
                    for u in range(2):
                        b = 1 - u
                        open_bank(b)
                        for i in range(4):
                            h = 4 * u + i
                            last = tr(bank(b)[0:DR, P * i:P * i + r], qr_r[0:r, DR * h:DR * h + DR], ident[0:r, 0:r])
                        last.then_inc(b_mm[b], 1)
                    pe.wait_ge(b_ev[0], used[0])
                    pe.wait_ge(b_ev[1], used[1])
                elif what == "S":
                    t, h = units[n]
                    s, sl = t % 2, n % 2
                    if n >= 2:
                        pe.wait_ge(s_exp, n - 1)
                    for c0 in range(0, P * (t + 1), 512):
                        w = min(512, P * (t + 1) - c0)
                        out = bank(2 + 2 * sl, 2)[:, c0:c0 + w]
                        mm(out, ql_t[s][:, h, 0, :], ckv_t[:, 0, c0:c0 + w], start=True, stop=False)
                        mm(out, ql_t[s][:, h, 1, :], ckv_t[:, 1, c0:c0 + w], start=False, stop=False)
                        diag = c0 <= P * t < c0 + w
                        last = mm(out, qr_t[s][0:DR, h, :], kr_t[0:DR, c0:c0 + w], start=False, stop=True)
                        if diag:
                            last = mm(bank(2 + 2 * sl, 2)[:, P * t:P * t + P], ident, const("negmask"),
                                      start=False, stop=True, skip_group_check=True)
                    last.then_inc(s_mm, 1)
                elif what == "T":
                    t, h = units[n]
                    pe.wait_ge(s_exp, n + 1)
                    for half in range(2):
                        js = range(4 * half, min(4 * half + 4, t + 1))
                        if not js:
                            continue
                        k = n if half == 0 else n - 4 * H
                        if k >= 1:
                            pe.wait_ge(t_ev[half], k)
                        for j in js:
                            last = tr(bank(6 + half)[:, P * (j % 4):P * (j % 4) + P], prob[n % 2][:, P * j:P * j + P], ident)
                        last.then_inc(t_mm[half], 1)
                elif what == "PV":
                    t, h = units[n]
                    b = n % 2
                    pe.wait_ge(t_ev[0], n + 1)
                    if t >= 4:
                        pe.wait_ge(t_ev[1], n - 4 * H + 1)
                    open_bank(b)
                    for c in range(2):
                        for j in range(t + 1):
                            last = mm(bank(b)[:, P * c:P * c + P], ckv_n[:, j, P * c:P * c + P], prob_t[b][:, j, :],
                                      start=(j == 0), stop=(j == t))
                    last.then_inc(b_mm[b], 1)
                elif what == "UV":
                    t, h = units[n]
                    b = n % 2
                    open_bank(b)
                    for c in range(2):
                        last = mm(bank(b)[:, 0:DV], pv_t[b][:, c, :], w_uv_sb[:, c, DV * h:DV * h + DV],
                                  start=(c == 0), stop=(c == 1))
                    last.then_inc(b_mm[b], 1)
            pe.wait_ge(b_ev[0], used[0])
            pe.wait_ge(b_ev[1], used[1])
            stage_end(pe, 2)

            pe.wait_ge(n_dve, 1)
            for b in range(NB):
                new, cols = bank(5)[0:RS, RS * b:RS * b + RS], slice(RS * b, RS * b + RS)
                mm(new, qs[:, 0, cols], ckv_t[:, 0, SEQ:TOK], start=True, stop=False)
                mm(new, qs[:, 1, cols], ckv_t[:, 1, SEQ:TOK], start=False, stop=False)
                last = mm(new, qsr[0:DR, cols], kr_t[0:DR, SEQ:TOK], start=False, stop=True)
            last.then_inc(n_pe, 1)
            pe.wait_ge(n_act, 1)
            for b in range(NB):
                last = tr(bank(6)[0:RS, RS * b:RS * b + RS], p_new[0:RS, RS * b:RS * b + RS], ident[0:RS, 0:RS])
            last.then_inc(n_pe, 1)
            pe.wait_ge(n_dve, 2)
            for b in range(NB):
                last = mm(bank(0, 4)[0:RS, KVL * b:KVL * b + KVL], p_new_t[0:RS, RS * b:RS * b + RS], ckv_n[0:RS, NTP, :],
                          start=True, stop=True)
            last.then_inc(n_pe, 1)
            pe.wait_ge(n_dve, 3)

            def turn(n, q, us, first=False):
                for u in us:
                    if u >= 5:
                        pe.wait_ge(kt_in[(u - 5) % 2], 5 * n + (u - 5) // 2 + 1)
                    elif not first:
                        pe.wait_ge(kt_in[(u + 5) % 2], 5 * n - 5 + (u + 5) // 2 + 1)
                    kind, j, c = turn_units[u]
                    for kk in range(4):
                        if kind == "c":
                            src = ck[q][:, key_row(j, kk), P * c:P * c + P]
                        else:
                            src = kr[q][:, 8 * j + 2 * kk:8 * j + 2 * kk + 2, :].rearrange("p r n -> p (r n)")
                        last = tr(bank(u % 5)[:, P * kk:P * kk + P], src, ident)
                    last.then_inc(c_tr, 1)

            def score(n):
                for e in range(2):
                    pe.wait_ge(kt_in[e], 5 * n + 5)
                for c in range(3):
                    for j in range(4):
                        half = slice(DR * (j % 2), DR * (j % 2) + DR)
                        last = mm(bank(5)[RS * j:RS * j + RS, :], q_now[:, c, :] if c < 2 else qr_now[half, :],
                                  ck_t[:, c, j, :] if c < 2 else kr_tt[half, j // 2, :], start=(c == 0), stop=(c == 2))
                last.then_inc(c_s, 1)

            def turn_probs(n):
                pe.wait_ge(c_p, n + 1)
                for kk in range(4):
                    last = tr(bank(6)[:, P * kk:P * kk + P], p_exp[:, P * kk:P * kk + P], ident)
                last.then_inc(c_pt, 1)

            def weigh(n, q):
                pe.wait_ge(c_ptc, n + 1)
                pe.wait_ge(c_acc, n + 1)
                for kk in range(4):
                    for j in range(4):
                        last = mm(bank(7)[RS * j:RS * j + RS, 0:KVL], p_t[:, kk, RS * j:RS * j + RS],
                                  ck[q][:, key_row(j, kk), :], start=(kk == 0), stop=(kk == 3))
                last.then_inc(c_pv, 1)

            pe.wait_ge(c_in[0], 32)
            turn(0, 0, range(NU), first=True)
            pe.wait_ge(q_ready, 1)
            score(0)

            def batch(i, last_batch):
                for q in range(4):
                    n = 4 * i + q
                    more = q < 3 or not last_batch
                    if more:
                        pe.wait_ge(c_in[(q + 1) % 4], 32 * i + (32 if q < 3 else 64))
                        turn(n + 1, (q + 1) % 4, range(6))
                    turn_probs(n)
                    if more:
                        turn(n + 1, (q + 1) % 4, range(6, NU))
                    weigh(n, q)
                    if more:
                        if q == 3:
                            pe.wait_ge(q_ready, i + 2)
                        score(n + 1)

            with pe.Fori(0, NB - 1) as i:
                batch(i, False)
            batch(NB - 1, True)
            pe.wait_ge(n_dve, 4)
            tr(bank(6)[0:NB, 0:P], m_all, ident).then_inc(n_pe, 1)
            pe.wait_ge(n_dve, 5)
            tr(bank(6)[:, P:P + NB], m8b[0:NB, :], ident[0:NB, 0:NB]).then_inc(n_pe, 1)
            pe.wait_ge(n_dve, 6)
            mm(bank(6)[:, 2 * P:2 * P + NB], const("same_q"), l_w, start=True, stop=True).then_inc(n_pe, 1)
            pe.wait_ge(n_dve, 7)
            for c in range(2):
                for b in range(NB):
                    last = mm(bank(7)[:, NB * RS * c + RS * b:NB * RS * c + RS * b + RS], acc[:, b, P * c:P * c + P],
                              const("same_q")[:, 0:RS], start=True, stop=True)
            last.then_inc(n_pe, 1)
            pe.wait_ge(n_dve, 8)
            for h in range(H):
                for c in range(2):
                    last = mm(bank(0, 2)[0:RS, DV * h:DV * h + DV], o_lat[:, c, RS * h:RS * h + RS],
                              w_uv_sb[:, c, DV * h:DV * h + DV], start=(c == 0), stop=(c == 1))
            last.then_inc(n_pe, 1)
            pe.wait_ge(n_act, 3)
            stage_end(pe, 3)

            def mix(n, s):
                last_tile = isinstance(n, int) and n == NTP
                r, wst = (RS, ws_ts) if last_tile else (P, ws_t)
                pe.wait_ge(v_n, n + 1)
                pe.wait_ge(sgu_ok, n + 1)
                for g in range(KD):
                    last = mm(bank(0, 2)[0:r, P * g:P * g + P], wst[0:r, g, 0:r], zt[s][0:r, D + P * g:D + P * g + P],
                              start=True, stop=True)
                last.then_inc(mix_mm, 1)

            def turn_merged(n, s, r=P):
                pe.wait_ge(mrg_ok, n + 1)
                for k in range(KD):
                    last = tr(bank(2, 2)[:, P * k:P * k + r], zt[s][0:r, P * k:P * k + P], ident[0:r, 0:r])
                last.then_inc(mt_mm, 1)

            def out_product(n, r=P):
                pe.wait_ge(mt_ev, n + 1)
                for half in range(2):
                    for k in range(KD):
                        last = mm(bank(4 + half)[0:r, :], m_t[:, k, 0:r], w_o_sb[:, k, 512 * half:512 * half + 512],
                                  start=(k == 0), stop=(k == KD - 1))
                last.then_inc(y_mm, 1)

            def turn_normed(n, s, r=P):
                pe.wait_ge(o_n, n + 1)
                pe.wait_ge(lg_ok, n + 1)
                for k in range(KD):
                    last = tr(bank(6, 2)[:, P * k:P * k + r], xo[s][0:r, P * k:P * k + P], ident[0:r, 0:r])
                last.then_inc(ot_mm, 1)

            def router(n, r=P):
                pe.wait_ge(ot_ev, n + 1)
                for k in range(KD):
                    last = mm(bank(6)[0:r, 0:72], x2_t[:, k, 0:r], w_router[:, k, :], start=(k == 0), stop=(k == KD - 1))
                last.then_inc(lg_mm, 1)

            mix(0, 0)
            turn_merged(0, 0)
            mix(1, 1)
            pe.wait_ge(wo_in, 16)
            out_product(0)
            turn_merged(1, 1)

            def step5(n, s):
                mix(n + 1, 1 - s)
                turn_normed(n - 1, 1 - s)
                out_product(n)
                turn_merged(n + 1, 1 - s, RS if isinstance(n, int) else P)
                router(n - 1)

            with pe.Fori(0, 3) as i:
                for s in range(1, 3):
                    step5(2 * i + s, s % 2)
            step5(7, 1)
            turn_normed(7, 1)
            out_product(8, RS)
            router(7)
            turn_normed(8, 0, RS)
            router(8, RS)
            pe.wait_ge(lg_ok, NT + 1)
            stage_end(pe, 4)

            pe.wait_ge(r_dve, 1)
            for t in range(NT):
                out = bank(t // 8)[:, NE * (t % 8):NE * (t % 8) + NE]
                mm(out, const("before"), mask[:, t, :], start=True, stop=False)
                mm(out, ones, cum[:, t, :], start=False, stop=True)
            mm(bank(1)[:, NE:2 * NE], ones, rank[:, 0, :], start=True, stop=True).then_inc(r_pe, 1)
            pe.wait_ge(r_dve, 2)
            for c in range(2):
                last = tr(bank(2)[:, P * c:P * c + NBLK], slot_f.rearrange("p (r c) -> p c r", c=2)[0:NBLK, c, :],
                          ident[0:NBLK, 0:NBLK])
            last.then_inc(r_pe, 1)
            pe.wait_ge(slots_ok, 1)

            def turn_rows(n, s, i_x):
                pe.wait_ge(e_x[s], 16 * i_x)
                if not (isinstance(n, int) and n == 0):
                    pe.wait_ge(e_xe, 2 * n)
                for k in range(KD):
                    last = tr(bank(0, 2)[:, P * k:P * k + P], xg[s].rearrange("p (n k) -> p k n", k=KD)[:, k, :], ident)
                last.then_inc(e_xt, 1)

            def gate_up(n, sw, u, i_w):
                pe.wait_ge(e_w[sw], 32 * i_w)
                pe.wait_ge(e_xe, 2 * n + 2)
                for x in range(2):
                    for k in range(KD):
                        last = mm(bank(2 + u)[:, DE * x:DE * x + DE], xg_t[u][:, k, :], w_e[sw][x][:, k, :],
                                  start=(k == 0), stop=(k == KD - 1))
                last.then_inc(e_gu, 1)

            def turn_hidden(n):
                pe.wait_ge(e_h, n + 1)
                for f in range(2):
                    last = tr(bank(4)[:, P * f:P * f + P], h_n.rearrange("p (n f) -> p f n", f=2)[:, f, :], ident)
                last.then_inc(e_ht, 1)

            def down(n, sw, i_w):
                pe.wait_ge(e_he, n + 1)
                pe.wait_ge(e_wd[sw], 16 * i_w)
                for half in range(2):
                    pe.wait_ge(e_ye[half], n + 1)
                    for f in range(2):
                        last = mm(bank(5 + half), h_t[:, f, :], w_e[sw][2][:, f, 512 * half:512 * half + 512],
                                  start=(f == 0), stop=(f == 1))
                    last.then_inc(e_y[half], 1)

            def step7(n, q, i):
                if not (isinstance(n, int) and n == NE - 1):
                    turn_rows(n + 1, (q + 1) % 4, i + 1 + (q + 1) // 4)
                turn_hidden(n - 1)
                gate_up(n, q % 4, q % 2, i + 1 + q // 4)
                down(n - 1, (q - 1) % 4, i + 1 + (q - 1) // 4)

            turn_rows(0, 0, 1)
            turn_rows(1, 1, 1)
            gate_up(0, 0, 0, 1)
            with pe.Fori(0, 15) as i:
                for q in range(1, 5):
                    step7(4 * i + q, q, i)
            for q in range(1, 4):
                step7(60 + q, q, 15)
            turn_hidden(NE - 1)
            down(NE - 1, 3, NE // 4)
            total = pe.value_load(ovf_id[0:1, NOVF:NOVF + 1], min_val=0, max_val=NOVF)
            with pe.Fori(0, NOVF) as j:
                with pe.If(total > j):
                    turn_rows(NE + j, 0, 17 + j)
                    gate_up(NE + j, 0, 0, 17 + j)
                    turn_hidden(NE + j)
                    down(NE + j, 0, 17 + j)

        @block.scalar
        def _(act):
            A = nc.scalar.activation
            act.sem_inc(xt_ev[0], 2)
            act.sem_inc(e_ye[0], 1)
            for u in range(2):
                act.sem_inc(z_stored[u], 16)
            act.wait_ge(tab_in, 16)
            act.wait_ge(small_zero, 1)

            for u in range(4):
                act.wait_ge(setup_mm, u + 1)
                nc.scalar.copy(w_uk_t[:, 2 * u:2 * u + 2, :].rearrange("p h c -> p (h c)"), bank(6 + u % 2)).then_inc(setup_ev, 1)
            for u in range(2):
                act.wait_ge(setup_mm, 5 + u)
                nc.scalar.copy(ws_t[:, 4 * u:4 * u + 4, :].rearrange("p g i -> p (g i)"), bank(6 + u)).then_inc(setup_ev, 1)
            act.wait_ge(setup_mm, 7)
            nc.scalar.copy(ws_ts[0:RS, :, :].rearrange("p g i -> p (g i)"), bank(6)[0:RS, 0:RS * KD]).then_inc(setup_ev, 1)

            def square_x(n, s, r, i_l):
                act.wait_ge(x_loaded[s], 16 * i_l)
                A(junk1[0:r, :], x_in[s][0:r, :], ACT.Square, scale=D ** -0.5, accum_out=small[0:r, s:s + 1]).then_inc(x_sq, 1)
                act.wait_ge(x_sq, n + 1)
                A(small[0:r, 2 + s:3 + s], small[0:r, s:s + 1], ACT.Sqrt, bias=eps[0:r]).then_inc(x_rstd, 1)

            def copy_x(n, s, r, dst):
                act.wait_ge(xt_mm, n + 1)
                nc.scalar.copy(dst, bank(2 * s).rearrange("p (k n) -> p k n", k=4)[:, :, 0:r]).then_inc(xt_ev[0], 1)

            with act.Fori(0, 4) as i:
                for s in range(2):
                    square_x(2 * i + s, s, P, i + 1)
                    copy_x(2 * i + s, s, P, xn_t[:, 0:4, bass.ds(2 * P * i + P * s, P)])
            square_x(8, 0, RS, 5)
            copy_x(8, 0, RS, xn_t[:, 0:4, SEQ:TOK])

            def take_z(n, s):
                for t in range(NT):
                    r = rows_of(t)
                    u = (s * NT + t) % 2
                    act.wait_ge(z_mm, NT * n + t + 1)
                    nc.scalar.copy(z0[0:r, t, 352 * s:352 * s + 352], bank(4 + u)[0:r, 0:352]).then_inc(z_ev, 1)

            take_z(0, 0)
            take_z(1, 1)

            def take_pair(i, func):
                for s in range(2):
                    for t in range(NT):
                        r = rows_of(t)
                        u = (s * NT + t) % 2
                        act.wait_ge(z_mm, 2 * NT * i + 2 * NT + s * NT + t + 1)
                        act.wait_ge(z_stored[u], 16 * NT * i + 16 * ((s * NT + t) // 2) + 16)
                        A(zst[u][0:r, :], bank(4 + u)[0:r, :], func).then_inc(z_ev, 1)

            with act.Fori(0, 2) as i:
                take_pair(i, ACT.Gelu_apprx_tanh)
            with act.Fori(2, 4) as i:
                take_pair(i, ACT.Sigmoid)
            act.wait_ge(p_sq, 1)
            A(stat, stat, ACT.Sqrt, bias=eps).then_inc(p_rs, 1)
            for u in range(2):
                act.wait_ge(z_stored[u], 16 * (8 * NT // 2) + 16)
            stage_end(act, 1)

            got = 0
            for what, n in sched:
                if what == "Q":
                    t, r, s = n, rows_of(n), n % 2

                    def from0(dst, src):
                        nonlocal got
                        got += 1
                        act.wait_ge(b_mm[0], got)
                        nc.scalar.copy(dst, src).then_inc(b_ev[0], 1)

                    b0 = bank(0).rearrange("p (i n) -> p i n", i=4)
                    got += 1
                    act.wait_ge(b_mm[0], got)
                    nc.scalar.copy(kr_t[0:DR, t * P:t * P + r], b0[0:DR, 3, 0:r])
                    nc.scalar.copy(cq_t[:, :, 0:r], b0[:, 0:3, 0:r]).then_inc(b_ev[0], 1)
                    from0(qn_t[:, 0:4, 0:r], b0[:, :, 0:r])
                    from0(qr_n[0:r, :], bank(0)[0:r, :])
                    act.wait_ge(b_ev[0], got)
                    act.sem_inc(qrn_ready, 1)
                    for h in (2, 6):
                        from0(ql_t[s][:, h:h + 2, :, 0:r].rearrange("p h c n -> p (h c) n"), b0[:, :, 0:r])
                    from0(qr_t[s][0:DR, 4:8, 0:r], b0[0:DR, :, 0:r])
                elif what == "S":
                    t, h = units[n]
                    w = P * (t + 1)
                    act.wait_ge(s_nm, n + 1)
                    A(prob[n % 2][:, 0:w], bank(2 + 2 * (n % 2), 2)[:, 0:w], ACT.Exp, bias=negmax[:, n:n + 1], scale=SCALE,
                      accum_out=psumq[:, n:n + 1]).then_inc(s_exp, 1)
                elif what == "T":
                    t, h = units[n]
                    w = P * min(t + 1, 4)
                    act.wait_ge(t_mm[0], n + 1)
                    nc.scalar.copy(prob_t[n % 2][:, 0:w // P, :].rearrange("p j n -> p (j n)"), bank(6)[:, 0:w]).then_inc(t_ev[0], 1)
                elif what != "prep" and n % 2 == 0:
                    t, h = units[n]
                    got += 1
                    act.wait_ge(b_mm[0], got)
                    if what == "PV":
                        nc.scalar.copy(pv_t[0].rearrange("p c n -> p (c n)"), bank(0)[:, 0:2 * P]).then_inc(b_ev[0], 1)
                    else:
                        act.wait_ge(s_rinv, n + 1)
                        A(attn[:, t, DV * h:DV * h + DV], bank(0)[:, 0:DV], ACT.Copy, scale=rinv[:, n:n + 1]).then_inc(b_ev[0], 1)
            stage_end(act, 2)

            act.wait_ge(c_sub, 1)
            A(p_new[0:RS, :], s_new[0:RS, :], ACT.Exp, scale=SCALE).then_inc(n_act, 1)

            def turned(n, us):
                for u in us:
                    act.wait_ge(c_tr, NU * n + u + 1)
                    nc.scalar.copy(turned_at(u), bank(u % 5)).then_inc(kt_in[0], 1)

            act.wait_ge(n_dve, 3)
            turned(0, range(0, NU, 2))

            def batch(i, last_batch):
                for q in range(4):
                    n = 4 * i + q
                    more = q < 3 or not last_batch
                    if more:
                        turned(n + 1, (0,))
                    act.wait_ge(c_neg, n + 1)
                    A(alpha, m_now[:, q:q + 1], ACT.Exp, bias=neg_m, scale=SCALE)
                    A(p_exp, bank(5), ACT.Exp, bias=neg_m, scale=SCALE, accum_out=l_add).then_inc(c_p, 1)
                    if more:
                        turned(n + 1, (2, 4))
                    act.wait_ge(c_pt, n + 1)
                    nc.scalar.copy(p_t.rearrange("p k n -> p (k n)"), bank(6)).then_inc(c_ptc, 1)
                    if more:
                        turned(n + 1, (6, 8))

            with act.Fori(0, NB - 1) as i:
                batch(i, False)
            batch(NB - 1, True)
            act.wait_ge(c_sub, 2)
            A(w_all, w_dif, ACT.Exp, scale=SCALE).then_inc(n_act, 1)
            act.wait_ge(n_pe, 8)
            nc.scalar.copy(attn[0:RS, NTP, :], bank(0, 2)[0:RS, :]).then_inc(n_act, 1)
            stage_end(act, 3)

            def v_stat(n, s, i_in, r=P):
                act.wait_ge(z_in[s], 16 * i_in)
                A(junk5[0:r, :], zt[s][0:r, D:2 * D], ACT.Square, scale=D ** -0.5, accum_out=stat5[s][0:r, 0:1]).then_inc(v_sq, 1)
                act.wait_ge(v_sq, n + 1)
                A(stat5[s][0:r, 0:1], stat5[s][0:r, 0:1], ACT.Sqrt, bias=eps[0:r]).then_inc(v_rs, 1)

            def merged_t(n, r=P):
                act.wait_ge(mt_mm, n + 1)
                nc.scalar.copy(m_t[:, :, 0:r], bank(2, 2).rearrange("p (k n) -> p k n", k=KD)[:, :, 0:r]).then_inc(mt_ev, 1)

            def x2_stat(n, s, r=P):
                act.wait_ge(x2_ok, n + 1)
                A(junk5[0:r, :], xr[s][0:r, :], ACT.Square, scale=D ** -0.5, accum_out=stat5[s][0:r, 2:3]).then_inc(o_sq, 1)
                act.wait_ge(o_sq, n + 1)
                A(stat5[s][0:r, 2:3], stat5[s][0:r, 2:3], ACT.Sqrt, bias=eps[0:r]).then_inc(o_rs, 1)

            def normed_t(n, r=P):
                act.wait_ge(ot_mm, n + 1)
                nc.scalar.copy(x2_t[:, :, 0:r], bank(6, 2).rearrange("p (k n) -> p k n", k=KD)[:, :, 0:r]).then_inc(ot_ev, 1)

            v_stat(0, 0, 1)
            v_stat(1, 1, 1)
            merged_t(0)
            v_stat(2, 0, 2)
            x2_stat(0, 0)
            merged_t(1)
            with act.Fori(0, 2) as i:
                for s in range(1, 3):
                    n = 2 * i + s
                    normed_t(n - 1)
                    v_stat(n + 2, s % 2, i + 2 if s == 1 else i + 3)
                    x2_stat(n, s % 2)
                    merged_t(n + 1)
            for n in range(5, NT):
                normed_t(n - 1)
                if n + 2 < NT:
                    v_stat(n + 2, n % 2, (n + 2) // 2 + 1, rows_of(n + 2))
                x2_stat(n, n % 2, rows_of(n))
                if n + 1 < NT:
                    merged_t(n + 1, rows_of(n + 1))
            normed_t(8, RS)
            stage_end(act, 4)

            act.wait_ge(r_sub, 1)
            A(g_exp, g_sub, ACT.Exp)
            A(d_exp, d_sub, ACT.Exp).then_inc(r_exp, 1)

            def rows_t(n, u):
                act.wait_ge(e_xt, n + 1)
                nc.scalar.copy(xg_t[u][:, 0:4, :].rearrange("p k n -> p (k n)"), bank(0)).then_inc(e_xe, 1)

            def silu(n, u):
                act.wait_ge(e_gu, n + 1)
                A(h_s, bank(2 + u)[:, 0:DE], ACT.Silu).then_inc(e_si, 1)

            def expert_out(n, s, i_s):
                act.wait_ge(e_y[0], n + 1)
                act.wait_ge(yo_free[s], i_s)
                nc.scalar.copy(yo[s][:, 0:512], bank(5)).then_inc(e_ye[0], 1)

            rows_t(0, 0)
            rows_t(1, 1)
            silu(0, 0)
            with act.Fori(0, 15) as i:
                for q in range(1, 5):
                    rows_t(4 * i + q + 1, (q + 1) % 2)
                    silu(4 * i + q, q % 2)
                    expert_out(4 * i + q - 1, q - 1, i + 1)
            for n in range(61, NE):
                if n < NE - 1:
                    rows_t(n + 1, (n + 1) % 2)
                silu(n, n % 2)
                expert_out(n - 1, (n - 1) % 4, (n - 1) // 4 + 1)
            expert_out(NE - 1, 3, NE // 4)
            total = act.value_load(ovf_id[0:1, NOVF:NOVF + 1], min_val=0, max_val=NOVF)
            with act.Fori(0, NOVF) as j:
                with act.If(total > j):
                    rows_t(NE + j, 0)
                    silu(NE + j, 0)
                    expert_out(NE + j, 0, 17 + j)

            def last_norm(n, s, r):
                act.wait_ge(f_sum, n + 1)
                A(junk8[0:r, :], fin[s][0:r, :], ACT.Square, scale=D ** -0.5, accum_out=stat8[s][0:r, 0:1]).then_inc(f_sq, 1)
                act.wait_ge(f_sq, n + 1)
                A(stat8[s][0:r, 0:1], stat8[s][0:r, 0:1], ACT.Sqrt, bias=eps[0:r]).then_inc(f_rs, 1)

            with act.Fori(0, 4) as i:
                for s in range(2):
                    last_norm(2 * i + s, s, P)
            last_norm(8, 0, RS)

        @block.gpsimd
        def _(pool):
            G = nc.gpsimd
            step = Count(pool, pool_c)
            for u in range(4):
                pool.sem_inc(yo_free[u], 1)
            for u in range(2):
                pool.sem_inc(xt_st[u], 16)
                pool.sem_inc(f_st[u], 16)

            G.memset(ws_ns[0:RS, :, :], 0.0).then_inc(ws_zero, 1)
            pool.wait_ge(tab_in, 16)
            pool.wait_ge(pt_in, 16 * PG)
            step(G.tensor_copy(page_idx, page_raw))
            G.tensor_scalar(page_int, page_idx, 8.0, const("p_mod"), ALU.mult, ALU.add).then_inc(idx_ready, 1)
            pool.wait_ge(ws_ready, 16 * (1 + NB))
            for g in range(KD):
                G.tensor_tensor(ws_n[:, g, :], ws_n[:, g, :], const("keep"), ALU.mult)
                last = G.tensor_tensor(ws_ns[0:RS, g, :], ws_ns[0:RS, g, :], const("keep_s")[0:RS, :], ALU.mult)
            last.then_inc(wsm_ready, 1)
            stage_end(pool, 1)

            for what, t in sched:
                r = rows_of(t) if what in ("prep", "Q") else 0
                if what == "prep":
                    c, sn = cos[0:r, t, :], sin[0:r, t, :]
                    x1, x2_ = z0[0:r, t, QL + KVL:QL + KVL + 32], z0[0:r, t, QL + KVL + 32:ZL]
                    G.tensor_tensor(kr_tmp[0:r, 0:32], x1, c, ALU.mult)
                    G.tensor_tensor(kr_tmp[0:r, 32:64], x2_, sn, ALU.mult)
                    G.tensor_tensor(kr_tmp[0:r, 64:96], x2_, c, ALU.mult)
                    step(G.tensor_tensor(kr_tmp[0:r, 96:128], x1, sn, ALU.mult))
                    G.tensor_tensor(kr_n[0:r, t, 0:32], kr_tmp[0:r, 0:32], kr_tmp[0:r, 32:64], ALU.subtract)
                    step(G.tensor_tensor(kr_n[0:r, t, 32:64], kr_tmp[0:r, 64:96], kr_tmp[0:r, 96:128], ALU.add))
                    pool.sem_inc(p_kr, 1)
                    if t == NTP:
                        pool.sem_inc(lat_ready, 1)
                elif what == "Q":
                    pool.wait_ge(qrn_ready, t + 1)
                    v = [x.rearrange("p (h f) -> p h f", h=H) for x in (qr_n, qr_r)]
                    x1, x2_ = v[0][0:r, :, 0:32], v[0][0:r, :, 32:64]
                    tmp = qr_tmp.rearrange("p (a h f) -> p a h f", a=4, h=H)
                    cb = cos[0:r, t, :].unsqueeze(1).broadcast_to([r, H, 32])
                    sb = sin[0:r, t, :].unsqueeze(1).broadcast_to([r, H, 32])
                    G.tensor_tensor(tmp[0:r, 0], x1, cb, ALU.mult)
                    G.tensor_tensor(tmp[0:r, 1], x2_, sb, ALU.mult)
                    G.tensor_tensor(tmp[0:r, 2], x2_, cb, ALU.mult)
                    step(G.tensor_tensor(tmp[0:r, 3], x1, sb, ALU.mult))
                    G.tensor_tensor(v[1][0:r, :, 0:32], tmp[0:r, 0], tmp[0:r, 1], ALU.subtract)
                    G.tensor_tensor(v[1][0:r, :, 32:64], tmp[0:r, 2], tmp[0:r, 3], ALU.add).then_inc(qrope_done, 1)
            stage_end(pool, 2)

            ckv_g = cache_ckv[0].rearrange("n (a r) c -> (n a) (r c)", r=PG)
            kr_g = cache_krope[0].rearrange("n (a r) c -> (n a) (r c)", r=PG)

            def gather(q, n, col):
                step_g = G.tensor_copy(idx_now[q], page_int[:, col].bitcast(U32))
                return step_g

            def fetch(q):
                off = bass.IndirectOffsetOnAxis(ap=idx_now[q], axis=0)
                pool.indirect_dma_start(ck[q].rearrange("p r c -> p (r c)"), None, ckv_g, off).then_inc(c_in[q], 16)
                pool.indirect_dma_start(kr[q].rearrange("p r c -> p (r c)"), None, kr_g, off).then_inc(c_in[q], 16)

            for q in range(4):
                gather(q, q, slice(q, q + 1)).then_inc(idx_step, 1)
                pool.wait_ge(idx_step, q + 1)
                fetch(q)
            with pool.Fori(0, NB - 1) as i:
                for q in range(4):
                    pool.wait_ge(c_pv, 4 * i + q + 1)
                    gather(q, None, bass.ds(4 * i + q + 4, 1)).then_inc(idx_step, 1)
                    pool.wait_ge(idx_step, 4 * i + q + 5)
                    pool.sem_inc(marks, 1)
                    fetch(q)
            stage_end(pool, 3)

            def gate_attn(s, attn_rows, i_in, r=P):
                pool.wait_ge(z_in[s], 16 * i_in)
                G.tensor_tensor(zt[s][0:r, 2 * D:3 * D], zt[s][0:r, 2 * D:3 * D], attn_rows, ALU.mult).then_inc(at_ok, 1)

            def keep_x2(n, s, x2_rows, r=P):
                pool.wait_ge(x2_ok, n + 1)
                G.tensor_copy(x2_rows, xr[s][0:r, :]).then_inc(x2_cp, 1)

            attn_flat, x2_flat = (x.rearrange("p t n -> p (t n)") for x in (attn, x2))
            gate_attn(0, attn[:, 0, :], 1)
            gate_attn(1, attn[:, 1, :], 1)
            with pool.Fori(0, 3) as i:
                for s in range(2):
                    n = 2 * i + s
                    gate_attn(s, attn_flat[:, bass.ds(2 * D * i + D * (s + 2), D)], i + 2)
                    keep_x2(n, s, x2_flat[:, bass.ds(2 * D * i + D * s, D)])
            gate_attn(0, attn[0:RS, NTP, :], 5, RS)
            for n in range(6, NT):
                keep_x2(n, n % 2, x2[0:rows_of(n), n, :], rows_of(n))
            stage_end(pool, 4)

            G.memset(fill.bitcast(I32), 1 << 29).then_inc(fill_ok, 1)
            pool.wait_ge(fill_in, 16)
            pool.wait_ge(r_pos, 1)
            ids_v = ids_sb.rearrange("p (n c) -> p n c", c=2)
            for n in range(2 * NT):
                pool.indirect_dma_start(slot_rows, bass.IndirectOffsetOnAxis(ap=pos_i[:, n:n + 1], axis=0),
                                        ids_v[:, n, :], None, bounds_check=NBLK * P - 1, oob_is_err=False).then_inc(scat_in, 16)
            pool.wait_ge(slots_ok, 1)
            for s in range(4):
                last = G.memset(xg[s], 0.0)
            last.then_inc(xg_zero, 1)
            pool.wait_ge(xg_zero, 1)
            for u in range(2):
                pool.wait_ge(xt_st[u], 16 * (6 - u))

            last_tok, last_slot = pool.to_reg(TOK - 1), pool.to_reg(2 * TOK - 1)

            def index_copy(dst, n, c, k):
                G.tensor_copy(dst, slot_idx[:, n, c:c + 1] if isinstance(n, int) else slot_idx[:, bass.ds(n, 1), c]).then_inc(x_idx, 1)
                pool.wait_ge(x_idx, k + 1)

            def rows_in(s, n, k):
                index_copy(idx_tok[s], n, 1, k)
                pool.sem_inc(marks, 1)
                pool.indirect_dma_start(xg[s], None, xt_rows, bass.IndirectOffsetOnAxis(ap=idx_tok[s], axis=0),
                                        bounds_check=last_tok, oob_is_err=False).then_inc(e_x[s], 16)

            def rows_out(s, n, k):
                index_copy(idx_row[s], n, 0, k)
                pool.wait_ge(e_ye[0], n + 2)
                pool.wait_ge(e_ye[1], n + 2)
                pool.sem_inc(marks, 1)
                pool.indirect_dma_start(y_rows, bass.IndirectOffsetOnAxis(ap=idx_row[s], axis=0), yo[s], None,
                                        bounds_check=last_slot, oob_is_err=False).then_inc(e_sc[s], 16)

            def scattered(s, i_s):
                pool.wait_ge(e_sc[s], 16 * i_s)
                pool.sem_inc(yo_free[s], 1)

            for n in range(4):
                rows_in(n, n, n)
            for n in range(2):
                pool.wait_ge(e_xt, n + 1)
                rows_in(n, n + 4, n + 4)
            for n in range(2):
                rows_out(n, n, 2 * n + 6)
                rows_in(n + 2, n + 6, 2 * n + 7)
            with pool.Fori(0, 14) as i:
                for q in range(2, 6):
                    n = 4 * i + q
                    scattered(q - 2, i + 1)
                    rows_out(q % 4, n, 2 * n + 6)
                    rows_in((q + 2) % 4, n + 6, 2 * n + 7)
            for n in range(58, NE):
                scattered((n - 2) % 4, (n - 2) // 4 + 1)
                rows_out(n % 4, n, 64 + n)
            scattered(2, NE // 4)
            scattered(3, NE // 4)
            total = pool.value_load(ovf_id[0:1, NOVF:NOVF + 1], min_val=0, max_val=NOVF)
            with pool.Fori(0, NOVF) as j:
                with pool.If(total > j):
                    rows_in(0, NE + j, 2 * j + 128)
                    rows_out(0, NE + j, 2 * j + 129)
                    scattered(0, j + 17)
            pool.sem_inc(moe_end, 1)


        @block.vector
        def _(dve):
            V = nc.vector
            copy, tt, ts, stt, red = V.tensor_copy, V.tensor_tensor, V.tensor_scalar, V.scalar_tensor_tensor, V.tensor_reduce
            step = Count(dve, dve_c)
            dve.sem_inc(xt_ev[1], 2)
            dve.sem_inc(c_acc, 1)
            dve.sem_inc(sgu_ok, 1)
            dve.sem_inc(lg_ok, 1)
            dve.sem_inc(e_ye[1], 1)
            V.memset(logits, 0.0)
            step(V.memset(small, 0.0))
            dve.sem_inc(small_zero, 1)
            dve.wait_ge(small_in, 16 * (9 + NB))

            def norm_x(n, s, r, dst):
                dve.wait_ge(x_rstd, n + 1)
                V.reciprocal(small[0:r, 4 + s:5 + s], small[0:r, 2 + s:3 + s]).then_inc(x_inv, 1)
                dve.wait_ge(x_inv, n + 1)
                stt(xn[s][0:r, :], x_in[s][0:r, :], small[0:r, 4 + s:5 + s], g1[0:r, :], ALU.mult, ALU.mult).then_inc(xn_ready, 1)
                dve.wait_ge(xt_mm, n + 1)
                ts(dst, bank(2 * s + 1).rearrange("p (k n) -> p k n", k=4)[:, :, 0:r], 1.0, None, ALU.mult).then_inc(xt_ev[1], 1)

            with dve.Fori(0, 4) as i:
                for s in range(2):
                    norm_x(2 * i + s, s, P, xn_t[:, 4:8, bass.ds(2 * P * i + P * s, P)])
            norm_x(8, 0, RS, xn_t[:, 4:8, SEQ:TOK])
            for t in range(NT):
                r = rows_of(t)
                dve.wait_ge(z_ev, NT + t + 1)
                for c, (a0, w) in enumerate(((0, QL), (QL, KVL))):
                    step(stt(junk2[0:r, c * QL:c * QL + w], z0[0:r, t, a0:a0 + w], 1.0 / w, z0[0:r, t, a0:a0 + w], ALU.mult,
                             ALU.mult, accum_out=stat[0:r, t, c:c + 1]))
            dve.sem_inc(p_sq, 1)
            dve.wait_ge(p_rs, 1)
            step(V.reciprocal(rstd, stat))
            stage_end(dve, 1)

            got = 0
            for what, n in sched:
                if what == "prep":
                    t, r = n, rows_of(n)
                    if t >= 1:
                        dve.wait_ge(b_mm[0], cq_read)
                    stt(cq[0:r, :], z0[0:r, t, 0:QL], rstd[0:r, t, 0:1], gq[0:r, :], ALU.mult, ALU.mult)
                    last = stt(ckv_n[0:r, t, :], z0[0:r, t, QL:QL + KVL], rstd[0:r, t, 1:2], gkv[0:r, :], ALU.mult, ALU.mult)
                    last.then_inc(p_cn, 1)
                    if t == NTP:
                        dve.wait_ge(p_cn, NT)
                        dve.sem_inc(lat_ready, 1)
                elif what == "Q":
                    t, r, s = n, rows_of(n), n % 2
                    b1 = bank(1).rearrange("p (i n) -> p i n", i=4)

                    def from1(dst, src):
                        nonlocal got
                        got += 1
                        dve.wait_ge(b_mm[1], got)
                        copy(dst, src).then_inc(b_ev[1], 1)

                    from1(ckv_t[:, :, t * P:t * P + r], b1[:, 0:2, 0:r])
                    from1(qn_t[:, 4:8, 0:r], b1[:, :, 0:r])
                    for h in (0, 4):
                        from1(ql_t[s][:, h:h + 2, :, 0:r].rearrange("p h c n -> p (h c) n"), b1[:, :, 0:r])
                    from1(qr_t[s][0:DR, 0:4, 0:r], b1[0:DR, :, 0:r])
                    cq_read = q_units(sched, t)
                elif what == "S":
                    t, h = units[n]
                    w = P * (t + 1)
                    dve.wait_ge(s_mm, n + 1)
                    step(red(rinv[:, n:n + 1], bank(2 + 2 * (n % 2), 2)[:, 0:w], AX.X, ALU.max))
                    ts(negmax[:, n:n + 1], rinv[:, n:n + 1], -SCALE, None, ALU.mult).then_inc(s_nm, 1)
                    dve.wait_ge(s_exp, n + 1)
                    V.reciprocal(rinv[:, n:n + 1], psumq[:, n:n + 1]).then_inc(s_rinv, 1)
                elif what == "T":
                    t, h = units[n]
                    if t >= 4:
                        dve.wait_ge(t_mm[1], n - 4 * H + 1)
                        copy(prob_t[n % 2][:, 4:t + 1, :].rearrange("p j n -> p (j n)"), bank(7)[:, 0:P * (t - 3)]).then_inc(t_ev[1], 1)
                elif n % 2 == 1:
                    t, h = units[n]
                    got += 1
                    dve.wait_ge(b_mm[1], got)
                    if what == "PV":
                        copy(pv_t[1].rearrange("p c n -> p (c n)"), bank(1)[:, 0:2 * P]).then_inc(b_ev[1], 1)
                    else:
                        dve.wait_ge(s_rinv, n + 1)
                        ts(attn[:, t, DV * h:DV * h + DV], bank(1)[:, 0:DV], rinv[:, n:n + 1], None, ALU.mult).then_inc(b_ev[1], 1)
            dve.wait_ge(b_ev[0], bank0_units)
            for c in range(2):
                copy(qs[:, c, :].rearrange("p (b h t) -> p b h t", b=NB, h=H),
                     ql_t[0][:, :, c, 0:RS].rearrange("p h (b t) -> p b h t", b=NB))
            copy(qsr[0:DR, :].rearrange("p (b h t) -> p b h t", b=NB, h=H),
                 qr_t[0][0:DR, :, 0:RS].rearrange("p h (b t) -> p b h t", b=NB))
            copy(qsr[DR:P, :].rearrange("p (b h t) -> p b h t", b=NB, h=H),
                 qr_t[0][0:DR, :, 0:RS].rearrange("p h (b t) -> p b h t", b=NB)).then_inc(n_dve, 1)
            stage_end(dve, 2)

            dve.wait_ge(n_dve, 1)
            for c in range(2):
                copy(q_now[:, c, :], qs[:, c, 0:RS])
            copy(qr_now, qsr[:, 0:RS]).then_inc(q_ready, 1)
            dve.wait_ge(lat_stored, 64)
            V.memset(acc, 0.0)
            V.memset(l_all, 0.0)
            step(V.memset(m_all, NEG))
            dve.wait_ge(n_pe, 1)
            keys = s_new[0:RS, :].rearrange("p (b k) -> p b k", b=NB)
            step(tt(s_new[0:RS, :], bank(5)[0:RS, 0:NB * RS], const("mask_new")[0:RS, :], ALU.add))
            step(red(m_all[0:RS, :], keys, AX.X, ALU.max))
            tt(keys, keys, m_all[0:RS, :].unsqueeze(2).broadcast_to([RS, NB, RS]), ALU.subtract).then_inc(c_sub, 1)
            copy(m_now[:, 0:1], m_all[:, 0:1])
            dve.wait_ge(n_act, 1)
            red(l_all[0:RS, :], p_new[0:RS, :].rearrange("p (b k) -> p b k", b=NB), AX.X, ALU.add)
            dve.wait_ge(n_pe, 2)
            copy(p_new_t[0:RS, :], bank(6)[0:RS, 0:NB * RS]).then_inc(n_dve, 1)
            dve.wait_ge(n_pe, 3)
            step(copy(acc[0:RS, :, :].rearrange("p b c -> p (b c)"), bank(0, 4)[0:RS, :]))
            dve.sem_inc(n_dve, 1)

            PER4 = 18
            chain4 = step.n

            def turned(n, us):
                for u in us:
                    dve.wait_ge(c_tr, NU * n + u + 1)
                    copy(turned_at(u), bank(u % 5)).then_inc(kt_in[1], 1)

            turned(0, range(1, NU, 2))
            acc_flat = acc.rearrange("p b c -> p (b c)")

            def batch(i, last_batch):
                ch = Count(dve, dve_c, chain4 + PER4 * i)
                acc_b, l_b, m_b = acc_flat[:, bass.ds(KVL * i, KVL)], l_all[:, bass.ds(i, 1)], m_all[:, bass.ds(i, 1)]
                for q in range(4):
                    n = 4 * i + q
                    more = q < 3 or not last_batch
                    dve.wait_ge(c_s, n + 1)
                    ch(red(m_part, bank(5), AX.X, ALU.max))
                    ch(tt(m_now[:, q + 1:q + 2], m_now[:, q:q + 1], m_part, ALU.max))
                    ts(neg_m, m_now[:, q + 1:q + 2], -SCALE, None, ALU.mult).then_inc(c_neg, 1)
                    if q == 3 and more:
                        for c in range(2):
                            ts(q_now[:, c, :], qs[:, c, bass.ds(RS * i + RS, RS)], 1.0, None, ALU.mult)
                        ts(qr_now, qsr[:, bass.ds(RS * i + RS, RS)], 1.0, None, ALU.mult).then_inc(q_ready, 1)
                    if more:
                        turned(n + 1, range(1, NU, 2))
                    dve.wait_ge(c_p, n + 1)
                    ch(stt(l_b, l_b, alpha, l_add, ALU.mult, ALU.add))
                    dve.wait_ge(c_pv, n + 1)
                    ch(stt(acc_b, acc_b, alpha, bank(7)[:, 0:KVL], ALU.mult, ALU.add))
                    dve.sem_inc(c_acc, 1)
                ch(ts(m_b, m_now[:, 4:5], 1.0, None, ALU.mult))
                if last_batch:
                    ch.n += 1
                else:
                    ch(ts(m_now[:, 0:1], m_all[:, bass.ds(i + 1, 1)], 1.0, None, ALU.mult))
                assert ch.n == PER4, ch.n

            with dve.Fori(0, NB - 1) as i:
                batch(i, False)
            batch(NB - 1, True)
            step.n += PER4 * NB - 1
            dve.sem_inc(n_dve, 1)
            dve.wait_ge(n_pe, 4)
            step(red(m8[0:NB, :], bank(6)[0:NB, 0:P].rearrange("p (j q) -> p q j", j=4), AX.X, ALU.max))
            copy(m8b[0:NB, :].rearrange("p (j q) -> p j q", j=4),
                 m8[0:NB, :].unsqueeze(1).broadcast_to([NB, 4, RS])).then_inc(n_dve, 1)
            dve.wait_ge(n_pe, 5)
            tt(w_dif, m_all, bank(6)[:, P:P + NB], ALU.subtract).then_inc(c_sub, 1)
            dve.wait_ge(n_act, 2)
            tt(l_w, l_all, w_all, ALU.mult).then_inc(n_dve, 1)
            dve.wait_ge(n_pe, 6)
            step(V.reciprocal(l_inv, bank(6)[:, 2 * P:2 * P + NB]))
            step(tt(l_inv, l_inv, w_all, ALU.mult))
            for b in range(NB):
                last = ts(acc[:, b, :], acc[:, b, :], l_inv[:, b:b + 1], None, ALU.mult)
            last.then_inc(n_dve, 1)
            dve.wait_ge(n_pe, 7)
            for c in range(2):
                last = copy(o_lat[:, c, :].rearrange("p (h b t) -> p b h t", h=H, b=NB),
                            bank(7)[:, NB * RS * c:NB * RS * c + NB * RS].rearrange("p (b h t) -> p b h t", h=H, b=NB))
            last.then_inc(n_dve, 1)
            stage_end(dve, 3)

            def v_norm(n, s, r=P):
                v = zt[s][0:r, D:2 * D]
                dve.wait_ge(v_rs, n + 1)
                V.reciprocal(stat5[s][0:r, 1:2], stat5[s][0:r, 0:1]).then_inc(v_inv, 1)
                dve.wait_ge(v_inv, n + 1)
                stt(v, v, stat5[s][0:r, 1:2], gv[0:r, :], ALU.mult, ALU.mult).then_inc(v_n, 1)

            def merge(n, s, r=P, bs=bs_t):
                u, v, ga, gb = (zt[s][0:r, D * x:D * x + D] for x in range(4))
                dve.wait_ge(mix_mm, n + 1)
                for g in range(KD):
                    last = stt(u[:, P * g:P * g + P], bank(0, 2)[0:r, P * g:P * g + P], bs[0:r, g:g + 1],
                               u[:, P * g:P * g + P], ALU.add, ALU.mult)
                last.then_inc(sgu_ok, 1)
                dve.wait_ge(sgu_ok, n + 2)
                tt(u, u, gb, ALU.mult).then_inc(sgu_gated, 1)
                dve.wait_ge(sgu_gated, n + 1)
                dve.wait_ge(at_ok, n + 1)
                tt(u, u, ga, ALU.add).then_inc(mrg_ok, 1)

            def add_x(n, s, i_in, r=P):
                dve.wait_ge(y_mm, n + 1)
                dve.wait_ge(xr_in[s], 16 * i_in)
                tt(xr[s][0:r, :], xr[s][0:r, :], bank(4, 2)[0:r, :], ALU.add).then_inc(x2_ok, 1)

            def take_logits(n, lg_rows, r=P):
                dve.wait_ge(lg_mm, n + 1)
                tt(lg_rows, bank(6)[0:r, 0:72], rbias[0:r, :], ALU.add).then_inc(lg_ok, 1)

            def norm2(n, s, k, r=P):
                dve.wait_ge(o_rs, n + 1)
                V.reciprocal(stat5[s][0:r, 3:4], stat5[s][0:r, 2:3]).then_inc(o_inv, 1)
                dve.wait_ge(o_inv, n + 1)
                dve.wait_ge(xt_st[s], 16 * k + 16)
                stt(xo[s][0:r, :], xr[s][0:r, :], stat5[s][0:r, 3:4], g2[0:r, :], ALU.mult, ALU.mult).then_inc(o_n, 1)

            dve.wait_ge(late_in, 48)
            lg_flat = logits.rearrange("p t n -> p (t n)")
            v_norm(0, 0)
            merge(0, 0)
            v_norm(1, 1)
            merge(1, 1)
            v_norm(2, 0)
            add_x(0, 0, 1)
            norm2(0, 0, 0)
            with dve.Fori(0, 2) as i:
                for s in range(1, 3):
                    n, u = 2 * i + s, s % 2
                    merge(n + 1, 1 - u)
                    v_norm(n + 2, u)
                    add_x(n, u, i + 1 + s // 2)
                    take_logits(n - 1, lg_flat[:, bass.ds(144 * i + 72 * (s - 1), 72)])
                    norm2(n, u, i + s // 2)
            for n in range(5, NT):
                u, r = n % 2, rows_of(n)
                if n + 1 < NT:
                    merge(n + 1, 1 - u, rows_of(n + 1), bs_t if n + 1 < NTP else bs_ts)
                if n + 2 < NT:
                    v_norm(n + 2, u, rows_of(n + 2))
                add_x(n, u, n // 2 + 1, r)
                take_logits(n - 1, logits[:, n - 1, :])
                norm2(n, u, n // 2, r)
            take_logits(8, logits[0:RS, NTP, :], RS)
            for u in range(2):
                dve.wait_ge(xt_st[u], 16 * (6 - u))
            dve.wait_ge(v_st, 16)
            stage_end(dve, 4)

            def wide(x, n):
                return x.unsqueeze(len(x.shape)).broadcast_to(list(x.shape) + [n])

            for t in range(NT):
                last = V.max(g_top[:, t, :], logits[:, t, 0:NG])
            step(last)
            for t in range(NT):
                last = V.max_index(g_ind[:, t, :], g_top[:, t, :], logits[:, t, 0:NG])
            step(last)
            step(copy(g_f, g_ind[:, :, 0]))
            iota = const("iota")
            step(tt(pen, iota[:, 0:NG].unsqueeze(1).broadcast_to([P, NT, NG]), wide(g_f, NG), ALU.is_equal))
            step(ts(pen, pen, -NEG, NEG, ALU.mult, ALU.add))
            step(tt(e_log.rearrange("p t (g e) -> p t g e", g=NG), logits[:, :, NG:].rearrange("p t (g e) -> p t g e", g=NG),
                    wide(pen, 8), ALU.add))
            for t in range(NT):
                last = V.max(e_top[:, t, :], e_log[:, t, :])
            step(last)
            for t in range(NT):
                last = V.max_index(e_ind[:, t, :], e_top[:, t, :], e_log[:, t, :])
            tt(g_sub, logits[:, :, 0:NG], g_top[:, :, 0:1].broadcast_to([P, NT, NG]), ALU.subtract)
            step(tt(d_sub, e_top[:, :, 1], e_top[:, :, 0], ALU.subtract))
            dve.sem_inc(r_sub, 1)
            step(copy(e_f, e_ind[:, :, 0:2]))
            step(tt(e_f, e_f, wide(const("pad"), 2), ALU.add))
            step(tt(hot.rearrange("p t c n -> p (t c) n"), iota.unsqueeze(1).broadcast_to([P, 2 * NT, NE]),
                    wide(e_f.rearrange("p t c -> p (t c)"), NE), ALU.is_equal))
            step(tt(mask, hot[:, :, 0, :], hot[:, :, 1, :], ALU.add))
            step(V.memset(cum[:, 0, :], 0.0))
            for t in range(1, NT):
                step(tt(cum[:, t, :], cum[:, t - 1, :], mask[:, t - 1, :], ALU.add))
            step(tt(rank[:, 0, :], cum[:, NT - 1, :], mask[:, NT - 1, :], ALU.add))
            dve.sem_inc(r_dve, 1)
            dve.wait_ge(r_exp, 1)
            step(red(g_den, g_exp, AX.X, ALU.add))
            step(ts(d_sub, d_exp, 1.0, None, ALU.add))
            step(tt(g_den, g_den, d_sub, ALU.mult))
            step(V.reciprocal(gates[:, :, 0], g_den))
            step(tt(gates[:, :, 1], gates[:, :, 0], d_exp, ALU.mult))
            dve.wait_ge(r_pe, 1)
            step(copy(cnt[0], bank(1)[:, NE:2 * NE]))
            prod8 = prod.rearrange("p t c n -> p (t c n)")
            big = prod8[:, 0:NE * CAP_STEPS].rearrange("p (e s) -> p e s", s=CAP_STEPS)
            step(tt(big, wide(cnt[0], CAP_STEPS), const("steps").unsqueeze(1).broadcast_to([P, NE, CAP_STEPS]), ALU.is_gt))
            step(red(cnt[1], big, AX.X, ALU.add))
            step(V.tensor_tensor_scan(cnt[2], ones[:, 0:NE], cnt[1], 0.0, ALU.mult, ALU.add))
            step(tt(cnt[3], cnt[2], cnt[1], ALU.subtract))
            big = prod8[:, 0:NE * NOVF].rearrange("p (j e) -> p j e", j=NOVF)
            step(tt(big, cnt[2].unsqueeze(1).broadcast_to([P, NOVF, NE]), wide(const("blocks"), NE), ALU.is_le))
            step(red(cnt[0][:, 0:NOVF], big, AX.X, ALU.add))
            ts(ovf_id[:, 0:NOVF], cnt[0][:, 0:NOVF], NE - 1.0, None, ALU.min)
            copy(ovf_id[:, NOVF:NOVF + 1], cnt[2][:, NE - 1:NE])
            step(copy(rank[:, 0:8, :].rearrange("p t n -> p (t n)"), bank(0)))
            step(copy(rank[:, 8, :], bank(1)[:, 0:NE]))
            rk, xs_, q_, rem, b_, tmp_ = (x.rearrange("p t c -> p (t c)") for x in n_rt)
            ef = e_f.rearrange("p t c -> p (t c)")
            for c in range(2):
                last = tt(prod[:, :, c, :], hot[:, :, c, :], rank, ALU.mult)
            step(last)
            step(red(rk, prod.rearrange("p t c n -> p (t c) n"), AX.X, ALU.add))
            step(tt(prod.rearrange("p t c n -> p (t c) n"), hot.rearrange("p t c n -> p (t c) n"),
                    cnt[3].unsqueeze(1).broadcast_to([P, 2 * NT, NE]), ALU.mult))
            step(red(xs_, prod.rearrange("p t c n -> p (t c) n"), AX.X, ALU.add))
            big = prod8[:, 0:2 * NT * CAP_STEPS].rearrange("p (e s) -> p e s", s=CAP_STEPS)
            step(tt(big, wide(rk, CAP_STEPS), const("steps").unsqueeze(1).broadcast_to([P, 2 * NT, CAP_STEPS]), ALU.is_ge))
            step(red(q_, big, AX.X, ALU.add))
            step(stt(rem, q_, -float(P), rk, ALU.mult, ALU.add))
            step(stt(b_, q_, NE - 1.0, xs_, ALU.add, ALU.add))
            step(tt(b_, b_, ef, ALU.subtract))
            step(ts(tmp_, q_, 1.0, None, ALU.min))
            step(tt(b_, b_, tmp_, ALU.mult))
            step(tt(b_, b_, ef, ALU.add))
            step(stt(pos_i, b_, float(P), rem, ALU.mult, ALU.add))
            dve.sem_inc(r_pos, 1)
            dve.wait_ge(slots_in, 16)
            step(copy(slot_f[0:NBLK, :], fill[0:NBLK, :].bitcast(I32)))
            dve.sem_inc(r_dve, 1)
            dve.wait_ge(r_pe, 2)
            for c in range(2):
                last = copy(slot_idx[:, :, c], bank(2)[:, P * c:P * c + NBLK])
            step(last)
            dve.sem_inc(slots_ok, 1)

            def rows_t(n, u):
                dve.wait_ge(e_xt, n + 1)
                copy(xg_t[u][:, 4:8, :].rearrange("p k n -> p (k n)"), bank(1)).then_inc(e_xe, 1)

            def hidden(n, u):
                dve.wait_ge(e_si, n + 1)
                tt(h_n, h_s, bank(2 + u)[:, DE:2 * DE], ALU.mult).then_inc(e_h, 1)

            def hidden_t(n):
                dve.wait_ge(e_ht, n + 1)
                copy(h_t.rearrange("p f n -> p (f n)"), bank(4)[:, 0:DE]).then_inc(e_he, 1)

            def expert_out(n, s, i_s):
                dve.wait_ge(e_y[1], n + 1)
                dve.wait_ge(yo_free[s], i_s)
                copy(yo[s][:, 512:D], bank(6)).then_inc(e_ye[1], 1)

            rows_t(0, 0)
            rows_t(1, 1)
            hidden(0, 0)
            with dve.Fori(0, 15) as i:
                for q in range(1, 5):
                    rows_t(4 * i + q + 1, (q + 1) % 2)
                    hidden_t(4 * i + q - 1)
                    hidden(4 * i + q, q % 2)
                    expert_out(4 * i + q - 1, q - 1, i + 1)
            for n in range(61, NE):
                if n < NE - 1:
                    rows_t(n + 1, (n + 1) % 2)
                hidden_t(n - 1)
                hidden(n, n % 2)
                expert_out(n - 1, (n - 1) % 4, (n - 1) // 4 + 1)
            hidden_t(NE - 1)
            expert_out(NE - 1, 3, NE // 4)
            total = dve.value_load(ovf_id[0:1, NOVF:NOVF + 1], min_val=0, max_val=NOVF)
            with dve.Fori(0, NOVF) as j:
                with dve.If(total > j):
                    rows_t(NE + j, 0)
                    hidden(NE + j, 0)
                    hidden_t(NE + j)
                    expert_out(NE + j, 0, 17 + j)

            for t in range(NT):
                s, r = t % 2, rows_of(t)
                dve.wait_ge(f_in[s], 16 * (t // 2 + 1))
                dve.wait_ge(f_st[s], 16 * (t // 2) + 16)
                step(stt(fin[s][0:r, :], y2[s][0:r, 0:D], gates[0:r, t, 0:1], x2[0:r, t, :], ALU.mult, ALU.add))
                stt(fin[s][0:r, :], y2[s][0:r, D:2 * D], gates[0:r, t, 1:2], fin[s][0:r, :], ALU.mult, ALU.add).then_inc(f_sum, 1)
                dve.wait_ge(f_rs, t + 1)
                V.reciprocal(stat8[s][0:r, 1:2], stat8[s][0:r, 0:1]).then_inc(f_inv, 1)
                dve.wait_ge(f_inv, t + 1)
                stt(fin[s][0:r, :], fin[s][0:r, :], stat8[s][0:r, 1:2], gf[0:r, :], ALU.mult, ALU.mult).then_inc(f_ok, 1)


_INS = ["x_prompt", "x_sample", "cache_ckv", "cache_krope", "page_table", "norm1_g", "w_in", "q_norm_g", "kv_norm_g",
        "w_uq", "w_qr", "w_uk", "w_uv", "sgu_norm_g", "w_s", "b_s", "w_o", "norm2_g", "w_rg", "b_rg", "w_re", "b_re",
        "w_gate", "w_up", "w_down", "norm_f_g"]
_OUTS = [(1, SEQ, D), (NB, TS, D), (1, 1, NTP, P, KVL), (1, 1, NTP, P, DR), (1, NB, TS, KVL), (1, NB, TS, DR),
         (1, NB, TS, D)]
_SCRATCH = [("z_act", [TOK, 4 * D], F32), ("xt_rows", [TOK, D], F32), ("slot_rows", [NBLK * P, 2], I32),
            ("y_rows", [2 * TOK, D], F32)]


def kernel(**inputs):
    import numpy as _np
    import concourse.bacc as _bacc
    from concourse import mybir as _mybir
    from concourse.bass_utils import run_bass_kernel_spmd as _run

    nc = _bacc.Bacc("TRN2", target_bir_lowering=False, num_devices=1)
    arrays, args = {}, []
    tables, ids = const_tables()
    for name, a in [(n, _np.ascontiguousarray(inputs[n])) for n in _INS] + [("tables", tables), ("ids", ids)]:
        arrays[f"in_{name}_dram"] = a
        args.append(nc.dram_tensor(f"in_{name}_dram", a.shape, _mybir.dt.from_np(a.dtype), kind="ExternalInput").ap())
    for i, shape in enumerate(_OUTS):
        args.append(nc.dram_tensor(f"out_{i}_dram", shape, _mybir.dt.float32, kind="ExternalOutput").ap())
    for name, shape, dt in _SCRATCH:
        args.append(nc.dram_tensor(name, shape, dt, kind="Internal").ap())
    build(nc, *args)
    r = _run(nc, [arrays], core_ids=[0])
    return tuple(r.results[0][f"out_{i}_dram"] for i in range(len(_OUTS)))
```
